# Optimizing a Trainium2 kernel written in Bass

```python
import jax
import jax.numpy as jnp
from jax import lax
import numpy as np

D_MODEL = 1024
BATCH = 1
SEQ = 512
DEPTH = 1

CHUNK = 64
PLE_DIM = 256
HEAD_DIM = 64
D_RWKV = D_MODEL // 2
H_RWKV = D_RWKV // HEAD_DIM
D_ATT = D_MODEL - D_RWKV
H_ATT = D_ATT // HEAD_DIM
LORA_DECAY = 64
LORA_ICLR = 64
LORA_GATE = 128
LORA_VRES = 32
N_RWKV_IN = 3 * D_RWKV + LORA_DECAY + LORA_ICLR + LORA_GATE
N_ATT_IN = 3 * D_ATT
N_IN = N_RWKV_IN + N_ATT_IN
RWKV_SPLITS = (D_RWKV, 2 * D_RWKV, 3 * D_RWKV, 3 * D_RWKV + LORA_DECAY, 3 * D_RWKV + LORA_DECAY + LORA_ICLR)
LEFT_CHUNKS = 8
BAND = (LEFT_CHUNKS + 1) * CHUNK
MAX_REL = 256
N_REL = CHUNK + MAX_REL
N_GROUPS = 4
EXPERTS_PER_GROUP = 8
TOP_K = 2
D_EXPERT = 256
RMS_EPS = 1e-6
GN_EPS = 64e-5
NEG_INF = -1e30

kernel_name = 'hybrid_rwkv7_chunkattn_hmoe_ple'

def rms_norm(x, w):
    xf = x.astype(jnp.float32)
    y = xf * lax.rsqrt(jnp.mean(xf * xf, axis=-1, keepdims=True) + RMS_EPS)
    return (y * w.astype(jnp.float32)).astype(x.dtype)

def token_shift_mix(z, mu):
    z_prev = jnp.pad(z, ((0, 0), (1, 0), (0, 0)))[:, :-1]
    return z + (z_prev - z) * mu

def rwkv7_recurrence(r, decay, k, v, a, b):
    bsz, _, nh, n = r.shape

    def step(state, inp):
        r_t, w_t, k_t, v_t, a_t, b_t = inp
        sa = jnp.einsum('bhij,bhj->bhi', state, a_t)
        state = (state * w_t[:, :, None, :] + sa[..., None] * b_t[:, :, None, :]
                 + v_t[..., None] * k_t[:, :, None, :])
        y_t = jnp.einsum('bhij,bhj->bhi', state, r_t)
        return state, y_t

    s0 = jnp.zeros((bsz, nh, n, n), jnp.float32)
    xs = tuple(jnp.moveaxis(t, 1, 0) for t in (r, decay, k, v, a, b))
    _, ys = lax.scan(step, s0, xs)
    return jnp.moveaxis(ys, 0, 1)

def rwkv7_time_mix(z, v_first, v_res, w0, w2, a0, a2, g2, k_k, k_a, r_k, ln_w, ln_b):
    out_dtype = z.dtype
    z = z.astype(jnp.float32)
    bsz, seq, _ = z.shape
    r, k, v, w_lo, a_lo, g_lo = jnp.split(z, RWKV_SPLITS, axis=-1)
    if v_res is None:
        v_first = v
    else:
        v0, v1, v2 = v_res
        v = v + (v_first - v) * jax.nn.sigmoid(v0 + (v @ v1) @ v2)
    w_log = -jax.nn.softplus(-(w0 + jnp.tanh(w_lo) @ w2)) - 0.5
    decay = jnp.exp(-jnp.exp(w_log))
    a = jax.nn.sigmoid(a0 + a_lo @ a2)
    g = jax.nn.sigmoid(g_lo) @ g2

    def heads(t):
        return t.reshape(bsz, seq, H_RWKV, HEAD_DIM)

    kk = heads(k * k_k)
    kk = kk * lax.rsqrt(jnp.maximum(jnp.sum(kk * kk, axis=-1, keepdims=True), 1e-24))
    k = k * (1.0 + (a - 1.0) * k_a)
    rh, kh, vh, ah = heads(r), heads(k), heads(v), heads(a)
    y = rwkv7_recurrence(rh, heads(decay), kh, vh, -kk, kk * ah)
    mean = jnp.mean(y, axis=-1, keepdims=True)
    var = jnp.mean(jnp.square(y - mean), axis=-1, keepdims=True)
    y = ((y - mean) * lax.rsqrt(var + GN_EPS)).reshape(bsz, seq, D_RWKV) * ln_w + ln_b
    bonus = jnp.sum(rh * kh * r_k.reshape(H_RWKV, HEAD_DIM), axis=-1, keepdims=True) * vh
    y = y + bonus.reshape(bsz, seq, D_RWKV)
    return (y * g).astype(out_dtype), v_first

def chunk_band_attention(q, k, v, rel_bias):
    bsz, seq, nh, dh = q.shape
    nc = seq // CHUNK
    pad = ((0, 0), (LEFT_CHUNKS * CHUNK, 0), (0, 0), (0, 0))
    k_pad = jnp.pad(k, pad)
    v_pad = jnp.pad(v, pad)
    qi = jnp.arange(CHUNK)[:, None]
    kj = jnp.arange(BAND)
    rel = qi + LEFT_CHUNKS * CHUNK - kj[None, :]
    rel_idx = jnp.clip(rel, -(CHUNK - 1), MAX_REL) + (CHUNK - 1)
    bias = rel_bias[:, rel_idx].astype(jnp.float32)
    q_chunks = jnp.moveaxis(q.reshape(bsz, nc, CHUNK, nh, dh), 1, 0)
    scale = dh ** -0.5

    def one_chunk(args):
        c, qc = args
        kb = lax.dynamic_slice_in_dim(k_pad, c * CHUNK, BAND, axis=1)
        vb = lax.dynamic_slice_in_dim(v_pad, c * CHUNK, BAND, axis=1)
        s = jnp.einsum('bqhd,bkhd->bhqk', qc, kb).astype(jnp.float32) * scale + bias
        valid = kj >= (LEFT_CHUNKS - c) * CHUNK
        s = jnp.where(valid, s, NEG_INF)
        pr = jax.nn.softmax(s, axis=-1).astype(vb.dtype)
        return jnp.einsum('bhqk,bkhd->bqhd', pr, vb)

    out = lax.map(one_chunk, (jnp.arange(nc), q_chunks))
    return jnp.moveaxis(out, 0, 1).reshape(bsz, seq, nh * dh)

def hierarchical_moe(x, wg, bg, we, be, w1, w3, w2):
    bsz, seq, d = x.shape
    t = x.reshape(-1, d)
    group_prob = jax.nn.softmax((t @ wg + bg).astype(jnp.float32), axis=-1)
    g_sel = jnp.argmax(group_prob, axis=-1)
    p_g = jnp.take_along_axis(group_prob, g_sel[:, None], axis=-1)
    exp_logits = (t @ we + be).astype(jnp.float32).reshape(-1, N_GROUPS, EXPERTS_PER_GROUP)
    sel_logits = jnp.take_along_axis(exp_logits, g_sel[:, None, None], axis=1)[:, 0]
    exp_prob = jax.nn.softmax(sel_logits, axis=-1)
    top_v, top_i = lax.top_k(exp_prob, TOP_K)
    top_v = top_v / jnp.sum(top_v, axis=-1, keepdims=True)
    w_group = jnp.sum(jax.nn.one_hot(top_i, EXPERTS_PER_GROUP, dtype=jnp.float32) * top_v[..., None], axis=1)
    combine = (jax.nn.one_hot(g_sel, N_GROUPS, dtype=jnp.float32)[:, :, None]
               * (p_g * w_group)[:, None, :]).astype(x.dtype)
    out = jnp.zeros_like(t)
    for gi in range(N_GROUPS):
        h_gate = jnp.einsum('td,edf->tef', t, w1[gi])
        h_up = jnp.einsum('td,edf->tef', t, w3[gi])
        hid = jax.nn.silu(h_gate) * h_up * combine[:, gi, :, None]
        out = out + jnp.einsum('tef,efd->td', hid, w2[gi])
    return out.reshape(bsz, seq, d)

def setup_inputs(seed: int = 0) -> dict:
    key = jax.random.key(seed)
    ks = list(jax.random.split(key, 40))
    cnt = [0]
    f32 = jnp.float32

    def nk():
        cnt[0] += 1
        return ks[cnt[0] - 1]

    def nrm(shape, scale):
        return jax.random.normal(nk(), shape, f32) * scale

    def unif(shape, lo, hi):
        return jax.random.uniform(nk(), shape, f32, lo, hi)

    L = DEPTH
    Lv = DEPTH - 1
    return {
        'x': nrm((BATCH, SEQ, D_MODEL), 1.0),
        'p': nrm((DEPTH, BATCH, SEQ, PLE_DIM), 1.0),
        'norm_mix_w': 1.0 + nrm((L, D_MODEL), 0.02),
        'w_in': nrm((L, D_MODEL, N_IN), D_MODEL ** -0.5),
        'rwkv_mu': unif((L, N_RWKV_IN), 0.0, 1.0),
        'rwkv_w0': unif((L, D_RWKV), -6.0, -1.0),
        'rwkv_w2': nrm((L, LORA_DECAY, D_RWKV), 0.5 * LORA_DECAY ** -0.5),
        'rwkv_a0': nrm((L, D_RWKV), 0.1),
        'rwkv_a2': nrm((L, LORA_ICLR, D_RWKV), 0.5 * LORA_ICLR ** -0.5),
        'rwkv_g2': nrm((L, LORA_GATE, D_RWKV), LORA_GATE ** -0.5),
        'rwkv_k_k': 0.85 + nrm((L, D_RWKV), 0.02),
        'rwkv_k_a': 1.0 + nrm((L, D_RWKV), 0.02),
        'rwkv_r_k': nrm((L, D_RWKV), 0.1),
        'rwkv_ln_w': 1.0 + nrm((L, D_RWKV), 0.02),
        'rwkv_ln_b': nrm((L, D_RWKV), 0.01),
        'rwkv_v0': 1.0 + nrm((Lv, D_RWKV), 0.1),
        'rwkv_v1': nrm((Lv, D_RWKV, LORA_VRES), D_RWKV ** -0.5),
        'rwkv_v2': nrm((Lv, LORA_VRES, D_RWKV), 0.5 * LORA_VRES ** -0.5),
        'att_rel_bias': nrm((L, H_ATT, N_REL), 0.1),
        'w_out': nrm((L, D_MODEL, D_MODEL), D_MODEL ** -0.5),
        'norm_ffn_w': 1.0 + nrm((L, D_MODEL), 0.02),
        'router_group_w': nrm((L, D_MODEL, N_GROUPS), D_MODEL ** -0.5),
        'router_group_b': nrm((L, N_GROUPS), 0.01),
        'router_expert_w': nrm((L, D_MODEL, N_GROUPS * EXPERTS_PER_GROUP), D_MODEL ** -0.5),
        'router_expert_b': nrm((L, N_GROUPS * EXPERTS_PER_GROUP), 0.01),
        'expert_w1': nrm((L, N_GROUPS, EXPERTS_PER_GROUP, D_MODEL, D_EXPERT), D_MODEL ** -0.5),
        'expert_w3': nrm((L, N_GROUPS, EXPERTS_PER_GROUP, D_MODEL, D_EXPERT), D_MODEL ** -0.5),
        'expert_w2': nrm((L, N_GROUPS, EXPERTS_PER_GROUP, D_EXPERT, D_MODEL), D_EXPERT ** -0.5),
        'norm_ple_w': 1.0 + nrm((L, D_MODEL), 0.02),
        'ple_gate_w': nrm((L, D_MODEL, D_MODEL), D_MODEL ** -0.5),
        'ple_gate_b': nrm((L, D_MODEL), 0.01),
        'ple_proj_w': nrm((L, PLE_DIM, D_MODEL), PLE_DIM ** -0.5),
        'final_norm_w': 1.0 + nrm((D_MODEL,), 0.02),
    }

def reference(x, p, norm_mix_w, w_in, rwkv_mu, rwkv_w0, rwkv_w2, rwkv_a0, rwkv_a2, rwkv_g2,
              rwkv_k_k, rwkv_k_a, rwkv_r_k, rwkv_ln_w, rwkv_ln_b, rwkv_v0, rwkv_v1, rwkv_v2,
              att_rel_bias, w_out, norm_ffn_w, router_group_w, router_group_b,
              router_expert_w, router_expert_b, expert_w1, expert_w3, expert_w2,
              norm_ple_w, ple_gate_w, ple_gate_b, ple_proj_w, final_norm_w):
    h = x
    bsz, seq, _ = x.shape
    v_first = None
    for i in range(DEPTH):
        hn = rms_norm(h, norm_mix_w[i])
        z = hn @ w_in[i]
        z_rwkv = token_shift_mix(z[..., :N_RWKV_IN], rwkv_mu[i])
        z_att = z[..., N_RWKV_IN:]
        v_res = None if i == 0 else (rwkv_v0[i - 1], rwkv_v1[i - 1], rwkv_v2[i - 1])
        y_rwkv, v_first = rwkv7_time_mix(z_rwkv, v_first, v_res, rwkv_w0[i], rwkv_w2[i],
                                         rwkv_a0[i], rwkv_a2[i], rwkv_g2[i], rwkv_k_k[i],
                                         rwkv_k_a[i], rwkv_r_k[i], rwkv_ln_w[i], rwkv_ln_b[i])
        q, k, v = jnp.split(z_att, 3, axis=-1)
        q = q.reshape(bsz, seq, H_ATT, HEAD_DIM)
        k = k.reshape(bsz, seq, H_ATT, HEAD_DIM)
        v = v.reshape(bsz, seq, H_ATT, HEAD_DIM)
        y_att = chunk_band_attention(q, k, v, att_rel_bias[i])
        h = h + jnp.concatenate([y_rwkv, y_att.astype(y_rwkv.dtype)], axis=-1) @ w_out[i]
        h = h + hierarchical_moe(rms_norm(h, norm_ffn_w[i]), router_group_w[i], router_group_b[i],
                                 router_expert_w[i], router_expert_b[i],
                                 expert_w1[i], expert_w3[i], expert_w2[i])
        gate = jax.nn.sigmoid(rms_norm(h, norm_ple_w[i]) @ ple_gate_w[i] + ple_gate_b[i])
        h = h + gate * (p[i] @ ple_proj_w[i])
    return rms_norm(h, final_norm_w)


_drawn_inputs = setup_inputs


def setup_inputs(seed=0):
    import zlib

    import numpy as np

    out = dict(_drawn_inputs(seed))
    spreads = {}
    factors = {'rwkv_w2': 3.612,
     'rwkv_k_k': 3.324,
     'rwkv_k_a': 3.502,
     'rwkv_ln_w': 2.868,
     'rwkv_ln_b': 8.0,
     'att_rel_bias': 2.958,
     'norm_ffn_w': 2.949,
     'router_group_b': 3.104,
     'router_expert_b': 3.852,
     'norm_ple_w': 8.0,
     'ple_gate_b': 8.0,
     'final_norm_w': 2.747}
    for name, (base, spread) in spreads.items():
        noise = np.random.default_rng([zlib.crc32(name.encode()), seed]).standard_normal(out[name].shape)
        drawn = base * np.exp(spread * noise) if base else spread * noise
        out[name] = jnp.asarray(drawn.astype(out[name].dtype))
    for name, factor in factors.items():
        out[name] = (out[name] * factor).astype(out[name].dtype)
    return out
```

```python
import math
from contextlib import ExitStack

import concourse.bass as bass
from concourse import mybir

F32 = mybir.dt.float32
U32 = mybir.dt.uint32
ALU = mybir.AluOpType
ACT = mybir.ActivationFunctionType
AX = mybir.AxisListType

P = 128
T = 512
NT = T // P
D = 1024
KD = D // P
DR = 512
NP = DR // P
NH = 8
HD = 64
C = 64
NC = T // C
N_RWKV = 3 * DR + 256
N_IN = N_RWKV + 3 * DR
SLAB = 256
RING = 3
NE = 32
NG = 4
EPG = 8
DE = 256
CAP = 64
KE = DE // P
NPAIR = NE // 2
PLE = 256
RMS_EPS = 1e-6
GN_EPS = 64e-5
DECAY_SCALE = 0.6065306597126334
NEG = -1e30
NORM_SCALE_LOG2 = 20

K_ID, K_ONES, K_MASK, K_LEVEL = 0, 128, 256, 768
LEVELS = 6
K_RESET = K_LEVEL + LEVELS * 128
K_TRI = K_RESET + T
K_ALL1 = K_TRI + 128
K_IOTA = K_ALL1 + 128
K_TOK = K_IOTA + NE
K_END = K_TOK + NT

V_MU, V_W0, V_A0, V_KK, V_KA, V_RK, V_LNW, V_LNB = 0, 14, 18, 22, 26, 30, 34, 38
V_MIX, V_FFN, V_PLE = 42, 50, 58
V_END = 66


def hybrid_trunk(nc, a, out):
    with ExitStack() as ctx:
        def sem(name):
            return ctx.enter_context(nc.semaphore(name))

        arena = ctx.enter_context(nc.sbuf_tensor("arena", [P, 53200], F32))
        psum = ctx.enter_context(nc.psum_tensor("psum", [P, 8, 512], F32))

        def at(kib, n):
            return arena[:, int(kib * 256):int(kib * 256) + n]

        def grid(kib, *dims):
            n = 1
            for d in dims:
                n *= d
            names = "abcd"[:len(dims)]
            spec = "p (" + " ".join(names) + ") -> p " + " ".join(names)
            return at(kib, n).rearrange(spec, **dict(zip(names[1:], dims[1:])))

        def bank(b):
            return psum[:, b, :]

        const = at(48, K_END)
        vec = at(48 + K_END / 256, V_END)
        small = at(48 + (K_END + V_END) / 256, 3072 - K_END - V_END)
        ident = const[:, K_ID:K_ID + P]
        head_ones = const[:, K_ONES:K_ONES + P]
        z = grid(60, 14, T)
        q_head = grid(88, NH, T)
        k_pair = grid(104, NP, T)
        v_tok = grid(112, NT, DR)
        h_feat = grid(120, KD, T)
        slabs = grid(136, RING, KD, SLAB)
        x_in_sb = grid(160, NT, D)
        x_norm = grid(176, NT, D)
        prob = grid(120, 4, T)
        PT_W = 10 * P
        prob_t = grid(128, 2, 2, PT_W)
        bias_w = grid(148, 4, T)
        y_att = grid(196, NP, T)
        shift_buf = [grid(204, 520)[:, 0:T + 1], grid(192, 520)[:, 0:T + 1]]

        within = grid(88, NT, 4 * P)
        across = grid(96, NT, 4 * P)
        m_level = [grid(104, 8, P), grid(108, 8, P)]
        t_inv = grid(112, 8, P)
        t_inv_t = grid(116, 8, P)
        m_t = grid(120, 8, P)
        bk_chunk = grid(124, NT, 2, 2 * P)
        v_rows = grid(132, NT, P)
        rhs = grid(134, NT, 2, P)
        wy = grid(138, NT, 2, 2, HD)
        step_mat = grid(142, NC, P)
        step_add = grid(146, NC, P)
        r_eff = grid(150, T)
        y_buf = grid(152, T)
        state = grid(154, NC, P)
        r_dec = [grid(158, T), grid(178, T)]
        ar_head = grid(160, NT, 4 * P)
        a_dec = grid(168, T)
        b_inc = grid(170, T)
        k_inc = grid(172, T)
        b_end = grid(174, T)
        k_end = grid(176, T)
        sgw = grid(180, T)
        iclr = grid(182, T)
        cum = grid(184, T)
        cum_x = grid(186, T)
        dec = grid(188, T)
        cum_e = grid(190, T)
        kkn = grid(192, T)
        knorm = grid(194, T)
        k_mod = grid(204, T)
        lora_w = grid(0, 3, DR)
        h_res = grid(88, NT, D)
        w_out = grid(160, KD, D)
        n_rows = grid(60, NT, D)
        n_feat = grid(136, NT, KD, P)
        router_w = grid(204, KD, NG + NE)
        router_b = grid(205.25, NG + NE)
        zero_idx = at(206.5, P).bitcast(U32)
        table = at(80, 2048)
        used = [0]

        def col(n, *dims, dtype=None):
            ap = table[:, used[0]:used[0] + n]
            used[0] += n
            if dtype is not None:
                ap = ap.bitcast(dtype)
            if dims:
                names = "abcd"[:len(dims)]
                ap = ap.rearrange("p (" + " ".join(names) + ") -> p " + " ".join(names), **dict(zip(names[1:], dims[1:])))
            return ap

        e_logit = col(NT * NE, NT, NG, EPG)
        g_logit = col(NT * 8, NT, 8)
        g_top = col(NT * 8, NT, 8)
        g_idx = col(NT * 8, NT, 8, dtype=U32)
        g_sel = col(NT)
        g_exp = col(NT * NG, NT, NG)
        g_sum = col(NT)
        p_group = col(NT)
        g_hot = col(NT * NG, NT, NG)
        e_mask = col(NT * NE, NT, EPG, NG)
        sel = col(NT * 8, NT, 8)
        e_top = col(NT * 8, NT, 8)
        e_idx = col(NT * 8, NT, 8, dtype=U32)
        e_loc = col(NT * 2, NT, 2)
        e_ratio = col(NT)
        weight = col(NT * 2, NT, 2)
        expert = col(NT * 2, NT, 2)
        hot = [col(NT * NE, NT, NE), col(NT * NE, NT, NE)]
        hot_sum = col(NT * NE, NT, NE)
        hot_pos = col(NT * NE, NT, NE)
        pos = col(NT * 2, NT, 2)
        slot_f = col(NT * 2, NT, 2)
        fits = col(NT * 2, NT, 2)
        w_main = col(NT * 2, NT, 2)
        over_u = col(1, dtype=U32)
        over_rows = col(1)
        w_col = col(NT)
        y_row = col(NT * 2, NT, 2, dtype=U32)
        slot_u = col(NT * 2, NT, 2, dtype=U32)
        tok_u = col(NT, dtype=U32)
        slot_tok = col(NPAIR, dtype=U32)
        slot_now = [col(1, dtype=U32), col(1, dtype=U32)]

        w1_sb = [grid(b, 2, KD, DE) for b in (0, 104)]
        w3_sb = [grid(b + 16, 2, KD, DE) for b in (0, 104)]
        w2_sb = [grid(b + 32, 2, KE, D) for b in (0, 104)]
        x_slot = [grid(152, D), grid(156, D)]
        x_slot_t = [grid(160, KD, P), grid(164, KD, P)]
        y_slot = [grid(168, D), grid(172, D)]
        hid = [grid(176, DE), grid(177, DE)]
        hid_t = [grid(178, KE, P), grid(179, KE, P)]
        y_tok = [[grid(152 + 8 * b + 4 * x, D) for x in range(2)] for b in range(2)]

        over_feat = grid(128, NT, KD, P)
        over_w1 = grid(104, KD, DE)
        over_w3 = grid(112, KD, DE)
        over_w2 = grid(120, KE, D)
        w_over = hot_pos

        ple_wp = grid(180, KE, D)
        ple_p = grid(188, NT, PLE)
        ple_pt = grid(192, KE, T)
        gate_b = grid(196, D)
        final_w = grid(200, D)
        gate_w = grid(0, KD, D)
        n3_feat = grid(104, NT, KD, P)
        gate = [grid(120, D), grid(124, D)]
        out_rows = [grid(128, D), grid(132, D)]

        norm_rows = nc.dram_tensor("norm_rows", (T, D), F32, kind="Internal").ap()
        tok_of_slot = nc.dram_tensor("tok_of_slot", (T * NE, 1), U32, kind="Internal").ap()
        y_of_slot = nc.dram_tensor("y_of_slot", (CAP * NE, D), F32, kind="Internal").ap()

        d_end = [small[:, 128:136], small[:, 136:144]]

        ss = small[:, 0:4]
        ms = small[:, 4:8]
        rs = small[:, 8:12]
        one_mu = small[:, 12:26]
        ss2, rs2 = small[:, 144:148], small[:, 148:152]
        ss3, rs3 = small[:, 152:156], small[:, 156:160]
        ss4, rs4 = small[:, 160:164], small[:, 164:168]
        rms_eps = small[:, 26:27]
        gn_eps = small[:, 27:28]
        norm_bias = small[:, 28:29]
        nmax = small[:, 32:64]
        psumrow = small[:, 64:96]
        prow_inv = small[:, 96:128]

        consts_in = sem("consts_in")
        x_in = [sem(f"x_in{t}") for t in range(NT)]
        rs_ready = sem("rs_ready")
        eps_ready = sem("eps_ready")
        dve_step = sem("dve_step")
        act_step = sem("act_step")
        pool_step = sem("pool_step")
        xn_ready = sem("xn_ready")
        xt_mm = sem("xt_mm")
        hf_act = sem("hf_act")
        hf_dve = sem("hf_dve")
        slab_in = [sem(f"slab_in{i}") for i in range(RING)]
        slab_used = sem("slab_used")
        z_mm = sem("z_mm")
        z_shift = sem("z_shift")
        z_act = sem("z_act")
        z_dve = sem("z_dve")
        zeros_ready = sem("zeros_ready")
        bias_in = [sem(f"bias_in{i}") for i in range(4)]
        bias_masked = sem("bias_masked")
        att_s_mm = sem("att_s_mm")
        att_s_read = sem("att_s_read")
        att_max = sem("att_max")
        att_exp = sem("att_exp")
        att_p = sem("att_p")
        att_tr = sem("att_tr")
        att_pt = sem("att_pt")
        att_pv = sem("att_pv")
        att_y = sem("att_y")
        lora_in = sem("lora_in")
        idx_zeroed = sem("idx_zeroed")
        w_out_in = [sem("w_out_in0"), sem("w_out_in1")]
        res_in = sem("res_in")
        op_mm = sem("op_mm")
        h_ready = sem("h_ready")
        nrow_mm = sem("nrow_mm")
        nf_ready = sem("nf_ready")
        rows_out = sem("rows_out")
        router_in = sem("router_in")
        route_mm = sem("route_mm")
        routed = sem("routed")
        GROUP_DIFF, EXPERT_DIFF, CHOICES, SLOTS, OVERFLOWS = 1, 2, 3, 4, 5
        route_exp = sem("route_exp")
        scattered = sem("scattered")
        slot_tok_in = sem("slot_tok_in")
        slot_now_ready = sem("slot_now_ready")
        gather_go = sem("gather_go")
        x_slot_in = [sem(f"x_slot_in{i}") for i in range(2)]
        w_exp_in = [sem(f"w_exp_in{i}") for i in range(2)]
        w_exp_used = sem("w_exp_used")
        xs_mm = sem("xs_mm")
        xs_ready = sem("xs_ready")
        up_mm = sem("up_mm")
        silu_ready = sem("silu_ready")
        hid_ready = sem("hid_ready")
        hid_mm = sem("hid_mm")
        hidt_ready = sem("hidt_ready")
        down_mm = sem("down_mm")
        y_lo = sem("y_lo")
        y_hi = sem("y_hi")
        y_out = [sem(f"y_out{i}") for i in range(2)]
        y_tok_in = [sem(f"y_tok_in{i}") for i in range(2)]
        ple_in = sem("ple_in")
        ple_mm = sem("ple_mm")
        ple_t_ready = sem("ple_t_ready")
        gate_w_in = sem("gate_w_in")
        gate_mm = sem("gate_mm")
        proj_mm = sem("proj_mm")
        gate_pre = sem("gate_pre")
        gate_ready = sem("gate_ready")
        out_ready = sem("out_ready")
        over_counted = sem("over_counted")
        over_w_in = sem("over_w_in")
        over_mm = sem("over_mm")
        over_act = sem("over_act")
        over_dve = sem("over_dve")
        out_stored = [sem("out_stored0"), sem("out_stored1")]
        lo_ready = sem("lo_ready")
        prep_mm = sem("prep_mm")
        sg_ready = sem("sg_ready")
        aa_ready = sem("aa_ready")
        ksq_ready = sem("ksq_ready")
        cum_ready = sem("cum_ready")
        cum_split = sem("cum_split")
        decay_ready = sem("decay_ready")
        ksum_ready = sem("ksum_ready")
        kn_ready = sem("kn_ready")
        rk_ready = sem("rk_ready")
        rt_ready = sem("rt_ready")
        at_ready = sem("at_ready")
        prep_out = sem("prep_out")
        bonus_ready = sem("bonus_ready")
        g_ready = sem("g_ready")
        ar_ready = sem("ar_ready")
        unit_in_used = sem("unit_in_used")
        s1_mm = sem("s1_mm")
        s2_mm = sem("s2_mm")
        within_ready = sem("within_ready")
        across_ready = sem("across_ready")
        tok_mm = sem("tok_mm")
        tok_ready = sem("tok_ready")
        tt_init = sem("tt_init")
        mt_ready = sem("mt_ready")
        x_mm = sem("x_mm")
        x_ready = sem("x_ready")
        d_mm = sem("d_mm")
        t_ready = sem("t_ready")
        tr_mm = sem("tr_mm")
        tt_ready = sem("tt_ready")
        g_mm = sem("g_mm")
        ga_ready = sem("ga_ready")
        w_mm = sem("w_mm")
        w_ready = sem("w_ready")
        rp_mm = sem("rp_mm")
        rp_ready = sem("rp_ready")
        y0_mm = sem("y0_mm")
        y0_ready = sem("y0_ready")
        mc_mm = sem("mc_mm")
        mc_ready = sem("mc_ready")
        q_mm = sem("q_mm")
        q_ready = sem("q_ready")
        seq_mm = sem("seq_mm")
        s_ready = sem("s_ready")
        y_mm = sem("y_mm")
        y_ready = sem("y_ready")
        stat_mm = sem("stat_mm")
        yc_ready = sem("yc_ready")
        ysq_ready = sem("ysq_ready")
        rstd_ready = sem("rstd_ready")
        yr_ready = sem("yr_ready")
        rwkv_zero = sem("rwkv_zero")

        slab_order = [6, 2, 3, 0, 1, 4, 5, 7, 8, 9, 10, 11, 12]
        jobs = []
        for n, s in enumerate(slab_order):
            if s < 11:
                jobs += [(n, "feat", 2 * s), (n, "feat", 2 * s + 1)]
            else:
                jobs += [(n, "tok", (s - 11, t)) for t in range(NT)]
        NJ = len(jobs)
        last_job = {n: j for j, (n, _, _) in enumerate(jobs)}

        def units():
            return [(h, i) for h in range(NH) for i in range(NT)]

        def pt_col(i, j):
            return (i * (i + 1) // 2 + j) * P

        def z_reader(j):
            _, kind, what = jobs[j]
            return "act" if kind == "feat" and what >= 18 else "dve"

        def z_count(j, reader):
            return sum(z_reader(i) == reader for i in range(j + 1))

        def z_done(eng, j):
            r = z_reader(j)
            eng.wait_ge({"act": z_act, "dve": z_dve}[r], z_count(j, r))

        def over_up(e, t):
            return e * (3 * NT) + (2 * NT + 3 * t + 1)

        def over_turned(e, t):
            return e * (3 * NT) + (2 * NT + 3 * t + 2)

        def over_down(e, t):
            return e * (3 * NT) + (2 * NT + 3 * t + 3)

        def over_col(e):
            return e * (2 * NT + 1) + (NT + 1)

        def over_hid(e, t):
            return e * (2 * NT + 1) + (NT + 2 * t + 2)

        def over_silu(e, t):
            return e * (2 * NT) + (2 * t + 1)

        def over_hid_t(e, t):
            return e * (2 * NT) + (2 * t + 2)

        def if_over(eng):
            eng.wait_ge(routed, OVERFLOWS)
            return eng.If(eng.value_load(over_u[0:1, 0:1], min_val=0, max_val=2 * T) > 0)

        def one_of(src, pair, i):
            return src[bass.ds(pair + i * NPAIR, 1), :, :].rearrange("o p f -> (o p) f")

        def one_row(dst, j, e):
            return dst[bass.ds(j, 1), e, :, :].rearrange("o c d -> (o c) d")

        w_in_v = a["w_in"].rearrange("(p k) n -> p k n", k=KD)

        LV = LEVELS - 1
        NSLOT = 2 * LV

        def level_mask(l):
            return const[:, K_LEVEL + l * P:K_LEVEL + (l + 1) * P]

        def mats(m):
            return lambda s: m[:, 4 * s:4 * s + 4, :]

        def n_of(s):
            return within.rearrange("p n (h x t) -> p n h x t", h=2, x=2)[:, 2 * s:2 * s + 2, :, 0, :]

        def heads4(ap):
            return ap.rearrange("p (n h) t -> p n h t", h=2)

        def over(ap, *dims):
            return ap.unsqueeze(1).unsqueeze(1).to_broadcast([P, 2, 2, P])

        block = ctx.enter_context(nc.Block())

        @block.sync
        def _(sp):
            sp.dma_start(vec, a["vec"]).then_inc(consts_in, 16)
            for t in range(NT):
                sp.dma_start(x_in_sb[:, t, :], a["x"][t * P:(t + 1) * P, :]).then_inc(x_in[t], 16)
            sp.dma_start(const, a["const"]).then_inc(consts_in, 16)
            sp.dma_start(lora_w[0:64, 0, :], a["w2"]).then_inc(lora_in, 16)
            sp.dma_start(lora_w[64:128, 1, :], a["a2"]).then_inc(lora_in, 16)
            sp.dma_start(lora_w[:, 2, :], a["g2"]).then_inc(lora_in, 16)
            for n, s in enumerate(slab_order):
                if n >= RING:
                    sp.wait_ge(slab_used, n - RING + 1)
                sp.dma_start(slabs[:, n % RING], w_in_v[:, :, s * SLAB:(s + 1) * SLAB]).then_inc(slab_in[n % RING], 16)
            sp.wait_ge(z_mm, NJ)
            for h in range(NH):
                if h >= 4:
                    sp.wait_ge(att_s_read, 4 * (h - 4) + 4)
                sp.dma_start(bias_w[:, h % 4, :], a["bias"][h]).then_inc(bias_in[h % 4], 16)

            w_out_v = a["w_out"].rearrange("(k p) n -> p k n", p=P)
            sp.wait_ge(unit_in_used, NP)
            sp.wait_ge(prep_out, NP)
            sp.dma_start(w_out[:, 0:4, :], w_out_v[:, 0:4, :]).then_inc(w_out_in[0], 16)
            sp.wait_ge(rp_ready, NP)
            sp.dma_start(w_out[:, 4:8, :], w_out_v[:, 4:8, :]).then_inc(w_out_in[1], 16)
            sp.dma_start(router_w, a["router_w"].rearrange("(p k) n -> p k n", k=KD)).then_inc(router_in, 16)
            sp.dma_start(router_b, a["router_b"].to_broadcast([P, NG + NE])).then_inc(router_in, 16)
            sp.wait_ge(y0_mm, NP)
            sp.dma_start(h_res, a["x"].rearrange("(n p) d -> p n d", p=P)).then_inc(res_in, 16)

            def expert_loads(s, pair, which=(0, 1)):
                for i in which:
                    for w, sb, rows in (("w1", w1_sb, KD), ("w3", w3_sb, KD), ("w2e", w2_sb, KE)):
                        src = a[w].rearrange("e (p k) f -> e p (k f)", k=rows)
                        sp.dma_start(sb[s][:, i].rearrange("p k f -> p (k f)"), one_of(src, pair, i)).then_inc(w_exp_in[s], 16)

            sp.wait_ge(prep_mm, 5 * NP)
            expert_loads(0, 0)
            for t in range(NT):
                sp.wait_ge(xn_ready, NT + t + 1)
                sp.dma_start(norm_rows[t * P:(t + 1) * P, :], n_rows[:, t, :]).then_inc(rows_out, 16)
            sp.wait_ge(op_mm, 2 * NT)
            sp.dma_start(ple_wp, a["ple_wp"].rearrange("(p k) n -> p k n", k=KE)).then_inc(ple_in, 16)
            sp.dma_start(ple_p, a["p"].rearrange("(n p) f -> p n f", p=P)).then_inc(ple_in, 16)
            sp.dma_start(gate_b, a["gate_b"].to_broadcast([P, D])).then_inc(ple_in, 16)
            sp.dma_start(final_w, a["final_w"].to_broadcast([P, D])).then_inc(ple_in, 16)
            sp.wait_ge(route_mm, 1)
            expert_loads(1, 1)
            sp.wait_ge(scattered, 16 * 2 * NT)
            sp.dma_start(slot_tok, tok_of_slot[0:CAP * NE, :].rearrange("(c e j) o -> e c (j o)", e=2, j=NPAIR)).then_inc(slot_tok_in, 16)

            def expert_pass(it, last=False):
                for s in range(2):
                    if not last:
                        sp.wait_ge(w_exp_used, it * 2 + s + 1)
                        expert_loads(s, it * 2 + 2 + s)
                    elif s == 0:
                        sp.wait_ge(w_exp_used, NPAIR - 1)
                        sp.dma_start(gate_w, a["gate_w"].rearrange("(p k) n -> p k n", k=KD)).then_inc(gate_w_in, 16)
                    sp.wait_ge(y_lo, it * 2 + s + 1)
                    sp.wait_ge(y_hi, it * 2 + s + 1)
                    dst = y_of_slot.rearrange("(c e j) d -> j e c d", e=2, j=NPAIR)
                    for e in range(2):
                        sp.dma_start(one_row(dst, it * 2 + s, e), y_slot[s][64 * e:64 * e + 64, :]).then_inc(y_out[s], 16)

            with sp.Fori(0, NPAIR // 2 - 1) as it:
                expert_pass(it)
            expert_pass(NPAIR // 2 - 1, last=True)
            with if_over(sp):
                sp.wait_ge(w_exp_used, NPAIR)
                with sp.Fori(0, NE) as e:
                    sp.wait_ge(over_mm, e * (3 * NT) + 2 * NT)
                    for w, dst, rows in (("w1", over_w1, KD), ("w3", over_w3, KD), ("w2e", over_w2, KE)):
                        src = a[w].rearrange("e (p k) f -> e p (k f)", k=rows)
                        sp.dma_start(dst.rearrange("p k f -> p (k f)"), one_of(src, e, 0)).then_inc(over_w_in, 16)
            for t in range(NT):
                sp.wait_ge(out_ready, t + 1)
                sp.dma_start(out[t * P:(t + 1) * P, :], out_rows[t % 2]).then_inc(out_stored[t % 2], 16)
            for b in out_stored:
                sp.wait_ge(b, 16 * NT // 2)

        @block.gpsimd
        def _(pool):
            steps = [0]

            def chain(ins):
                steps[0] += 1
                ins.then_inc(pool_step, 1)
                pool.wait_ge(pool_step, steps[0])

            def copy(out, in_):
                return pool.tensor_scalar(out, in_, 1.0, 1.0, ALU.mult, ALU.mult)

            pool.memset(zero_idx, 0).then_inc(zeros_ready, 1)
            pool.wait_ge(zeros_ready, 1)
            pool.dma_start(tok_of_slot.rearrange("(p n) o -> p (n o)", p=P), zero_idx).then_inc(idx_zeroed, 16)
            pool.memset(lora_w[64:128, 0, :], 0.0).then_inc(zeros_ready, 1)
            pool.wait_ge(zeros_ready, 2)
            pool.memset(lora_w[0:64, 1, :], 0.0).then_inc(zeros_ready, 1)
            pool.wait_ge(zeros_ready, 3)
            for n, b in enumerate(shift_buf):
                pool.memset(b[:, 0:1], 0.0).then_inc(zeros_ready, 1)
                pool.wait_ge(zeros_ready, n + 4)
            for h in range(NH):
                other = 64 * (1 - h % 2)
                pool.memset(q_head[other:other + 64, h, :], 0.0).then_inc(zeros_ready, 1)
                pool.wait_ge(zeros_ready, h + 6)
            for h in range(NH):
                pool.wait_ge(bias_in[h % 4], 16 * (h // 4 + 1))
                pool.memset(bias_w[0:64, h % 4, T - 64:T], NEG).then_inc(bias_masked, 1)
            pool.wait_ge(att_y, NP)
            chain(pool.memset(state, 0.0))
            chain(pool.memset(bk_chunk, 0.0))
            pool.memset(ar_head, 0.0).then_inc(rwkv_zero, 1)
            pool.wait_ge(rwkv_zero, 1)

            def slot(k, prep):
                if prep is None:
                    return
                if k == 1:
                    pool.wait_ge(cum_ready, prep + 1)
                    pool.wait_ge(prep_out, prep)
                    pool.tensor_tensor(cum_x, cum, sgw, ALU.subtract).then_inc(cum_split, 1)
                    pool.wait_ge(cum_split, 2 * prep + 1)
                    ends = cum.rearrange("p (c t) -> p c t", t=C)[:, :, C - 1:C].to_broadcast([P, NC, C])
                    pool.tensor_tensor(cum_e.rearrange("p (c t) -> p c t", t=C), ends, cum.rearrange("p (c t) -> p c t", t=C),
                                       ALU.subtract).then_inc(cum_split, 1)
                    pool.wait_ge(cum_split, 2 * prep + 2)
                if k == NSLOT - 1:
                    pool.wait_ge(unit_in_used, prep)
                    pool.wait_ge(rt_ready, prep + 1)
                    pool.wait_ge(at_ready, prep + 1)
                    for x, src in enumerate((a_dec, r_dec[prep % 2])):
                        for h in range(2):
                            rows = slice(64 * h, 64 * h + 64)
                            copy(ar_head[rows, :, (2 * h + x) * P:(2 * h + x + 1) * P],
                                 src[rows, :].rearrange("p (n t) -> p n t", t=P)).then_inc(ar_ready, 1)
                            pool.wait_ge(ar_ready, 4 * prep + 2 * x + h + 1)

            for k in range(NSLOT):
                slot(k, 0)
            for p in range(NP):
                pool.wait_ge(within_ready, NT * (p + 1))
                for l in range(1, LV + 1):
                    m = LV * p + l - 1
                    for s in range(2):
                        if m >= 2:
                            pool.wait_ge(x_mm, 2 * (m - 2) + s + 1)
                        pool.tensor_tensor(heads4(mats(m_level[m % 2])(s)), n_of(s), over(level_mask(l)), ALU.mult).then_inc(mt_ready, 1)
                        pool.wait_ge(mt_ready, 2 * m + s + 1)
                        slot(2 * (l - 1) + s, p + 1 if p + 1 < NP else None)

            pool.wait_ge(idx_zeroed, 16)
            pool.wait_ge(routed, SLOTS)
            for t in range(NT):
                for x in range(2):
                    pool.indirect_dma_start(tok_of_slot, bass.IndirectOffsetOnAxis(ap=slot_u[:, t, x:x + 1], axis=0),
                                            tok_u[:, t:t + 1], None).then_inc(scattered, 16)
            pool.wait_ge(slot_tok_in, 16)
            pool.wait_ge(rows_out, 16 * NT)

            def gather(s, it):
                pool.tensor_copy(slot_now[s], slot_tok[:, bass.ds(it * 2 + s, 1)]).then_inc(slot_now_ready, 1)
                pool.wait_ge(slot_now_ready, it * 2 + s + 1)
                pool.sem_inc(gather_go, 1)
                pool.indirect_dma_start(x_slot[s], None, norm_rows, bass.IndirectOffsetOnAxis(ap=slot_now[s], axis=0)).then_inc(x_slot_in[s], 16)

            for s in range(2):
                gather(s, 0)
            with pool.Fori(1, NPAIR // 2) as it:
                for s in range(2):
                    pool.wait_ge(xs_mm, it * 4 + 2 * s - 2)
                    gather(s, it)
            for s in range(2):
                pool.wait_ge(y_out[s], 16 * NPAIR)
            for t in range(NT):
                if t >= 2:
                    pool.wait_ge(h_ready, 2 * NT + t - 1)
                for x in range(2):
                    pool.indirect_dma_start(y_tok[t % 2][x], None, y_of_slot, bass.IndirectOffsetOnAxis(ap=y_row[:, t, x:x + 1], axis=0)).then_inc(y_tok_in[t % 2], 16)

        @block.scalar
        def _(act):
            steps = [0]

            def chain(ins):
                steps[0] += 1
                ins.then_inc(act_step, 1)
                act.wait_ge(act_step, steps[0])

            def rms(t):
                chain(act.activation(ms[:, t:t + 1], ss[:, t:t + 1], ACT.Ln, scale=1.0 / D, bias=rms_eps))
                act.activation(rs[:, t:t + 1], ms[:, t:t + 1], ACT.Exp, scale=-0.5).then_inc(rs_ready, 1)

            act.wait_ge(eps_ready, 1)
            for t in range(NT):
                act.wait_ge(x_in[t], 16)
                chain(act.activation(x_norm[:, t, :], x_in_sb[:, t, :], ACT.Square, accum_out=ss[:, t:t + 1]))
                rms(t)
            for k in range(0, KD, 2):
                act.wait_ge(xt_mm, k + 1)
                act.activation(h_feat[:, k, :], bank(k % 2), ACT.Copy, scale=vec[:, V_MIX + k:V_MIX + k + 1]).then_inc(hf_act, 1)
            for j, (n, kind, what) in enumerate(jobs):
                if kind == "feat" and what < 14:
                    act.wait_ge(z_mm, j + 1)
                    if j >= 2:
                        z_done(act, j - 2)
                    act.activation(shift_buf[j % 2][:, 1:T + 1], bank(2 + j % 2), ACT.Copy,
                                   scale=vec[:, V_MU + what:V_MU + what + 1]).then_inc(z_shift, 1)
                    if j == 1:
                        z_done(act, 1)
                        act.activation(z[0:64, 12, :], z[0:64, 12, :], ACT.Tanh).then_inc(lo_ready, 1)
                        act.activation(z[:, 13, :], z[:, 13, :], ACT.Sigmoid).then_inc(lo_ready, 1)
                elif z_reader(j) == "act":
                    act.wait_ge(z_mm, j + 1)
                    act.activation(k_pair[:, what - 18, :], bank(2 + j % 2), ACT.Copy).then_inc(z_act, 1)

            def exp(u):
                h, i = units()[u]
                n = P * (i + 1)
                act.wait_ge(att_max, u + 1)
                act.activation(prob[:, u % 4, 0:n], prob[:, u % 4, 0:n], ACT.Exp, bias=nmax[:, u:u + 1],
                               accum_out=psumrow[:, u:u + 1]).then_inc(att_exp, 1)

            def evac_t(u):
                h, i = units()[u]
                if u % 8 == 0 and u >= 16:
                    act.wait_ge(att_pv, u // 8 - 1)
                act.wait_ge(att_tr, u + 1)
                act.activation(prob_t[:, (h // 2) % 2, h % 2, pt_col(i, 0):pt_col(i, i) + P], bank(6 + u % 2)[:, 0:P * (i + 1)], ACT.Copy).then_inc(att_pt, 1)

            def evac_y(pr):
                act.wait_ge(att_pv, pr + 1)
                act.activation(y_att[:, pr, :], bank(2 + pr % 2), ACT.Copy).then_inc(att_y, 1)

            for step in range(4 * NH + 7):
                if step < 4 * NH:
                    exp(step)
                if 3 <= step < 4 * NH + 3:
                    evac_t(step - 3)
                if step >= 14 and (step - 14) % 8 == 0:
                    evac_y((step - 14) // 8)

            def slot(k, seq, prep):
                if prep is not None:
                    q = prep
                    w0, a0, kk = (vec[:, v + q:v + q + 1] for v in (V_W0, V_A0, V_KK))
                    if k == 0:
                        act.wait_ge(prep_out, q)
                        act.wait_ge(prep_mm, 5 * q + 1)
                        act.activation(sgw, bank(6), ACT.Sigmoid, bias=w0).then_inc(sg_ready, 1)
                        act.activation(knorm, z[:, 4 + q, :], ACT.Square, scale=kk).then_inc(ksq_ready, 1)
                    if k == 1:
                        act.wait_ge(prep_mm, 5 * q + 2)
                        act.activation(iclr, bank(6), ACT.Sigmoid, bias=a0).then_inc(aa_ready, 1)
                    if k == 3:
                        act.wait_ge(cum_split, 2 * q + 2)
                        act.activation(dec, cum, ACT.Exp, scale=-DECAY_SCALE).then_inc(decay_ready, 1)
                        act.activation(cum_x, cum_x, ACT.Exp, scale=-DECAY_SCALE).then_inc(decay_ready, 1)
                        act.activation(cum, cum, ACT.Exp, scale=DECAY_SCALE).then_inc(decay_ready, 1)
                        act.activation(cum_e, cum_e, ACT.Exp, scale=-DECAY_SCALE).then_inc(decay_ready, 1)
                    if k == 4:
                        act.wait_ge(ksum_ready, q + 1)
                        chain(act.activation(knorm, knorm, ACT.Ln))
                        act.activation(knorm, knorm, ACT.Exp, scale=-0.5, bias=norm_bias).then_inc(kn_ready, 1)
                    if k == 5:
                        act.wait_ge(rk_ready, q + 1)
                        act.wait_ge(rt_ready, q + 1)
                        act.wait_ge(prep_mm, 5 * q + 5)
                        act.activation(z[:, q, :], bank(6), ACT.Copy).then_inc(g_ready, 1)
                if seq is not None:
                    if k == 7:
                        act.wait_ge(yc_ready, seq + 1)
                        act.activation(r_eff, y_buf, ACT.Square).then_inc(ysq_ready, 1)
                    if k == 8:
                        act.wait_ge(stat_mm, 2 * seq + 2)
                        chain(act.activation(r_eff, bank(7), ACT.Ln, scale=1.0 / HD, bias=gn_eps))
                        act.activation(r_eff, r_eff, ACT.Exp, scale=-0.5).then_inc(rstd_ready, 1)

            act.wait_ge(rwkv_zero, 1)
            for k in range(NSLOT):
                slot(k, None, 0)
            for p in range(NP):
                for t in range(NT):
                    act.wait_ge(tok_mm, NT * p + t + 1)
                    b = bank(4 + t % 2)
                    act.activation(rhs[:, t, :, 0:HD], b[:, 0:P].rearrange("p (h d) -> p h d", h=2), ACT.Copy)
                    act.activation(v_rows[:, t, :], b[:, P:2 * P], ACT.Copy)
                    act.activation(bk_chunk[0:64, t, 0, :], b[0:64, 2 * P:4 * P], ACT.Copy)
                    act.activation(bk_chunk[64:128, t, 1, :], b[64:128, 2 * P:4 * P], ACT.Copy).then_inc(tok_ready, 1)
                for s in range(2):
                    act.wait_ge(tr_mm, 2 * LV * p + s + 1)
                    act.activation(mats(t_inv)(s), bank(4 + s).rearrange("p (m t) -> p m t", t=P), ACT.Copy).then_inc(tt_ready, 1)
                act.wait_ge(g_mm, p + 1)
                act.activation(rhs[:, :, :, HD:P], bank(6).rearrange("p (n h d) -> p n h d", n=NT, h=2), ACT.Copy).then_inc(ga_ready, 1)
                for l in range(1, LV + 1):
                    m = LV * p + l - 1
                    for s in range(2):
                        if l >= 2:
                            act.wait_ge(tr_mm, 2 * m + s + 1)
                            act.activation(mats(t_inv_t)(s), bank(4 + s).rearrange("p (m t) -> p m t", t=P), ACT.Copy).then_inc(tt_ready, 1)
                        act.wait_ge(x_mm, 2 * m + s + 1)
                        act.activation(mats(m_t)(s), bank(s).rearrange("p (m t) -> p m t", t=P), ACT.Copy).then_inc(x_ready, 1)
                    for s in range(2):
                        slot(2 * (l - 1) + s, p - 1 if p else None, p + 1 if p + 1 < NP else None)
                for s in range(2):
                    act.wait_ge(w_mm, 2 * p + s + 1)
                    for t in (2 * s, 2 * s + 1):
                        ins = act.activation(wy[:, t, :, :, :].rearrange("p x h d -> p h x d"),
                                             bank(s)[:, (t % 2) * 2 * P:(t % 2 + 1) * 2 * P].rearrange("p (h x d) -> p h x d", h=2, x=2), ACT.Copy)
                    ins.then_inc(w_ready, 1)
                act.wait_ge(yr_ready, p)
                act.wait_ge(y0_mm, p + 1)
                act.activation(y_buf, bank(3), ACT.Copy).then_inc(y0_ready, 1)
                act.wait_ge(s_ready, 7 * p)
                for s in range(2):
                    act.wait_ge(q_mm, 2 * p + s + 1)
                    act.activation(step_add[:, 4 * s:4 * s + 4, :], bank(s).rearrange("p (c i) -> p c i", i=P), ACT.Copy).then_inc(q_ready, 1)
            for k in range(NSLOT):
                slot(k, NP - 1, None)

            def rms_rows(t, rows, junk, ssq, rsq):
                chain(act.activation(junk, rows, ACT.Square, accum_out=ssq[:, t:t + 1]))
                chain(act.activation(ssq[:, t:t + 1], ssq[:, t:t + 1], ACT.Ln, scale=1.0 / D, bias=rms_eps))
                act.activation(rsq[:, t:t + 1], ssq[:, t:t + 1], ACT.Exp, scale=-0.5).then_inc(rs_ready, 1)

            for t in range(NT):
                act.wait_ge(h_ready, 2 * t + 2)
                rms_rows(t, h_res[:, t, :], n_rows[:, t, :], ss2, rs2)
            act.wait_ge(routed, GROUP_DIFF)
            act.activation(g_exp, g_exp, ACT.Exp).then_inc(route_exp, 1)
            act.wait_ge(routed, EXPERT_DIFF)
            act.activation(e_ratio, e_ratio, ACT.Exp).then_inc(route_exp, 1)
            act.wait_ge(ple_mm, 1)
            for k in range(KE):
                act.activation(ple_pt[:, k, :], bank(6 + k), ACT.Copy).then_inc(ple_t_ready, 1)

            def expert_pass(it, first=False):
                for s in range(2):
                    act.wait_ge(up_mm, it * 2 + s + 1)
                    act.activation(hid[s], bank(2 + s)[:, 0:DE], ACT.Silu).then_inc(silu_ready, 1)
                    act.wait_ge(hid_mm, it * 2 + s + 1)
                    act.activation(hid_t[s], bank(4)[:, 0:2 * P].rearrange("p (k t) -> p k t", k=KE), ACT.Copy).then_inc(hidt_ready, 1)
                    act.wait_ge(down_mm, it * 4 + 2 * s + 1)
                    if not first:
                        act.wait_ge(y_out[s], it * 32)
                    act.activation(y_slot[s][:, 0:512], bank(5), ACT.Copy).then_inc(y_lo, 1)

            expert_pass(0, first=True)
            with act.Fori(1, NPAIR // 2) as it:
                expert_pass(it)
            with if_over(act):
                with act.Fori(0, NE) as e:
                    for t in range(NT):
                        act.wait_ge(over_mm, over_up(e, t))
                        act.activation(hid[0], bank(2)[:, 0:DE], ACT.Silu).then_inc(over_act, 1)
                        act.wait_ge(over_mm, over_turned(e, t))
                        act.activation(hid_t[0], bank(4)[:, 0:2 * P].rearrange("p (k t) -> p k t", k=KE), ACT.Copy).then_inc(over_act, 1)
            for t in range(NT):
                act.wait_ge(h_ready, 2 * NT + t + 1)
                rms_rows(t, h_res[:, t, :], n_rows[:, t, :], ss3, rs3)
            for t in range(NT):
                act.wait_ge(gate_pre, t + 1)
                act.activation(gate[t % 2], gate[t % 2], ACT.Sigmoid).then_inc(gate_ready, 1)
                act.wait_ge(h_ready, 3 * NT + t + 1)
                if t >= 2:
                    act.wait_ge(out_stored[t % 2], 16 * (t // 2))
                rms_rows(t, h_res[:, t, :], out_rows[t % 2], ss4, rs4)

        @block.vector
        def _(dve):
            steps = [0]

            def chain(ins):
                steps[0] += 1
                ins.then_inc(dve_step, 1)
                dve.wait_ge(dve_step, steps[0])

            dve.memset(gn_eps, GN_EPS)
            dve.memset(norm_bias, 0.5 * NORM_SCALE_LOG2 * math.log(2.0))
            dve.memset(rms_eps, RMS_EPS).then_inc(eps_ready, 1)
            dve.wait_ge(consts_in, 32)
            dve.tensor_scalar(one_mu, vec[:, V_MU:V_MU + 14], -1.0, 1.0, ALU.mult, ALU.add)
            for t in range(NT):
                dve.wait_ge(rs_ready, t + 1)
                dve.tensor_scalar(x_norm[:, t, :], x_in_sb[:, t, :], rs[:, t:t + 1], None, ALU.mult).then_inc(xn_ready, 1)
            for k in range(1, KD, 2):
                dve.wait_ge(xt_mm, k + 1)
                dve.tensor_scalar(h_feat[:, k, :], bank(k % 2), vec[:, V_MIX + k:V_MIX + k + 1], None, ALU.mult).then_inc(hf_dve, 1)
            dve.wait_ge(zeros_ready, 5 + NH)
            for j, (n, kind, what) in enumerate(jobs):
                if z_reader(j) != "dve":
                    continue
                dve.wait_ge(z_mm, j + 1)
                zb = bank(2 + j % 2)
                if kind == "tok":
                    half, t = what
                    dve.tensor_copy(v_tok[:, t, half * SLAB:(half + 1) * SLAB], zb[:, 0:SLAB]).then_inc(z_dve, 1)
                elif what < 14:
                    dve.wait_ge(z_shift, j + 1)
                    dve.scalar_tensor_tensor(out=z[:, what, :], in0=zb, scalar=one_mu[:, what:what + 1],
                                             in1=shift_buf[j % 2][:, 0:T], op0=ALU.mult, op1=ALU.add).then_inc(z_dve, 1)
                else:
                    h = 2 * (what - 14)
                    dve.tensor_scalar(q_head[0:64, h, :], zb[0:64, :], HD ** -0.5, None, ALU.mult)
                    dve.tensor_scalar(q_head[64:128, h + 1, :], zb[64:128, :], HD ** -0.5, None, ALU.mult).then_inc(z_dve, 1)

            def scores(u):
                h, i = units()[u]
                n = P * (i + 1)
                dve.wait_ge(att_s_mm, u + 1)
                if i == 0:
                    dve.wait_ge(bias_masked, h + 1)
                if u >= 4:
                    dve.wait_ge(att_tr, u - 3)
                dve.tensor_tensor(prob[:, u % 4, 0:n], bank(4 + u % 2)[:, 0:n], bias_w[:, h % 4, T - n:T], ALU.add).then_inc(att_s_read, 1)
                dve.wait_ge(att_s_read, u + 1)
                dve.tensor_reduce(nmax[:, u:u + 1], prob[:, u % 4, 0:n], AX.X, ALU.max, negate=True).then_inc(att_max, 1)

            def normalise(u):
                h, i = units()[u]
                n = P * (i + 1)
                dve.wait_ge(att_exp, u + 1)
                chain(dve.reciprocal(prow_inv[:, u:u + 1], psumrow[:, u:u + 1]))
                dve.tensor_scalar(prob[:, u % 4, 0:n], prob[:, u % 4, 0:n], prow_inv[:, u:u + 1], None, ALU.mult).then_inc(att_p, 1)

            for step in range(4 * NH + 1):
                if step < 4 * NH:
                    scores(step)
                if step >= 1:
                    normalise(step - 1)

            def slot(k, seq, prep):
                if seq is not None:
                    q = seq
                    if k < 7:
                        if k == 0:
                            dve.wait_ge(q_ready, 2 * q + 2)
                        else:
                            dve.wait_ge(seq_mm, 6 * q + k)
                        for h in range(2):
                            rows, d = slice(64 * h, 64 * h + 64), slice(64 * h, 64 * h + 64)
                            if k == 0:
                                ins = dve.tensor_copy(state[rows, 1, d], step_add[rows, 0, d])
                            else:
                                ins = dve.tensor_tensor(state[rows, k + 1, d], bank(7)[rows, 64 * h + P * (k % 4):64 * h + P * (k % 4) + 64],
                                                        step_add[rows, k, d], ALU.add)
                        ins.then_inc(s_ready, 1)
                    if k == 7:
                        dve.wait_ge(y_mm, q + 1)
                        dve.wait_ge(y0_ready, q + 1)
                        dve.tensor_tensor(y_buf[:, C:T], bank(7)[:, C:T], y_buf[:, C:T], ALU.add).then_inc(y_ready, 1)
                        dve.wait_ge(y_ready, q + 1)
                        dve.wait_ge(stat_mm, 2 * q + 1)
                        dve.scalar_tensor_tensor(out=y_buf, in0=bank(7), scalar=-1.0 / HD, in1=y_buf, op0=ALU.mult, op1=ALU.add).then_inc(yc_ready, 1)
                        dve.wait_ge(yc_ready, q + 1)
                    if k == 9:
                        dve.wait_ge(rstd_ready, q + 1)
                        chain(dve.scalar_tensor_tensor(out=y_buf, in0=y_buf, scalar=vec[:, V_LNW + q:V_LNW + q + 1], in1=r_eff, op0=ALU.mult, op1=ALU.mult))
                        chain(dve.scalar_tensor_tensor(out=y_buf, in0=y_buf, scalar=vec[:, V_LNB + q:V_LNB + q + 1], in1=z[:, 4 + q, :], op0=ALU.add, op1=ALU.add))
                        dve.wait_ge(g_ready, q + 1)
                        dve.tensor_tensor(z[:, 8 + q, :], y_buf, z[:, q, :], ALU.mult).then_inc(yr_ready, 1)
                if prep is not None:
                    q = prep
                    r, kq, v = z[:, q, :], z[:, 4 + q, :], z[:, 8 + q, :]
                    if k == 0:
                        chain(dve.tensor_scalar(kkn, kq, vec[:, V_KK + q:V_KK + q + 1], None, ALU.mult))
                        dve.wait_ge(sg_ready, q + 1)
                        dve.tensor_tensor_scan(cum, const[:, K_RESET:K_RESET + T], sgw, 0.0, ALU.mult, ALU.add).then_inc(cum_ready, 1)
                    if k == 2:
                        dve.wait_ge(prep_mm, 5 * q + 3)
                        dve.tensor_scalar(knorm, bank(6), 1e-24, 2.0 ** NORM_SCALE_LOG2, ALU.max, ALU.mult).then_inc(ksum_ready, 1)
                        dve.wait_ge(aa_ready, q + 1)
                        chain(dve.tensor_scalar(k_mod, iclr, -1.0, vec[:, V_KA + q:V_KA + q + 1], ALU.add, ALU.mult))
                        chain(dve.scalar_tensor_tensor(out=k_mod, in0=k_mod, scalar=1.0, in1=kq, op0=ALU.add, op1=ALU.mult))
                    if k == 3:
                        dve.wait_ge(cum_split, 2 * q + 2)
                        dve.scalar_tensor_tensor(out=sgw, in0=r, scalar=vec[:, V_RK + q:V_RK + q + 1], in1=k_mod, op0=ALU.mult, op1=ALU.mult).then_inc(rk_ready, 1)
                    if k == 4:
                        dve.wait_ge(decay_ready, 4 * q + 1)
                        dve.tensor_copy(d_end[q % 2], dec[:, C - 1::C])
                        dve.tensor_tensor(r_dec[q % 2], r, dec, ALU.mult).then_inc(rt_ready, 1)
                        dve.wait_ge(prep_mm, 5 * q + 4)
                        dve.tensor_tensor(kq, bank(6), v, ALU.mult).then_inc(bonus_ready, 1)
                    if k == 5:
                        dve.wait_ge(kn_ready, q + 1)
                        chain(dve.tensor_tensor(kkn, kkn, knorm, ALU.mult))
                        dve.wait_ge(unit_in_used, q)
                        dve.wait_ge(ar_ready, 4 * q)
                        dve.wait_ge(decay_ready, 4 * q + 2)
                        dve.scalar_tensor_tensor(out=a_dec, in0=kkn, scalar=-1.0, in1=cum_x, op0=ALU.mult, op1=ALU.mult).then_inc(at_ready, 1)
                        chain(dve.tensor_tensor(knorm, kkn, iclr, ALU.mult))
                    if k == 6:
                        dve.wait_ge(decay_ready, 4 * q + 4)
                        dve.tensor_tensor(b_inc, knorm, cum, ALU.mult)
                        dve.tensor_tensor(k_inc, k_mod, cum, ALU.mult)
                    if k == 7:
                        dve.tensor_tensor(b_end, knorm, cum_e, ALU.mult)
                        dve.tensor_tensor(k_end, k_mod, cum_e, ALU.mult).then_inc(prep_out, 1)

            dve.wait_ge(rwkv_zero, 1)
            for k in range(NSLOT):
                slot(k, None, 0)
            for p in range(NP):
                for t in range(NT):
                    dve.wait_ge(s1_mm, NT * p + t + 1)
                    dve.tensor_tensor(within[:, t, :], bank(6), const[:, K_MASK:K_MASK + 4 * P], ALU.mult).then_inc(within_ready, 1)
                    dve.wait_ge(s2_mm, NT * p + t + 1)
                    dve.tensor_tensor(across[:, t, :], bank(7), const[:, K_MASK:K_MASK + 4 * P], ALU.mult).then_inc(across_ready, 1)
                dve.wait_ge(within_ready, NT * (p + 1))
                for s in range(2):
                    chain(dve.tensor_tensor(heads4(mats(t_inv_t)(s)), n_of(s), over(level_mask(0)), ALU.mult))
                    dve.tensor_tensor(heads4(mats(t_inv_t)(s)), heads4(mats(t_inv_t)(s)), over(ident), ALU.add).then_inc(tt_init, 1)
                for l in range(1, LV + 1):
                    m = LV * p + l - 1
                    for s in range(2):
                        dve.wait_ge(d_mm, 2 * m + s + 1)
                        dst = mats(t_inv if l < LV else t_inv_t)(s)
                        dve.tensor_tensor(dst, bank(2 + s).rearrange("p (m t) -> p m t", t=P), dst, ALU.add).then_inc(t_ready, 1)
                        slot(2 * (l - 1) + s, p - 1 if p else None, p + 1 if p + 1 < NP else None)
                dve.wait_ge(rp_mm, p + 1)
                dve.tensor_tensor(r_eff, bank(2), r_dec[p % 2], ALU.add).then_inc(rp_ready, 1)
                for s in range(2):
                    dve.wait_ge(mc_mm, 2 * p + s + 1)
                    for c in range(4 * s, 4 * s + 4):
                        ins = dve.scalar_tensor_tensor(out=step_mat[:, c, :], in0=ident, scalar=d_end[p % 2][:, c:c + 1],
                                                       in1=bank(4 + s)[:, (c % 4) * P:(c % 4 + 1) * P], op0=ALU.mult, op1=ALU.add)
                    ins.then_inc(mc_ready, 1)
            for k in range(NSLOT):
                slot(k, NP - 1, None)

            dve.wait_ge(res_in, 16)
            for o in range(2 * NT):
                t, n = o // 2, o % 2
                dve.wait_ge(op_mm, o + 1)
                dve.tensor_tensor(h_res[:, t, n * 512:(n + 1) * 512], bank(o), h_res[:, t, n * 512:(n + 1) * 512], ALU.add).then_inc(h_ready, 1)

            def turn_rows(t, n_t, b0, mm, mm_at, w, ready):
                for g in range(2):
                    dve.wait_ge(mm, mm_at + g)
                    scale = vec[:, w + 4 * g:w + 4 * g + 4].unsqueeze(2).to_broadcast([P, 4, P])
                    ins = dve.tensor_tensor(n_t[:, 4 * g:4 * g + 4, :], bank(b0 + g).rearrange("p (k t) -> p k t", k=4), scale, ALU.mult)
                ins.then_inc(ready, 1)

            for t in range(NT):
                dve.wait_ge(rs_ready, NT + t + 1)
                dve.tensor_scalar(n_rows[:, t, :], h_res[:, t, :], rs2[:, t:t + 1], None, ALU.mult).then_inc(xn_ready, 1)
            for t in range(NT):
                turn_rows(t, n_feat[:, t], 2 * (t % 2), nrow_mm, 2 * t + 1, V_FFN, nf_ready)
            dve.wait_ge(router_in, 32)
            dve.memset(g_logit[:, :, NG:8], NEG)
            dve.tensor_copy(tok_u, const[:, K_TOK:K_TOK + NT])
            dve.wait_ge(route_mm, 1)
            lg = bank(4)[:, 0:NT * (NG + NE)].rearrange("p (n e) -> p n e", n=NT)
            bias = router_b.unsqueeze(1).to_broadcast([P, NT, NG + NE])
            chain(dve.tensor_tensor(g_logit[:, :, 0:NG], lg[:, :, 0:NG], bias[:, :, 0:NG], ALU.add))
            chain(dve.tensor_tensor(e_logit.rearrange("p n g e -> p n (g e)"), lg[:, :, NG:], bias[:, :, NG:], ALU.add))
            for t in range(NT):
                chain(dve.max(g_top[:, t, :], g_logit[:, t, :]))
                chain(dve.max_index(g_idx[:, t, :], g_top[:, t, :], g_logit[:, t, :]))
            dve.tensor_copy(g_sel.unsqueeze(2), g_idx[:, :, 0:1])
            dve.tensor_tensor(g_exp, g_logit[:, :, 0:NG], g_top[:, :, 0:1].to_broadcast([P, NT, NG]), ALU.subtract).then_inc(routed, 1)
            dve.wait_ge(routed, GROUP_DIFF)
            iota = const[:, K_IOTA:K_IOTA + NE].unsqueeze(1)
            chain(dve.tensor_tensor(g_hot, iota[:, :, 0:NG].to_broadcast([P, NT, NG]), g_sel.unsqueeze(2).to_broadcast([P, NT, NG]), ALU.is_equal))
            chain(dve.tensor_tensor(e_mask.rearrange("p n e g -> p n g e"), e_logit, g_hot.unsqueeze(3).to_broadcast([P, NT, NG, EPG]), ALU.mult))
            chain(dve.tensor_reduce(sel, e_mask, AX.X, ALU.add))
            for t in range(NT):
                chain(dve.max(e_top[:, t, :], sel[:, t, :]))
                chain(dve.max_index(e_idx[:, t, :], e_top[:, t, :], sel[:, t, :]))
            dve.tensor_tensor(e_ratio.unsqueeze(2), e_top[:, :, 1:2], e_top[:, :, 0:1], ALU.subtract).then_inc(routed, 1)
            chain(dve.tensor_copy(e_loc, e_idx[:, :, 0:2]))
            chain(dve.scalar_tensor_tensor(out=expert, in0=g_sel.unsqueeze(2).to_broadcast([P, NT, 2]), scalar=float(EPG), in1=e_loc, op0=ALU.mult, op1=ALU.add))
            for x in range(2):
                chain(dve.tensor_tensor(hot[x], iota.to_broadcast([P, NT, NE]), expert[:, :, x:x + 1].to_broadcast([P, NT, NE]), ALU.is_equal))
            dve.tensor_tensor(hot_sum, hot[0], hot[1], ALU.add).then_inc(routed, 1)
            dve.wait_ge(route_exp, 1)
            chain(dve.tensor_reduce(g_sum, g_exp, AX.X, ALU.add))
            chain(dve.reciprocal(p_group, g_sum))
            dve.wait_ge(route_exp, 2)
            chain(dve.tensor_scalar(g_sum, e_ratio, 1.0, None, ALU.add))
            chain(dve.reciprocal(g_sum, g_sum))
            chain(dve.tensor_tensor(weight[:, :, 0:1], p_group.unsqueeze(2), g_sum.unsqueeze(2), ALU.mult))
            chain(dve.tensor_tensor(weight[:, :, 1:2], weight[:, :, 0:1], e_ratio.unsqueeze(2), ALU.mult))
            dve.wait_ge(route_mm, 2)
            rank = bank(5)[:, 0:NT * NE].rearrange("p (n e) -> p n e", n=NT)
            for x in range(2):
                chain(dve.tensor_tensor(hot_pos, rank, hot[x], ALU.mult))
                chain(dve.tensor_reduce(pos[:, :, x:x + 1].rearrange("p n o -> p (n o)"), hot_pos, AX.X, ALU.add))
            chain(dve.scalar_tensor_tensor(out=slot_f, in0=pos, scalar=float(NE), in1=expert, op0=ALU.mult, op1=ALU.add))
            dve.tensor_copy(slot_u, slot_f)
            chain(dve.tensor_scalar(fits, pos, float(CAP), None, ALU.is_lt))
            dve.tensor_tensor(w_main, weight, fits, ALU.mult)
            chain(dve.tensor_tensor(slot_f, slot_f, fits, ALU.mult))
            dve.tensor_copy(y_row, slot_f).then_inc(routed, 1)
            chain(dve.tensor_scalar(fits, fits, -1.0, 1.0, ALU.mult, ALU.add))
            chain(dve.tensor_reduce(over_rows, fits, AX.XY, ALU.add))
            dve.tensor_tensor(pos, weight, fits, ALU.mult).then_inc(over_counted, 1)
            dve.wait_ge(over_counted, 1)
            for x in range(2):
                chain(dve.tensor_tensor(hot[x], hot[x], pos[:, :, x:x + 1].to_broadcast([P, NT, NE]), ALU.mult))
            dve.tensor_tensor(w_over, hot[0], hot[1], ALU.add)
            dve.wait_ge(route_mm, 3)
            dve.tensor_copy(over_u, bank(5)[:, 0:1]).then_inc(routed, 1)

            def expert_rows(s, it):
                for g in range(2):
                    dve.wait_ge(xs_mm, it * 4 + 2 * s + 1 + g)
                    scale = vec[:, V_FFN + 4 * g:V_FFN + 4 * g + 4].unsqueeze(2).to_broadcast([P, 4, P])
                    ins = dve.tensor_tensor(x_slot_t[s][:, 4 * g:4 * g + 4, :], bank(g).rearrange("p (k t) -> p k t", k=4), scale, ALU.mult)
                ins.then_inc(xs_ready, 1)

            def expert_pass(it, last=False):
                for s in range(2):
                    dve.wait_ge(silu_ready, it * 2 + s + 1)
                    dve.tensor_tensor(hid[s], bank(2 + s)[:, DE:2 * DE], hid[s], ALU.mult).then_inc(hid_ready, 1)
                    if not (last and s == 1):
                        expert_rows(1 - s, it + s)
                    dve.wait_ge(down_mm, it * 4 + 2 * s + 2)
                    dve.wait_ge(y_lo, it * 2 + s + 1)
                    dve.tensor_copy(y_slot[s][:, 512:D], bank(6)).then_inc(y_hi, 1)

            expert_rows(0, 0)
            with dve.Fori(0, NPAIR // 2 - 1) as it:
                expert_pass(it)
            expert_pass(NPAIR // 2 - 1, last=True)
            with if_over(dve):
                scale = vec[:, V_FFN:V_FFN + KD].unsqueeze(2).to_broadcast([P, KD, P])
                for t in range(NT):
                    for g in range(2):
                        dve.wait_ge(over_mm, 2 * t + 1 + g)
                        ins = dve.tensor_tensor(over_feat[:, t, 4 * g:4 * g + 4, :], bank(2 * (t % 2) + g).rearrange("p (k t) -> p k t", k=4),
                                                scale[:, 4 * g:4 * g + 4, :], ALU.mult)
                    ins.then_inc(over_dve, 1)
                with dve.Fori(0, NE) as e:
                    dve.wait_ge(over_dve, over_col(e) - 1)
                    dve.tensor_copy(w_col.unsqueeze(2), w_over[:, :, bass.ds(e, 1)]).then_inc(over_dve, 1)
                    dve.wait_ge(over_dve, over_col(e))
                    for t in range(NT):
                        dve.wait_ge(over_act, over_silu(e, t))
                        dve.tensor_tensor(hid[0], bank(2)[:, DE:2 * DE], hid[0], ALU.mult).then_inc(over_dve, 1)
                        dve.wait_ge(over_mm, over_down(e, t))
                        for n in range(2):
                            half = slice(n * 512, (n + 1) * 512)
                            ins = dve.scalar_tensor_tensor(out=h_res[:, t, half], in0=bank(5 + n), scalar=w_col[:, t:t + 1],
                                                           in1=h_res[:, t, half], op0=ALU.mult, op1=ALU.add)
                        ins.then_inc(over_dve, 1)
                dve.wait_ge(over_dve, over_col(NE - 1) + 2 * NT)
            for t in range(NT):
                dve.wait_ge(y_tok_in[t % 2], 32 * (t // 2 + 1))
                for x in range(2):
                    ins = dve.scalar_tensor_tensor(out=h_res[:, t, :], in0=y_tok[t % 2][x], scalar=w_main[:, t, x:x + 1], in1=h_res[:, t, :], op0=ALU.mult, op1=ALU.add)
                    if x == 0:
                        chain(ins)
                ins.then_inc(h_ready, 1)
                dve.wait_ge(rs_ready, 2 * NT + t + 1)
                dve.tensor_scalar(n_rows[:, t, :], h_res[:, t, :], rs3[:, t:t + 1], None, ALU.mult).then_inc(xn_ready, 1)
                turn_rows(t, n3_feat[:, t], 2 * (t % 2), nrow_mm, 2 * NT + 2 * t + 1, V_PLE, nf_ready)
            dve.wait_ge(ple_in, 64)
            for t in range(NT):
                for n in range(2):
                    half = slice(n * 512, (n + 1) * 512)
                    dve.wait_ge(gate_mm, 2 * t + n + 1)
                    ins = dve.tensor_tensor(gate[t % 2][:, half], bank(4 + n), gate_b[:, half], ALU.add)
                ins.then_inc(gate_pre, 1)
                dve.wait_ge(gate_ready, t + 1)
                for n in range(2):
                    half = slice(n * 512, (n + 1) * 512)
                    dve.wait_ge(proj_mm, 2 * t + n + 1)
                    chain(dve.tensor_tensor(gate[t % 2][:, half], bank(6 + n), gate[t % 2][:, half], ALU.mult))
                dve.tensor_tensor(h_res[:, t, :], h_res[:, t, :], gate[t % 2], ALU.add).then_inc(h_ready, 1)
                dve.wait_ge(rs_ready, 3 * NT + t + 1)
                dve.scalar_tensor_tensor(out=out_rows[t % 2], in0=h_res[:, t, :], scalar=rs4[:, t:t + 1], in1=final_w, op0=ALU.mult, op1=ALU.mult).then_inc(out_ready, 1)

        @block.tensor
        def _(pe):
            pe.wait_ge(consts_in, 32)
            for k in range(KD):
                if k == 2 or k == 3:
                    pe.wait_ge(xn_ready, NT)
                if k >= 2:
                    pe.wait_ge((hf_act, hf_dve)[k % 2], k // 2)
                for t in range(NT):
                    if k == 0:
                        pe.wait_ge(xn_ready, t + 1)
                    ins = pe.transpose(bank(k % 2)[:, t * P:(t + 1) * P], x_norm[:, t, k:k + (P - 1) * KD + 1:KD], ident)
                ins.then_inc(xt_mm, 1)
            pe.wait_ge(hf_act, KD // 2)
            pe.wait_ge(hf_dve, KD // 2)
            for j, (n, kind, what) in enumerate(jobs):
                pe.wait_ge(slab_in[n % RING], 16 * (n // RING + 1))
                if j >= 2:
                    z_done(pe, j - 2)
                zb = bank(2 + j % 2)
                for k in range(KD):
                    if kind == "tok":
                        ins = pe.matmul(zb[:, 0:SLAB], h_feat[:, k, what[1] * P:(what[1] + 1) * P], slabs[:, n % RING, k, :],
                                        start=(k == 0), stop=(k == KD - 1))
                    else:
                        c = (what % 2) * P
                        ins = pe.matmul(zb, slabs[:, n % RING, k, c:c + P], h_feat[:, k, :], start=(k == 0), stop=(k == KD - 1))
                ins.then_inc(z_mm, 1)
                if last_job[n] == j:
                    pe.wait_ge(z_mm, j + 1)
                    pe.sem_inc(slab_used, 1)
            pe.wait_ge(z_act, z_count(NJ - 1, "act"))
            pe.wait_ge(z_dve, z_count(NJ - 1, "dve"))

            def scores(u):
                h, i = units()[u]
                if u >= 2:
                    pe.wait_ge(att_s_read, u - 1)
                n = P * (i + 1)
                pe.matmul(bank(4 + u % 2)[:, 0:n], q_head[:, h, i * P:(i + 1) * P], k_pair[:, h // 2, 0:n],
                          start=True, stop=True).then_inc(att_s_mm, 1)

            def turn(u):
                h, i = units()[u]
                pe.wait_ge(att_p, u + 1)
                if u >= 2:
                    pe.wait_ge(att_pt, u - 1)
                for j in range(i + 1):
                    ins = pe.transpose(bank(6 + u % 2)[:, j * P:(j + 1) * P], prob[:, u % 4, j * P:(j + 1) * P], ident)
                ins.then_inc(att_tr, 1)

            def values(pr):
                pe.wait_ge(att_pt, 8 * (pr + 1))
                if pr >= 2:
                    pe.wait_ge(att_y, pr - 1)
                for i in range(NT):
                    for j in range(i + 1):
                        for par in range(2):
                            h = 2 * pr + par
                            ins = pe.matmul(bank(2 + pr % 2)[64 * par:64 * par + 64, i * P:(i + 1) * P],
                                            v_tok[:, j, h * HD:(h + 1) * HD],
                                            prob_t[:, pr % 2, par, pt_col(i, j):pt_col(i, j) + P],
                                            start=(j == 0), stop=(j == i))
                ins.then_inc(att_pv, 1)

            for step in range(4 * NH + 7):
                if step < 4 * NH:
                    scores(step)
                if 3 <= step < 4 * NH + 3:
                    turn(step - 3)
                if step >= 13 and (step - 13) % 8 == 0:
                    values((step - 13) // 8)

            def slot(k, seq, prep):
                if seq is not None:
                    q = seq
                    if 1 <= k < 7:
                        pe.wait_ge(s_ready, 7 * q + k)
                        pe.matmul(bank(7)[:, P * (k % 4):P * (k % 4) + P], step_mat[:, k, :], state[:, k, :], start=True, stop=True).then_inc(seq_mm, 1)
                    if k == 7:
                        pe.wait_ge(s_ready, 7 * q + 7)
                        for c in range(1, NC):
                            ins = pe.matmul(bank(7)[:, c * C:(c + 1) * C], state[:, c, :], r_eff[:, c * C:(c + 1) * C], start=True, stop=True)
                        ins.then_inc(y_mm, 1)
                        pe.wait_ge(y_ready, q + 1)
                        pe.matmul(bank(7), head_ones, y_buf, start=True, stop=True).then_inc(stat_mm, 1)
                    if k == 8:
                        pe.wait_ge(ysq_ready, q + 1)
                        pe.matmul(bank(7), head_ones, r_eff, start=True, stop=True).then_inc(stat_mm, 1)
                if prep is not None:
                    q = prep
                    cols = slice(q * P, (q + 1) * P)
                    if k == 0:
                        if q == 0:
                            pe.wait_ge(lo_ready, 2)
                            pe.wait_ge(lora_in, 48)
                            pe.wait_ge(zeros_ready, 3)
                        pe.matmul(bank(6), lora_w[:, 0, cols], z[:, 12, :], start=True, stop=True).then_inc(prep_mm, 1)
                    if k == 1:
                        pe.wait_ge(sg_ready, q + 1)
                        pe.matmul(bank(6), lora_w[:, 1, cols], z[:, 12, :], start=True, stop=True).then_inc(prep_mm, 1)
                    if k == 2:
                        pe.wait_ge(aa_ready, q + 1)
                        pe.wait_ge(ksq_ready, q + 1)
                        pe.matmul(bank(6), head_ones, knorm, start=True, stop=True).then_inc(prep_mm, 1)
                    if k == 4:
                        pe.wait_ge(ksum_ready, q + 1)
                        pe.wait_ge(rk_ready, q + 1)
                        pe.matmul(bank(6), head_ones, sgw, start=True, stop=True).then_inc(prep_mm, 1)
                    if k == 5:
                        pe.wait_ge(bonus_ready, q + 1)
                        pe.matmul(bank(6), lora_w[:, 2, cols], z[:, 13, :], start=True, stop=True).then_inc(prep_mm, 1)

            pe.wait_ge(rwkv_zero, 1)
            for k in range(NSLOT):
                slot(k, None, 0)
            for p in range(NP):
                pe.wait_ge(prep_out, p + 1)
                pe.wait_ge(ar_ready, 4 * (p + 1))
                pe.wait_ge(g_ready, p + 1)
                if p >= 2:
                    pe.wait_ge(rstd_ready, p - 1)
                pe.wait_ge(mc_ready, 2 * p)
                for t in range(NT):
                    tok = slice(t * P, (t + 1) * P)
                    if t:
                        pe.wait_ge(within_ready, NT * p + t)
                    pe.matmul(bank(6), b_inc[:, tok], ar_head[:, t, :], start=True, stop=True).then_inc(s1_mm, 1)
                    if t:
                        pe.wait_ge(across_ready, NT * p + t)
                    pe.matmul(bank(7), k_inc[:, tok], ar_head[:, t, :], start=True, stop=True).then_inc(s2_mm, 1)
                    if t >= 2:
                        pe.wait_ge(tok_ready, NT * p + t - 1)
                    for n, src in enumerate((a_dec, z[:, 8 + p, :], b_end, k_end)):
                        ins = pe.transpose(bank(4 + t % 2)[:, n * P:(n + 1) * P], src[:, tok], ident)
                    ins.then_inc(tok_mm, 1)
                pe.wait_ge(tok_mm, NT * (p + 1))
                pe.sem_inc(unit_in_used, 1)
                pe.wait_ge(tok_ready, NT * (p + 1))
                for s in range(2):
                    pe.wait_ge(tt_init, 2 * p + s + 1)
                    for m in range(4):
                        ins = pe.transpose(bank(4 + s)[:, m * P:(m + 1) * P], t_inv_t[:, 4 * s + m, :], ident)
                    ins.then_inc(tr_mm, 1)
                pe.wait_ge(across_ready, NT * (p + 1))
                for t in range(NT):
                    for h in range(2):
                        n = 2 * t + h
                        ins = pe.matmul(bank(6)[:, n * HD:(n + 1) * HD], across[:, t, 2 * h * P:(2 * h + 1) * P],
                                        v_rows[:, t, h * HD:(h + 1) * HD], start=True, stop=True)
                ins.then_inc(g_mm, 1)
                pe.wait_ge(ga_ready, p + 1)
                pe.wait_ge(q_ready, 2 * p)
                pe.wait_ge(rp_ready, p)
                pe.wait_ge(y0_ready, p)
                for l in range(1, LV + 1):
                    m = LV * p + l - 1
                    for s in range(2):
                        if l >= 2:
                            pe.wait_ge(t_ready, 2 * (m - 1) + s + 1)
                            for n in range(4):
                                ins = pe.transpose(bank(4 + s)[:, n * P:(n + 1) * P], t_inv[:, 4 * s + n, :], ident)
                            ins.then_inc(tr_mm, 1)
                        else:
                            pe.wait_ge(tt_ready, 2 * LV * p + s + 1)
                        pe.wait_ge(mt_ready, 2 * m + s + 1)
                        for n in range(4):
                            ins = pe.matmul(bank(s)[:, n * P:(n + 1) * P], m_level[m % 2][:, 4 * s + n, :], t_inv[:, 4 * s + n, :], start=True, stop=True)
                        ins.then_inc(x_mm, 1)
                    for s in range(2):
                        pe.wait_ge(x_ready, 2 * m + s + 1)
                        if l >= 2:
                            pe.wait_ge(tt_ready, 2 * m + s + 1)
                        for n in range(4):
                            i = 4 * s + n
                            if l < LV:
                                ins = pe.matmul(bank(2 + s)[:, n * P:(n + 1) * P], t_inv_t[:, i, :], m_t[:, i, :], start=True, stop=True)
                            else:
                                ins = pe.matmul(bank(2 + s)[:, n * P:(n + 1) * P], m_t[:, i, :], t_inv_t[:, i, :], start=True, stop=True)
                        ins.then_inc(d_mm, 1)
                        slot(2 * (l - 1) + s, p - 1 if p else None, p + 1 if p + 1 < NP else None)
                for s in range(2):
                    pe.wait_ge(t_ready, 2 * (LV * p + LV - 1) + s + 1)
                    for n in range(4):
                        i = 4 * s + n
                        ins = pe.matmul(bank(s)[:, n * P:(n + 1) * P], t_inv_t[:, i, :], rhs[:, i // 2, i % 2, :], start=True, stop=True)
                    ins.then_inc(w_mm, 1)
                if p:
                    pe.wait_ge(yr_ready, p)
                pe.wait_ge(w_ready, 2 * p + 2)
                for t in range(NT):
                    tok = slice(t * P, (t + 1) * P)
                    for h in range(2):
                        ins = pe.matmul(bank(2)[64 * h:64 * h + 64, tok], wy[:, t, 0, h, :], within[:, t, (2 * h + 1) * P:(2 * h + 2) * P], start=True, stop=True)
                ins.then_inc(rp_mm, 1)
                for t in range(NT):
                    tok = slice(t * P, (t + 1) * P)
                    for x in range(2):
                        for h in range(2):
                            if x == 0:
                                ins = pe.matmul(bank(3)[64 * h:64 * h + 64, tok], wy[:, t, 1, h, :], within[:, t, (2 * h + 1) * P:(2 * h + 2) * P], start=True, stop=False)
                            else:
                                ins = pe.matmul(bank(3)[64 * h:64 * h + 64, tok], v_rows[:, t, h * HD:(h + 1) * HD], across[:, t, (2 * h + 1) * P:(2 * h + 2) * P], start=False, stop=True)
                ins.then_inc(y0_mm, 1)
                for s in range(2):
                    for c in range(4 * s, 4 * s + 4):
                        ins = pe.matmul(bank(4 + s)[:, (c % 4) * P:(c % 4 + 1) * P], wy[:, c // 2, 0, :, :].rearrange("p h d -> p (h d)"),
                                        bk_chunk[:, c // 2, c % 2, 0:P], start=True, stop=True)
                    ins.then_inc(mc_mm, 1)
                for s in range(2):
                    for c in range(4 * s, 4 * s + 4):
                        o = bank(s)[:, (c % 4) * P:(c % 4 + 1) * P]
                        pe.matmul(o, bk_chunk[:, c // 2, c % 2, 0:P], wy[:, c // 2, 1, :, :].rearrange("p h d -> p (h d)"), start=True, stop=False)
                        ins = pe.matmul(o, bk_chunk[:, c // 2, c % 2, P:2 * P], v_rows[:, c // 2, :], start=False, stop=True)
                    ins.then_inc(q_mm, 1)
            def project(o, rows, start):
                t, n = o // 2, o % 2
                for k in rows:
                    src = z[:, 8 + k, :] if k < NP else y_att[:, k - NP, :]
                    ins = pe.matmul(bank(o), src[:, t * P:(t + 1) * P], w_out[:, k, n * 512:(n + 1) * 512],
                                    start=(start and k == rows[0]), stop=(k == NP - 1))
                return ins

            pe.wait_ge(w_out_in[1], 16)
            pe.wait_ge(q_ready, 2 * NP)
            pe.wait_ge(rp_ready, NP)
            pe.wait_ge(y0_ready, NP)
            pe.wait_ge(mc_ready, 2 * NP)
            for k in range(NSLOT):
                if k < 7:
                    project(k, range(NP, 2 * NP), True)
                slot(k, NP - 1, None)
            pe.wait_ge(w_out_in[0], 16)
            pe.wait_ge(yr_ready, NP)
            for o in range(7):
                project(o, range(NP), False).then_inc(op_mm, 1)
            project(7, [4, 5, 6, 7, 0, 1, 2, 3], True).then_inc(op_mm, 1)

            def turn_rows(rows, b0, mm):
                for g in range(2):
                    for k in range(4 * g, 4 * g + 4):
                        ins = pe.transpose(bank(b0 + g)[:, (k % 4) * P:(k % 4 + 1) * P], rows[:, k:k + (P - 1) * KD + 1:KD], ident)
                    ins.then_inc(mm, 1)

            for t in range(NT):
                pe.wait_ge(xn_ready, NT + t + 1)
                pe.wait_ge(h_ready, 4 if t == 0 else 2 * NT)
                if t >= 2:
                    pe.wait_ge(nf_ready, t - 1)
                turn_rows(n_rows[:, t, :], 2 * (t % 2), nrow_mm)
            pe.wait_ge(router_in, 32)
            for t in range(NT):
                pe.wait_ge(nf_ready, t + 1)
                for k in range(KD):
                    ins = pe.matmul(bank(4)[:, t * (NG + NE):(t + 1) * (NG + NE)], n_feat[:, t, k, :], router_w[:, k, :], start=(k == 0), stop=(k == KD - 1))
            ins.then_inc(route_mm, 1)
            pe.wait_ge(ple_in, 64)
            for k in range(KE):
                for t in range(NT):
                    ins = pe.transpose(bank(6 + k)[:, t * P:(t + 1) * P], ple_p[:, t, k:k + (P - 1) * KE + 1:KE], ident)
            ins.then_inc(ple_mm, 1)
            pe.wait_ge(routed, CHOICES)
            for t in range(NT):
                for u in range(t + 1):
                    k = K_TRI if u == t else K_ALL1
                    ins = pe.matmul(bank(5)[:, t * NE:(t + 1) * NE], const[:, k:k + P], hot_sum[:, u, :], start=(u == 0), stop=(u == t))
            ins.then_inc(route_mm, 1)
            pe.wait_ge(routed, SLOTS)
            pe.wait_ge(over_counted, 1)
            pe.matmul(bank(5)[:, 0:1], const[:, K_ALL1:K_ALL1 + P], over_rows, start=True, stop=True).then_inc(route_mm, 1)
            pe.wait_ge(ple_t_ready, KE)

            def expert_rows(s, it, first=False):
                pe.wait_ge(x_slot_in[s], it * 16 + 16)
                if not (first and s == 0):
                    pe.wait_ge(xs_ready, it * 2 + s)
                turn_rows(x_slot[s], 0, xs_mm)

            def expert_pass(it, first=False, last=False):
                for s in range(2):
                    pe.wait_ge(w_exp_in[s], it * 96 + 96)
                    pe.wait_ge(xs_ready, it * 2 + s + 1)
                    if not first:
                        pe.wait_ge(hid_ready, it * 2 + s - 1)
                    for w in range(2):
                        for k in range(KD):
                            for e in range(2):
                                ins = pe.matmul(bank(2 + s)[64 * e:64 * e + 64, w * DE:(w + 1) * DE], x_slot_t[s][:, k, 64 * e:64 * e + 64],
                                                (w1_sb, w3_sb)[w][s][:, e, k, :], start=(k == 0), stop=(k == KD - 1))
                    ins.then_inc(up_mm, 1)
                    if not (last and s == 1):
                        expert_rows(1 - s, it + s)
                    pe.wait_ge(hid_ready, it * 2 + s + 1)
                    for k in range(KE):
                        ins = pe.transpose(bank(4)[:, k * P:(k + 1) * P], hid[s][:, k:k + (P - 1) * KE + 1:KE], ident)
                    ins.then_inc(hid_mm, 1)
                    pe.wait_ge(hidt_ready, it * 2 + s + 1)
                    for n in range(2):
                        if not (first and s == 0):
                            pe.wait_ge((y_lo, y_hi)[n], it * 2 + s)
                        for k in range(KE):
                            for e in range(2):
                                ins = pe.matmul(bank(5 + n)[64 * e:64 * e + 64, :], hid_t[s][:, k, 64 * e:64 * e + 64],
                                                w2_sb[s][:, e, k, n * 512:(n + 1) * 512], start=(k == 0), stop=(k == KE - 1))
                        ins.then_inc(down_mm, 1)
                    pe.wait_ge(down_mm, it * 4 + 2 * s + 2)
                    pe.sem_inc(w_exp_used, 1)

            expert_rows(0, 0, first=True)
            expert_pass(0, first=True)
            with pe.Fori(1, NPAIR // 2 - 1) as it:
                expert_pass(it)
            expert_pass(NPAIR // 2 - 1, last=True)
            with if_over(pe):
                pe.wait_ge(y_lo, NPAIR)
                pe.wait_ge(y_hi, NPAIR)
                for t in range(NT):
                    if t >= 2:
                        pe.wait_ge(over_dve, t - 1)
                    turn_rows(n_rows[:, t, :], 2 * (t % 2), over_mm)
                pe.wait_ge(over_dve, NT)
                with pe.Fori(0, NE) as e:
                    for t in range(NT):
                        if t == 0:
                            pe.wait_ge(over_w_in, e * 48 + 48)
                        for w, sb in enumerate((over_w1, over_w3)):
                            for k in range(KD):
                                ins = pe.matmul(bank(2)[:, w * DE:(w + 1) * DE], over_feat[:, t, k, :], sb[:, k, :], start=(k == 0), stop=(k == KD - 1))
                        ins.then_inc(over_mm, 1)
                        pe.wait_ge(over_dve, over_hid(e, t))
                        for k in range(KE):
                            ins = pe.transpose(bank(4)[:, k * P:(k + 1) * P], hid[0][:, k:k + (P - 1) * KE + 1:KE], ident)
                        ins.then_inc(over_mm, 1)
                        pe.wait_ge(over_act, over_hid_t(e, t))
                        for n in range(2):
                            for k in range(KE):
                                ins = pe.matmul(bank(5 + n), hid_t[0][:, k, :], over_w2[:, k, n * 512:(n + 1) * 512], start=(k == 0), stop=(k == KE - 1))
                        ins.then_inc(over_mm, 1)
            for t in range(NT):
                pe.wait_ge(xn_ready, 2 * NT + t + 1)
                if t >= 2:
                    pe.wait_ge(nf_ready, NT + t - 1)
                turn_rows(n_rows[:, t, :], 2 * (t % 2), nrow_mm)
            pe.wait_ge(gate_w_in, 16)
            pe.wait_ge(y_lo, NPAIR)
            pe.wait_ge(y_hi, NPAIR)
            for t in range(NT):
                pe.wait_ge(nf_ready, NT + t + 1)
                for n in range(2):
                    if t:
                        pe.wait_ge(gate_pre, t)
                    for k in range(KD):
                        ins = pe.matmul(bank(4 + n), n3_feat[:, t, k, :], gate_w[:, k, n * 512:(n + 1) * 512], start=(k == 0), stop=(k == KD - 1))
                    ins.then_inc(gate_mm, 1)
                for n in range(2):
                    if t:
                        pe.wait_ge(h_ready, 3 * NT + t)
                    for k in range(KE):
                        ins = pe.matmul(bank(6 + n), ple_pt[:, k, t * P:(t + 1) * P], ple_wp[:, k, n * 512:(n + 1) * 512], start=(k == 0), stop=(k == KE - 1))
                    ins.then_inc(proj_mm, 1)


def tables(np):
    c = np.zeros((P, K_END), np.float32)
    i = np.arange(P)
    c[:, K_ID:K_ID + P] = np.eye(P)
    c[:, K_ONES:K_ONES + P] = (i[:, None] // HD == i[None] // HD)
    same = i[:, None] // C == i[None] // C
    before = i[:, None] < i[None]
    upto = i[:, None] <= i[None]
    c[:, K_MASK:K_MASK + 4 * P] = np.concatenate([same & before, same & upto] * 2, axis=1)
    for l in range(LEVELS):
        b = 1 << l
        m = (i[:, None] // (2 * b) == i[None] // (2 * b)) & (i[:, None] // b < i[None] // b)
        c[:, K_LEVEL + l * P:K_LEVEL + (l + 1) * P] = m
    c[:, K_RESET:K_RESET + T] = (np.arange(T) % C != 0)
    c[:, K_TRI:K_TRI + P] = before
    c[:, K_ALL1:K_ALL1 + P] = 1
    c[:, K_IOTA:K_IOTA + NE] = np.arange(NE)
    c[:, K_TOK:K_TOK + NT] = i[:, None] + P * np.arange(NT)
    return c


def layout(np, v):
    def cols(x):
        return np.asarray(x).reshape(-1, P).T
    vec = np.concatenate([cols(v[n][0]) for n in ("rwkv_mu", "rwkv_w0", "rwkv_a0", "rwkv_k_k", "rwkv_k_a",
                                                  "rwkv_r_k", "rwkv_ln_w", "rwkv_ln_b")]
                         + [np.asarray(v[n][0]).reshape(P, KD) for n in ("norm_mix_w", "norm_ffn_w", "norm_ple_w")], axis=1)
    rel = np.clip(np.arange(P)[:, None] - np.arange(T)[None] + T - P, -(C - 1), 256) + C - 1
    return {
        "const": tables(np), "vec": vec, "x": v["x"][0], "w_in": v["w_in"][0],
        "w_out": v["w_out"][0], "p": v["p"][0, 0],
        "router_w": np.concatenate([v["router_group_w"][0], v["router_expert_w"][0]], axis=1),
        "router_b": np.concatenate([v["router_group_b"], v["router_expert_b"]], axis=1),
        "w1": np.asarray(v["expert_w1"][0]).reshape(NE, D, DE), "w3": np.asarray(v["expert_w3"][0]).reshape(NE, D, DE),
        "w2e": np.asarray(v["expert_w2"][0]).reshape(NE, DE, D),
        "gate_w": v["ple_gate_w"][0], "gate_b": v["ple_gate_b"], "ple_wp": v["ple_proj_w"][0], "final_w": np.asarray(v["final_norm_w"])[None],
        "w2": v["rwkv_w2"][0], "a2": v["rwkv_a2"][0], "g2": v["rwkv_g2"][0],
        "bias": np.asarray(v["att_rel_bias"][0])[:, rel],
    }


def kernel(**inputs):
    import numpy as np
    import concourse.bacc as bacc
    from concourse.bass_utils import run_bass_kernel_spmd

    nc = bacc.Bacc("TRN2", target_bir_lowering=False, num_devices=1)
    arrays = {f"{name}_in": np.ascontiguousarray(x) for name, x in layout(np, inputs).items()}
    aps = {name[:-3]: nc.dram_tensor(name, x.shape, mybir.dt.from_np(x.dtype), kind="ExternalInput").ap()
           for name, x in arrays.items()}
    out = nc.dram_tensor("out", (T, D), F32, kind="ExternalOutput").ap()
    hybrid_trunk(nc, aps, out)
    r = run_bass_kernel_spmd(nc, [arrays], core_ids=[0])
    return r.results[0]["out"].reshape(1, T, D)
```

```python
import math
from contextlib import ExitStack

import concourse.bass as bass
from concourse import mybir

F32 = mybir.dt.float32
F32R = mybir.dt.float32r
U32 = mybir.dt.uint32
ALU = mybir.AluOpType
ACT = mybir.ActivationFunctionType
AX = mybir.AxisListType

P = 128
T = 512
NT = T // P
D = 1024
KD = D // P
DR = 512
NP = DR // P
NH = 8
HD = 64
C = 64
NC = T // C
N_RWKV = 3 * DR + 256
N_IN = N_RWKV + 3 * DR
SLAB = 256
RING = 2
NE = 32
NG = 4
EPG = 8
DE = 256
CAP = 64
KE = DE // P
NPAIR = NE // 2
PLE = 256
RMS_EPS = 1e-6
GN_EPS = 64e-5
DECAY_SCALE = 0.6065306597126334
NEG = -1e30
NO_ROW = 1 << 16
NORM_SCALE_LOG2 = 20

K_ID, K_ONES, K_MASK, K_LEVEL = 0, 128, 256, 512
LEVELS = 6
K_RESET = K_LEVEL + LEVELS * 128
K_TRI = K_RESET + T
K_ALL1 = K_TRI + 128
K_IOTA = K_ALL1 + 128
K_TOK = K_IOTA + NE
K_END = K_TOK + NT

V_MU, V_W0, V_A0, V_KK, V_KA, V_RK, V_LNW, V_LNB = 0, 14, 18, 22, 26, 30, 34, 38
V_MIX, V_FFN, V_PLE = 42, 50, 58
V_END = 66


def hybrid_trunk(nc, a, out):
    with ExitStack() as ctx:
        def sem(name):
            return ctx.enter_context(nc.semaphore(name))

        with nc.sbuf_tensor("low_parts", [P, 48 * 256], F32R) as low_parts:
            pass
        arena = [(0, ctx.enter_context(nc.sbuf_tensor("arena_0", [P, 48 * 256], F32))),
                 (48, ctx.enter_context(nc.sbuf_tensor("arena_48", [P, 72 * 256], F32)))]
        with nc.sbuf_tensor("high_parts", [P, 16 * 256], F32R) as high_parts:
            pass
        arena += [(120, ctx.enter_context(nc.sbuf_tensor("arena_120", [P, 16 * 256], F32))),
                  (136, ctx.enter_context(nc.sbuf_tensor("arena_136", [P, 53200 - 136 * 256], F32)))]
        psum = ctx.enter_context(nc.psum_tensor("psum", [P, 8, 512], F32))

        def at(kib, n):
            base, part = [x for x in arena if x[0] <= kib][-1]
            first = int((kib - base) * 256)
            return part[:, first:first + n]

        def grid(kib, *dims):
            n = 1
            for d in dims:
                n *= d
            names = "abcd"[:len(dims)]
            spec = "p (" + " ".join(names) + ") -> p " + " ".join(names)
            return at(kib, n).rearrange(spec, **dict(zip(names[1:], dims[1:])))

        def bank(b):
            return psum[:, b, :]

        const = at(48, K_END)
        vec = at(48 + K_END / 256, V_END)
        small = at(48 + (K_END + V_END) / 256, 3072 - K_END - V_END)
        ident = const[:, K_ID:K_ID + P]
        head_ones = const[:, K_ONES:K_ONES + P]
        mask_2h = const[:, K_MASK:K_MASK + 2 * P].unsqueeze(1).to_broadcast([P, 2, 2 * P])
        z = grid(60, 14, T)
        q_head = grid(88, NH, T)
        k_pair = grid(104, NP, T)
        v_tok = grid(112, NT, DR)
        h_hi = low_parts[:, 0:KD * T].rearrange("p (k t) -> p k t", k=KD)
        h_lo = high_parts[:, 0:KD * T].rearrange("p (k t) -> p k t", k=KD)
        slab_hi, slab_lo = (low_parts[:, (1 + i) * KD * T:(2 + i) * KD * T].rearrange("p (r k n) -> p r k n", r=2, k=KD) for i in range(2))
        slabs = grid(136, RING, KD, SLAB)
        x_in_sb = grid(160, NT, D)
        x_norm = grid(176, NT, D)
        prob = grid(120, 4, T)
        PT_W = 10 * P
        prob_t = grid(136, 2, 2, PT_W)
        bias_w = grid(128, 4, T)
        y_att = grid(196, NP, T)
        shift_buf = [grid(204, 520)[:, 0:T + 1], grid(192, 520)[:, 0:T + 1]]

        within = grid(88, NT, 4 * P)
        across = grid(96, NT, 4 * P)
        m_level = [grid(104, 8, P), grid(108, 8, P)]
        t_inv = grid(112, 8, P)
        t_inv_t = grid(116, 8, P)
        m_t = grid(120, 8, P)
        bk_chunk = grid(124, NT, 2, 2 * P)
        v_rows = grid(136, NT, P)
        rhs = grid(132, NT, 2, P)
        wy = grid(138, NT, 2, 2, HD)
        step_mat = grid(142, NC, P)
        step_add = grid(146, NC, P)
        r_eff = grid(150, T)
        y_buf = grid(152, T)
        state = grid(154, NC, P)
        r_dec = [grid(178, T), grid(158, T)]
        ar_head = grid(160, NT, 4 * P)
        a_dec = grid(168, T)
        b_inc = grid(170, T)
        k_inc = grid(172, T)
        b_end = grid(174, T)
        k_end = grid(176, T)
        sgw = grid(180, T)
        iclr = grid(182, T)
        cum = grid(184, T)
        cum_x = grid(186, T)
        dec = grid(188, T)
        cum_e = grid(190, T)
        kkn = grid(192, T)
        knorm = grid(194, T)
        k_mod = grid(204, T)
        lora_w = [grid(152, 3, DR), grid(0, 3, DR)]
        h_res = grid(88, NT, D)
        w_out = grid(160, KD, D)
        n_rows = grid(60, NT, D)
        n_feat = grid(136, NT, KD, P)
        router_w = grid(204, KD, NG + NE)
        router_b = grid(205.25, NG + NE)
        no_row = at(206.5, P).bitcast(U32)
        table = at(80, 2048)
        used = [0]

        def col(n, *dims, dtype=None):
            ap = table[:, used[0]:used[0] + n]
            used[0] += n
            if dtype is not None:
                ap = ap.bitcast(dtype)
            if dims:
                names = "abcd"[:len(dims)]
                ap = ap.rearrange("p (" + " ".join(names) + ") -> p " + " ".join(names), **dict(zip(names[1:], dims[1:])))
            return ap

        e_logit = col(NT * NE, NT, NG, EPG)
        g_logit = col(NT * 8, NT, 8)
        g_top = col(NT * 8, NT, 8)
        g_idx = col(NT * 8, NT, 8, dtype=U32)
        g_sel = col(NT)
        g_exp = col(NT * NG, NT, NG)
        g_sum = col(NT)
        p_group = col(NT)
        g_hot = col(NT * NG, NT, NG)
        e_mask = col(NT * NE, NT, EPG, NG)
        sel = col(NT * 8, NT, 8)
        e_top = col(NT * 8, NT, 8)
        e_idx = col(NT * 8, NT, 8, dtype=U32)
        e_loc = col(NT * 2, NT, 2)
        e_ratio = col(NT)
        weight = col(NT * 2, NT, 2)
        expert = col(NT * 2, NT, 2)
        hot = [col(NT * NE, NT, NE), col(NT * NE, NT, NE)]
        hot_sum = col(NT * NE, NT, NE)
        hot_pos = col(NT * NE, NT, NE)
        pos = col(NT * 2, NT, 2)
        slot_f = col(NT * 2, NT, 2)
        fits = col(NT * 2, NT, 2)
        w_main = col(NT * 2, NT, 2)
        over_u = col(1, dtype=U32)
        over_rows = col(1)
        w_col = col(NT)
        slot_u = col(NT * 2, NT, 2, dtype=U32)
        dest_u = col(NT * 2, NT, 2, dtype=U32)
        slot_dest = col(NPAIR, dtype=U32)
        slot_tok_f = col(NPAIR)
        slot_second = col(NPAIR)
        slot_tok = col(NPAIR, dtype=U32)
        tok_now = [col(1, dtype=U32), col(1, dtype=U32)]
        dest_now = [col(1, dtype=U32), col(1, dtype=U32)]

        w1_sb = [grid(b, 2, KD, DE) for b in (0, 104)]
        w3_sb = [grid(b + 16, 2, KD, DE) for b in (0, 104)]
        w2_sb = [grid(b + 32, 2, KE, D) for b in (0, 104)]
        x_slot = [grid(152, D), grid(156, D)]
        x_slot_t = [grid(160, KD, P), grid(164, KD, P)]
        y_slot = [grid(168, D), grid(172, D)]
        hid = [grid(176, DE), grid(177, DE)]
        hid_t = [grid(178, KE, P), grid(179, KE, P)]
        y_tok = grid(136, NT, 2, D)

        over_feat = grid(136, NT, KD, P)
        over_in = grid(32, NT, D)
        over_w1 = grid(104, KD, DE)
        over_w3 = grid(112, KD, DE)
        over_w2 = grid(120, KE, D)
        w_over = hot_pos

        ple_wp = grid(180, KE, D)
        ple_p = grid(188, NT, PLE)
        ple_pt = grid(192, KE, T)
        gate_b = grid(196, D)
        final_w = grid(200, D)
        gate_w = grid(0, KD, D)
        ple_proj = grid(60, NT, D)
        n3_rows = grid(32, NT, D)
        n3_feat = grid(104, NT, KD, P)
        gate = [grid(120, D), grid(124, D)]
        out_rows = [grid(128, D), grid(132, D)]

        norm_rows = nc.dram_tensor("norm_rows", (T, D), F32, kind="Internal").ap()
        dest_of_slot = nc.dram_tensor("dest_of_slot", (T * NE, 1), U32, kind="Internal").ap()
        y_rows = nc.dram_tensor("y_rows", (2 * T, D), F32, kind="Internal").ap()

        d_end = [small[:, 128:136], small[:, 136:144]]

        ss = small[:, 0:4]
        ms = small[:, 4:8]
        rs = small[:, 8:12]
        one_mu = small[:, 12:26]
        ss2, rs2 = small[:, 144:148], small[:, 148:152]
        ss3, rs3 = small[:, 152:156], small[:, 156:160]
        ss4, rs4 = small[:, 160:164], small[:, 164:168]
        rms_eps = small[:, 26:27]
        gn_eps = small[:, 27:28]
        norm_bias = small[:, 28:29]
        nmax = small[:, 32:64]
        psumrow = small[:, 64:96]
        prow_inv = small[:, 96:128]

        consts_in = sem("consts_in")
        x_in = [sem(f"x_in{t}") for t in range(NT)]
        rs_ready = sem("rs_ready")
        eps_ready = sem("eps_ready")
        dve_step = sem("dve_step")
        act_step = sem("act_step")
        pool_step = sem("pool_step")
        xn_ready = sem("xn_ready")
        xt_mm = sem("xt_mm")
        hf_hi = sem("hf_hi")
        hf_lo = sem("hf_lo")
        slab_in = [sem(f"slab_in{i}") for i in range(RING)]
        slab_hi_ready = sem("slab_hi_ready")
        slab_lo_ready = sem("slab_lo_ready")
        slab_used = sem("slab_used")
        z_mm = sem("z_mm")
        z_shift = sem("z_shift")
        z_act = sem("z_act")
        z_dve = sem("z_dve")
        zeros_ready = sem("zeros_ready")
        bias_in = [sem(f"bias_in{i}") for i in range(4)]
        bias_masked = sem("bias_masked")
        att_s_mm = sem("att_s_mm")
        att_s_read = sem("att_s_read")
        att_max = sem("att_max")
        att_exp = sem("att_exp")
        att_p = sem("att_p")
        att_tr = sem("att_tr")
        att_pt = sem("att_pt")
        att_pv = sem("att_pv")
        att_y = sem("att_y")
        lora_in = sem("lora_in")
        slots_cleared = sem("slots_cleared")
        w_out_in = [sem("w_out_in0"), sem("w_out_in1")]
        res_in = sem("res_in")
        op_mm = sem("op_mm")
        h_ready = sem("h_ready")
        nrow_mm = sem("nrow_mm")
        nf_ready = sem("nf_ready")
        rows_out = sem("rows_out")
        router_in = sem("router_in")
        route_mm = sem("route_mm")
        routed = sem("routed")
        GROUP_DIFF, EXPERT_DIFF, CHOICES, SLOTS, OVERFLOWS = 1, 2, 3, 4, 5
        route_exp = sem("route_exp")
        scattered = sem("scattered")
        slot_dest_in = sem("slot_dest_in")
        slot_tok_ready = sem("slot_tok_ready")
        tok_now_ready = sem("tok_now_ready")
        dest_now_ready = sem("dest_now_ready")
        gather_go = sem("gather_go")
        x_slot_in = [sem(f"x_slot_in{i}") for i in range(2)]
        w_exp_in = [sem(f"w_exp_in{i}") for i in range(2)]
        w_exp_used = sem("w_exp_used")
        xs_mm = sem("xs_mm")
        xs_ready = sem("xs_ready")
        up_mm = sem("up_mm")
        silu_ready = sem("silu_ready")
        hid_ready = sem("hid_ready")
        hid_mm = sem("hid_mm")
        hidt_ready = sem("hidt_ready")
        down_mm = sem("down_mm")
        y_lo = sem("y_lo")
        y_hi = sem("y_hi")
        y_out = [sem(f"y_out{i}") for i in range(2)]
        y_tok_in = [sem(f"y_tok_in{i}") for i in range(NT)]
        ple_in = sem("ple_in")
        ple_mm = sem("ple_mm")
        ple_t_ready = sem("ple_t_ready")
        gate_w_in = sem("gate_w_in")
        gate_mm = sem("gate_mm")
        proj_mm = sem("proj_mm")
        proj_ready = sem("proj_ready")
        gate_pre = sem("gate_pre")
        gate_ready = sem("gate_ready")
        out_ready = sem("out_ready")
        over_counted = sem("over_counted")
        over_in_ready = sem("over_in_ready")
        y_cleared = sem("y_cleared")
        over_w_in = sem("over_w_in")
        over_mm = sem("over_mm")
        over_act = sem("over_act")
        over_dve = sem("over_dve")
        out_stored = [sem("out_stored0"), sem("out_stored1")]
        lo_ready = sem("lo_ready")
        prep_mm = sem("prep_mm")
        sg_ready = sem("sg_ready")
        aa_ready = sem("aa_ready")
        ksq_ready = sem("ksq_ready")
        cum_ready = sem("cum_ready")
        cum_split = sem("cum_split")
        decay_ready = sem("decay_ready")
        ksum_ready = sem("ksum_ready")
        kn_ready = sem("kn_ready")
        rk_ready = sem("rk_ready")
        rt_ready = sem("rt_ready")
        at_ready = sem("at_ready")
        prep_out = sem("prep_out")
        bonus_ready = sem("bonus_ready")
        g_ready = sem("g_ready")
        ar_ready = sem("ar_ready")
        unit_in_used = sem("unit_in_used")
        s1_mm = sem("s1_mm")
        s2_mm = sem("s2_mm")
        within_ready = sem("within_ready")
        across_ready = sem("across_ready")
        tok_mm = sem("tok_mm")
        tok_ready = sem("tok_ready")
        tt_init = sem("tt_init")
        mt_ready = sem("mt_ready")
        x_mm = sem("x_mm")
        x_ready = sem("x_ready")
        d_mm = sem("d_mm")
        t_ready = sem("t_ready")
        tr_mm = sem("tr_mm")
        tt_ready = sem("tt_ready")
        g_mm = sem("g_mm")
        ga_ready = sem("ga_ready")
        w_mm = sem("w_mm")
        w_ready = sem("w_ready")
        rp_mm = sem("rp_mm")
        rp_ready = sem("rp_ready")
        y0_mm = sem("y0_mm")
        y0_ready = sem("y0_ready")
        mc_mm = sem("mc_mm")
        mc_ready = sem("mc_ready")
        q_mm = sem("q_mm")
        q_ready = sem("q_ready")
        seq_mm = sem("seq_mm")
        s_ready = sem("s_ready")
        y_mm = sem("y_mm")
        y_ready = sem("y_ready")
        stat_mm = sem("stat_mm")
        yc_ready = sem("yc_ready")
        ysq_ready = sem("ysq_ready")
        rstd_ready = sem("rstd_ready")
        yr_ready = sem("yr_ready")
        rwkv_zero = sem("rwkv_zero")

        slab_order = [6, 2, 3, 0, 1, 4, 5, 7, 8, 9, 10, 11, 12]
        jobs = []
        for n, s in enumerate(slab_order):
            if s < 11:
                jobs += [(n, "feat", 2 * s), (n, "feat", 2 * s + 1)]
            else:
                jobs += [(n, "tok", (s - 11, t)) for t in range(NT)]
        NJ = len(jobs)
        PREP_JOB = 14
        last_job = {n: j for j, (n, _, _) in enumerate(jobs)}

        first_job = {n: min(j for j, job in enumerate(jobs) if job[0] == n) for n in range(len(slab_order))}

        def units():
            return [(h, i) for h in range(NH) for i in range(NT)]

        def pt_col(i, j):
            return (i * (i + 1) // 2 + j) * P

        def z_reader(j):
            _, kind, what = jobs[j]
            return "act" if kind == "feat" and what >= 18 else "dve"

        def z_count(j, reader):
            return sum(z_reader(i) == reader for i in range(j + 1))

        def z_done(eng, j):
            r = z_reader(j)
            eng.wait_ge({"act": z_act, "dve": z_dve}[r], z_count(j, r))

        def over_up(e, t):
            return e * (3 * NT) + (2 * NT + 3 * t + 1)

        def over_turned(e, t):
            return e * (3 * NT) + (2 * NT + 3 * t + 2)

        def over_down(e, t):
            return e * (3 * NT) + (2 * NT + 3 * t + 3)

        def over_col(e):
            return e * (2 * NT + 1) + (NT + 1)

        def over_hid(e, t):
            return e * (2 * NT + 1) + (NT + 2 * t + 2)

        def over_silu(e, t):
            return e * (2 * NT) + (2 * t + 1)

        def over_hid_t(e, t):
            return e * (2 * NT) + (2 * t + 2)

        def if_over(eng):
            eng.wait_ge(routed, OVERFLOWS)
            return eng.If(eng.value_load(over_u[0:1, 0:1], min_val=0, max_val=2 * T) > 0)

        def one_of(src, pair, i):
            return src[bass.ds(pair + i * NPAIR, 1), :, :].rearrange("o p f -> (o p) f")

        w_in_v = a["w_in"].rearrange("(p k) n -> p k n", k=KD)

        LV = LEVELS - 1
        NSLOT = 2 * LV

        def level_mask(l):
            return const[:, K_LEVEL + l * P:K_LEVEL + (l + 1) * P]

        def mats(m):
            return lambda s: m[:, 4 * s:4 * s + 4, :]

        def n_of(s):
            return within.rearrange("p n (h x t) -> p n h x t", h=2, x=2)[:, 2 * s:2 * s + 2, :, 0, :]

        def heads4(ap):
            return ap.rearrange("p (n h) t -> p n h t", h=2)

        def over(ap, *dims):
            return ap.unsqueeze(1).unsqueeze(1).to_broadcast([P, 2, 2, P])

        block = ctx.enter_context(nc.Block())

        @block.sync
        def _(sp):
            sp.dma_start(vec, a["vec"]).then_inc(consts_in, 16)
            for t in range(NT):
                sp.dma_start(x_in_sb[:, t, :], a["x"][t * P:(t + 1) * P, :]).then_inc(x_in[t], 16)
            sp.dma_start(const, a["const"]).then_inc(consts_in, 16)
            def lora_loads(w):
                sp.dma_start(w[0:64, 0, :], a["w2"]).then_inc(lora_in, 16)
                sp.dma_start(w[64:128, 1, :], a["a2"]).then_inc(lora_in, 16)
                sp.dma_start(w[:, 2, :], a["g2"]).then_inc(lora_in, 16)

            for n, s in enumerate(slab_order):
                if n >= RING:
                    sp.wait_ge(slab_lo_ready, n - RING + 1)
                sp.dma_start(slabs[:, n % RING], w_in_v[:, :, s * SLAB:(s + 1) * SLAB]).then_inc(slab_in[n % RING], 16)
                if n == 1:
                    lora_loads(lora_w[0])
            sp.wait_ge(z_mm, NJ)
            lora_loads(lora_w[1])
            for h in range(NH):
                if h >= 4:
                    sp.wait_ge(att_s_read, 4 * (h - 4) + 4)
                sp.dma_start(bias_w[:, h % 4, :], a["bias"][h]).then_inc(bias_in[h % 4], 16)

            w_out_v = a["w_out"].rearrange("(k p) n -> p k n", p=P)
            sp.wait_ge(unit_in_used, NP)
            sp.wait_ge(prep_out, NP)
            sp.dma_start(w_out[:, 0:4, :], w_out_v[:, 0:4, :]).then_inc(w_out_in[0], 16)
            sp.wait_ge(rp_ready, NP)
            sp.dma_start(w_out[:, 4:8, :], w_out_v[:, 4:8, :]).then_inc(w_out_in[1], 16)
            sp.dma_start(router_w, a["router_w"].rearrange("(p k) n -> p k n", k=KD)).then_inc(router_in, 16)
            sp.dma_start(router_b, a["router_b"].to_broadcast([P, NG + NE])).then_inc(router_in, 16)
            sp.wait_ge(y0_mm, NP)
            sp.dma_start(h_res, a["x"].rearrange("(n p) d -> p n d", p=P)).then_inc(res_in, 16)

            def expert_loads(s, pair, which=(0, 1)):
                for i in which:
                    for w, sb, rows in (("w1", w1_sb, KD), ("w3", w3_sb, KD), ("w2e", w2_sb, KE)):
                        src = a[w].rearrange("e (p k) f -> e p (k f)", k=rows)
                        sp.dma_start(sb[s][:, i].rearrange("p k f -> p (k f)"), one_of(src, pair, i)).then_inc(w_exp_in[s], 16)

            sp.wait_ge(prep_mm, 5 * NP)
            expert_loads(0, 0)
            for t in range(NT):
                sp.wait_ge(xn_ready, NT + t + 1)
                sp.dma_start(norm_rows[t * P:(t + 1) * P, :], n_rows[:, t, :]).then_inc(rows_out, 16)
            sp.wait_ge(op_mm, 2 * NT)
            sp.dma_start(ple_wp, a["ple_wp"].rearrange("(p k) n -> p k n", k=KE)).then_inc(ple_in, 16)
            sp.dma_start(ple_p, a["p"].rearrange("(n p) f -> p n f", p=P)).then_inc(ple_in, 16)
            sp.dma_start(gate_b, a["gate_b"].to_broadcast([P, D])).then_inc(ple_in, 16)
            sp.dma_start(final_w, a["final_w"].to_broadcast([P, D])).then_inc(ple_in, 16)
            sp.wait_ge(route_mm, 1)
            expert_loads(1, 1)
            sp.wait_ge(scattered, 16 * 2 * NT)
            sp.dma_start(slot_dest, dest_of_slot[0:CAP * NE, :].rearrange("(c e j) o -> e c (j o)", e=2, j=NPAIR)).then_inc(slot_dest_in, 16)

            def expert_pass(it, last=False):
                for s in range(2):
                    if not last:
                        sp.wait_ge(w_exp_used, it * 2 + s + 1)
                        expert_loads(s, it * 2 + 2 + s)
                    elif s == 0:
                        sp.wait_ge(w_exp_used, NPAIR - 1)
                        sp.dma_start(gate_w, a["gate_w"].rearrange("(p k) n -> p k n", k=KD)).then_inc(gate_w_in, 16)

            with sp.Fori(0, NPAIR // 2 - 1) as it:
                expert_pass(it)
            expert_pass(NPAIR // 2 - 1, last=True)
            with if_over(sp):
                sp.wait_ge(w_exp_used, NPAIR)
                sp.dma_start(over_in, norm_rows.rearrange("(n p) d -> p n d", p=P)).then_inc(over_in_ready, 16)
                with sp.Fori(0, NE) as e:
                    sp.wait_ge(over_mm, e * (3 * NT) + 2 * NT)
                    for w, dst, rows in (("w1", over_w1, KD), ("w3", over_w3, KD), ("w2e", over_w2, KE)):
                        src = a[w].rearrange("e (p k) f -> e p (k f)", k=rows)
                        sp.dma_start(dst.rearrange("p k f -> p (k f)"), one_of(src, e, 0)).then_inc(over_w_in, 16)
                sp.wait_ge(over_dve, over_col(NE - 1) + 2 * NT)
            sp.wait_ge(w_exp_used, NPAIR)
            for s in range(2):
                sp.wait_ge(y_out[s], 16 * (NPAIR // 2))
            for t in range(NT):
                for x in range(2):
                    sp.dma_start(y_tok[:, t, x, :], y_rows[x * T + t * P:x * T + (t + 1) * P, :]).then_inc(y_tok_in[t], 16)
            for t in range(NT):
                sp.wait_ge(out_ready, t + 1)
                sp.dma_start(out[t * P:(t + 1) * P, :], out_rows[t % 2]).then_inc(out_stored[t % 2], 16)
            for b in out_stored:
                sp.wait_ge(b, 16 * NT // 2)

        @block.gpsimd
        def _(pool):
            steps = [0]

            def chain(ins):
                steps[0] += 1
                ins.then_inc(pool_step, 1)
                pool.wait_ge(pool_step, steps[0])

            def copy(out, in_):
                return pool.tensor_scalar(out, in_, 1.0, 1.0, ALU.mult, ALU.mult)

            pool.memset(no_row, NO_ROW).then_inc(zeros_ready, 1)
            pool.wait_ge(zeros_ready, 1)
            pool.dma_start(dest_of_slot.rearrange("(p n) o -> p (n o)", p=P), no_row).then_inc(slots_cleared, 16)
            pool.memset(lora_w[0][64:128, 0, :], 0.0).then_inc(zeros_ready, 1)
            pool.wait_ge(zeros_ready, 2)
            pool.memset(lora_w[0][0:64, 1, :], 0.0).then_inc(zeros_ready, 1)
            pool.wait_ge(zeros_ready, 3)
            for n, b in enumerate(shift_buf):
                pool.memset(b[:, 0:1], 0.0).then_inc(zeros_ready, 1)
                pool.wait_ge(zeros_ready, n + 4)
            for h in range(NH):
                other = 64 * (1 - h % 2)
                pool.memset(q_head[other:other + 64, h, :], 0.0).then_inc(zeros_ready, 1)
                pool.wait_ge(zeros_ready, h + 6)
            def slot(k, prep):
                if prep is None:
                    return
                if k == 1:
                    pool.wait_ge(cum_ready, prep + 1)
                    pool.wait_ge(prep_out, prep)
                    pool.tensor_tensor(cum_x, cum, sgw, ALU.subtract).then_inc(cum_split, 1)
                    pool.wait_ge(cum_split, 2 * prep + 1)
                    ends = cum.rearrange("p (c t) -> p c t", t=C)[:, :, C - 1:C].to_broadcast([P, NC, C])
                    pool.tensor_tensor(cum_e.rearrange("p (c t) -> p c t", t=C), ends, cum.rearrange("p (c t) -> p c t", t=C),
                                       ALU.subtract).then_inc(cum_split, 1)
                    pool.wait_ge(cum_split, 2 * prep + 2)
                if k == NSLOT - 1:
                    pool.wait_ge(unit_in_used, prep)
                    pool.wait_ge(rt_ready, prep + 1)
                    pool.wait_ge(at_ready, prep + 1)
                    for x, src in enumerate((a_dec, r_dec[prep % 2])):
                        for h in range(2):
                            rows = slice(64 * h, 64 * h + 64)
                            copy(ar_head[rows, :, (2 * h + x) * P:(2 * h + x + 1) * P],
                                 src[rows, :].rearrange("p (n t) -> p n t", t=P)).then_inc(ar_ready, 1)
                            pool.wait_ge(ar_ready, 4 * prep + 2 * x + h + 1)

            pool.wait_ge(xn_ready, NT)
            chain(pool.memset(ar_head, 0.0))
            for k in range(NSLOT):
                slot(k, 0)
            pool.wait_ge(z_mm, NJ)
            chain(pool.memset(lora_w[1][64:128, 0, :], 0.0))
            pool.memset(lora_w[1][0:64, 1, :], 0.0).then_inc(zeros_ready, 1)
            pool.wait_ge(zeros_ready, 6 + NH)
            for h in range(NH):
                pool.wait_ge(bias_in[h % 4], 16 * (h // 4 + 1))
                pool.memset(bias_w[0:64, h % 4, T - 64:T], NEG).then_inc(bias_masked, 1)
            pool.wait_ge(att_y, NP)
            chain(pool.memset(state, 0.0))
            pool.memset(bk_chunk, 0.0).then_inc(rwkv_zero, 1)
            pool.wait_ge(rwkv_zero, 1)

            for p in range(NP):
                pool.wait_ge(within_ready, NT * (p + 1))
                for l in range(1, LV + 1):
                    m = LV * p + l - 1
                    for s in range(2):
                        if m >= 2:
                            pool.wait_ge(x_mm, 2 * (m - 2) + s + 1)
                        pool.tensor_tensor(heads4(mats(m_level[m % 2])(s)), n_of(s), over(level_mask(l)), ALU.mult).then_inc(mt_ready, 1)
                        pool.wait_ge(mt_ready, 2 * m + s + 1)
                        slot(2 * (l - 1) + s, p + 1 if p + 1 < NP else None)

            pool.wait_ge(yr_ready, NP)
            for s in range(2):
                chain(pool.memset(x_slot[s], 0.0))
            pool.wait_ge(rs_ready, 2)
            pool.wait_ge(h_ready, 2 * NT)
            for t in range(NT):
                pool.tensor_scalar(n_rows[:, t, :], h_res[:, t, :], rs2[:, t:t + 1], 1.0, ALU.mult, ALU.mult).then_inc(xn_ready, 1)
                pool.wait_ge(xn_ready, NT + t + 1)
            pool.wait_ge(slots_cleared, 16)
            pool.wait_ge(routed, SLOTS)
            for t in range(NT):
                for x in range(2):
                    pool.indirect_dma_start(dest_of_slot, bass.IndirectOffsetOnAxis(ap=slot_u[:, t, x:x + 1], axis=0),
                                            dest_u[:, t, x:x + 1], None).then_inc(scattered, 16)
            with if_over(pool):
                pool.dma_start(y_rows.rearrange("(n p) d -> p n d", p=P), x_slot[0].unsqueeze(1).to_broadcast([P, 2 * NT, D])).then_inc(y_cleared, 16)
                pool.wait_ge(y_cleared, 16)
            pool.wait_ge(slot_tok_ready, 1)
            pool.wait_ge(rows_out, 16 * NT)

            def gather(s, it):
                pool.tensor_copy(tok_now[s], slot_tok[:, bass.ds(it * 2 + s, 1)]).then_inc(tok_now_ready, 1)
                pool.wait_ge(tok_now_ready, it * 2 + s + 1)
                pool.sem_inc(gather_go, 1)
                pool.indirect_dma_start(x_slot[s], None, norm_rows, bass.IndirectOffsetOnAxis(ap=tok_now[s], axis=0),
                                        bounds_check=T - 1, oob_is_err=False).then_inc(x_slot_in[s], 16)

            def scatter(s, it, first=False):
                if not first:
                    pool.wait_ge(y_out[s], it * 16)
                pool.tensor_copy(dest_now[s], slot_dest[:, bass.ds(it * 2 + s, 1)]).then_inc(dest_now_ready, 1)
                pool.wait_ge(dest_now_ready, it * 2 + s + 1)
                pool.wait_ge(y_lo, it * 2 + s + 1)
                pool.wait_ge(y_hi, it * 2 + s + 1)
                pool.sem_inc(gather_go, 1)
                pool.indirect_dma_start(y_rows, bass.IndirectOffsetOnAxis(ap=dest_now[s], axis=0), y_slot[s], None,
                                        bounds_check=2 * T - 1, oob_is_err=False).then_inc(y_out[s], 16)

            for s in range(2):
                gather(s, 0)

            def expert_pass(it, first=False):
                for s in range(2):
                    pool.wait_ge(xs_mm, it * 4 + 2 * s + 2)
                    gather(s, it + 1)
                    scatter(s, it, first)

            expert_pass(0, first=True)
            with pool.Fori(1, NPAIR // 2 - 1) as it:
                expert_pass(it)
            for s in range(2):
                scatter(s, NPAIR // 2 - 1)

        @block.scalar
        def _(act):
            steps = [0]

            def chain(ins):
                steps[0] += 1
                ins.then_inc(act_step, 1)
                act.wait_ge(act_step, steps[0])

            act.wait_ge(eps_ready, 1)
            for t in range(NT):
                act.wait_ge(x_in[t], 16)
                ins = act.activation(x_norm[:, t, :], x_in_sb[:, t, :], ACT.Square, accum_out=ss[:, t:t + 1])
            chain(ins)
            chain(act.activation(ms, ss, ACT.Ln, scale=1.0 / D, bias=rms_eps))
            act.activation(rs, ms, ACT.Exp, scale=-0.5).then_inc(rs_ready, 1)

            def slot(k, seq, prep):
                if prep is not None:
                    q = prep
                    w0, a0, kk = (vec[:, v + q:v + q + 1] for v in (V_W0, V_A0, V_KK))
                    if k == 0:
                        act.wait_ge(prep_out, q)
                        act.wait_ge(prep_mm, 5 * q + 1)
                        act.activation(sgw, bank(6), ACT.Sigmoid, bias=w0).then_inc(sg_ready, 1)
                        act.activation(knorm, z[:, 4 + q, :], ACT.Square, scale=kk).then_inc(ksq_ready, 1)
                    if k == 1:
                        act.wait_ge(prep_mm, 5 * q + 2)
                        act.activation(iclr, bank(6), ACT.Sigmoid, bias=a0).then_inc(aa_ready, 1)
                    if k == 3:
                        act.wait_ge(cum_split, 2 * q + 2)
                        act.activation(dec, cum, ACT.Exp, scale=-DECAY_SCALE).then_inc(decay_ready, 1)
                        act.activation(cum_x, cum_x, ACT.Exp, scale=-DECAY_SCALE).then_inc(decay_ready, 1)
                        act.activation(cum, cum, ACT.Exp, scale=DECAY_SCALE).then_inc(decay_ready, 1)
                        act.activation(cum_e, cum_e, ACT.Exp, scale=-DECAY_SCALE).then_inc(decay_ready, 1)
                    if k == 4:
                        act.wait_ge(ksum_ready, q + 1)
                        chain(act.activation(knorm, knorm, ACT.Ln))
                        act.activation(knorm, knorm, ACT.Exp, scale=-0.5, bias=norm_bias).then_inc(kn_ready, 1)
                    if k == 5:
                        act.wait_ge(rk_ready, q + 1)
                        act.wait_ge(rt_ready, q + 1)
                        act.wait_ge(prep_mm, 5 * q + 5)
                        act.activation(z[:, q, :], bank(6), ACT.Copy).then_inc(g_ready, 1)
                if seq is not None:
                    if k == 7:
                        act.wait_ge(yc_ready, seq + 1)
                        act.activation(r_eff, y_buf, ACT.Square).then_inc(ysq_ready, 1)
                    if k == 8:
                        act.wait_ge(stat_mm, 2 * seq + 2)
                        chain(act.activation(r_eff, bank(7), ACT.Ln, scale=1.0 / HD, bias=gn_eps))
                        act.activation(r_eff, r_eff, ACT.Exp, scale=-0.5).then_inc(rstd_ready, 1)

            def split_hi(n):
                act.wait_ge(slab_in[n % RING], 16 * (n // RING + 1))
                if n >= 2:
                    act.wait_ge(slab_used, n - 1)
                act.activation(slab_hi[:, n % 2], slabs[:, n % RING], ACT.Copy).then_inc(slab_hi_ready, 1)

            split_hi(0)
            for k in range(KD):
                act.wait_ge(xt_mm, k + 1)
                act.activation(h_hi[:, k, :], bank(k), ACT.Copy, scale=vec[:, V_MIX + k:V_MIX + k + 1]).then_inc(hf_hi, 1)
            split_hi(1)
            for j, (n, kind, what) in enumerate(jobs):
                if kind == "feat" and what < 14:
                    act.wait_ge(z_mm, j + 1)
                    if j >= 2:
                        z_done(act, j - 2)
                    act.activation(shift_buf[j % 2][:, 1:T + 1], bank(2 + j % 2), ACT.Copy,
                                   scale=vec[:, V_MU + what:V_MU + what + 1]).then_inc(z_shift, 1)
                    if j == 1:
                        z_done(act, 1)
                        act.activation(z[0:64, 12, :], z[0:64, 12, :], ACT.Tanh).then_inc(lo_ready, 1)
                        act.activation(z[:, 13, :], z[:, 13, :], ACT.Sigmoid).then_inc(lo_ready, 1)
                elif z_reader(j) == "act":
                    act.wait_ge(z_mm, j + 1)
                    act.activation(k_pair[:, what - 18, :], bank(2 + j % 2), ACT.Copy).then_inc(z_act, 1)
                if first_job[n] == j and 2 <= n + 1 < len(slab_order):
                    split_hi(n + 1)
                if j == PREP_JOB:
                    z_done(act, j - 1)
                if 0 <= j - PREP_JOB < NSLOT:
                    slot(j - PREP_JOB, None, 0)

            def exp(u):
                h, i = units()[u]
                n = P * (i + 1)
                act.wait_ge(att_max, u + 1)
                act.activation(prob[:, u % 4, 0:n], prob[:, u % 4, 0:n], ACT.Exp, bias=nmax[:, u:u + 1],
                               accum_out=psumrow[:, u:u + 1]).then_inc(att_exp, 1)

            def evac_t(u):
                h, i = units()[u]
                if u % 8 == 0 and u >= 16:
                    act.wait_ge(att_pv, u // 8 - 1)
                act.wait_ge(att_tr, u + 1)
                act.activation(prob_t[:, (h // 2) % 2, h % 2, pt_col(i, 0):pt_col(i, i) + P], bank(6 + u % 2)[:, 0:P * (i + 1)], ACT.Copy).then_inc(att_pt, 1)

            def evac_y(pr):
                act.wait_ge(att_pv, pr + 1)
                act.activation(y_att[:, pr, :], bank(2 + pr % 2), ACT.Copy).then_inc(att_y, 1)

            for step in range(4 * NH + 7):
                if step < 4 * NH:
                    exp(step)
                if 3 <= step < 4 * NH + 3:
                    evac_t(step - 3)
                if step >= 14 and (step - 14) % 8 == 0:
                    evac_y((step - 14) // 8)

            act.wait_ge(rwkv_zero, 1)
            for p in range(NP):
                for t in range(NT):
                    act.wait_ge(tok_mm, NT * p + t + 1)
                    b = bank(4 + t % 2)
                    act.activation(rhs[:, t, :, 0:HD], b[:, 0:P].rearrange("p (h d) -> p h d", h=2), ACT.Copy)
                    act.activation(v_rows[:, t, :], b[:, P:2 * P], ACT.Copy)
                    act.activation(bk_chunk[0:64, t, 0, :], b[0:64, 2 * P:4 * P], ACT.Copy)
                    act.activation(bk_chunk[64:128, t, 1, :], b[64:128, 2 * P:4 * P], ACT.Copy).then_inc(tok_ready, 1)
                for s in range(2):
                    act.wait_ge(tr_mm, 2 * LV * p + s + 1)
                    act.activation(mats(t_inv)(s), bank(4 + s).rearrange("p (m t) -> p m t", t=P), ACT.Copy).then_inc(tt_ready, 1)
                act.wait_ge(g_mm, p + 1)
                act.activation(rhs[:, :, :, HD:P], bank(6).rearrange("p (n h d) -> p n h d", n=NT, h=2), ACT.Copy).then_inc(ga_ready, 1)
                for l in range(1, LV + 1):
                    m = LV * p + l - 1
                    for s in range(2):
                        if l >= 2:
                            act.wait_ge(tr_mm, 2 * m + s + 1)
                            act.activation(mats(t_inv_t)(s), bank(4 + s).rearrange("p (m t) -> p m t", t=P), ACT.Copy).then_inc(tt_ready, 1)
                        act.wait_ge(x_mm, 2 * m + s + 1)
                        act.activation(mats(m_t)(s), bank(s).rearrange("p (m t) -> p m t", t=P), ACT.Copy).then_inc(x_ready, 1)
                    for s in range(2):
                        slot(2 * (l - 1) + s, p - 1 if p else None, p + 1 if p + 1 < NP else None)
                for s in range(2):
                    act.wait_ge(w_mm, 2 * p + s + 1)
                    for t in (2 * s, 2 * s + 1):
                        ins = act.activation(wy[:, t, :, :, :].rearrange("p x h d -> p h x d"),
                                             bank(s)[:, (t % 2) * 2 * P:(t % 2 + 1) * 2 * P].rearrange("p (h x d) -> p h x d", h=2, x=2), ACT.Copy)
                    ins.then_inc(w_ready, 1)
                act.wait_ge(yr_ready, p)
                act.wait_ge(y0_mm, p + 1)
                act.activation(y_buf, bank(3), ACT.Copy).then_inc(y0_ready, 1)
                act.wait_ge(s_ready, 7 * p)
                for s in range(2):
                    act.wait_ge(q_mm, 2 * p + s + 1)
                    act.activation(step_add[:, 4 * s:4 * s + 4, :], bank(s).rearrange("p (c i) -> p c i", i=P), ACT.Copy).then_inc(q_ready, 1)
            for k in range(NSLOT):
                slot(k, NP - 1, None)

            def square_sum(t, rows, junk, ssq):
                return act.activation(junk, rows, ACT.Square, accum_out=ssq[:, t:t + 1])

            def rms(ssq, rsq):
                chain(act.activation(ssq, ssq, ACT.Ln, scale=1.0 / D, bias=rms_eps))
                act.activation(rsq, ssq, ACT.Exp, scale=-0.5).then_inc(rs_ready, 1)

            for t in range(NT):
                act.wait_ge(h_ready, 2 * t + 2)
                ins = square_sum(t, h_res[:, t, :], n_rows[:, t, :], ss2)
            chain(ins)
            rms(ss2, rs2)
            act.wait_ge(routed, GROUP_DIFF)
            act.activation(g_exp, g_exp, ACT.Exp).then_inc(route_exp, 1)
            act.wait_ge(routed, EXPERT_DIFF)
            act.activation(e_ratio, e_ratio, ACT.Exp).then_inc(route_exp, 1)
            act.wait_ge(ple_mm, 1)
            for k in range(KE):
                act.activation(ple_pt[:, k, :], bank(6 + k), ACT.Copy).then_inc(ple_t_ready, 1)
            act.wait_ge(rows_out, 16 * NT)
            act.wait_ge(nrow_mm, 2 * NT)
            for t in range(NT):
                for n in range(2):
                    act.wait_ge(proj_mm, 2 * t + n + 1)
                    act.activation(ple_proj[:, t, n * 512:(n + 1) * 512], bank(6 + n), ACT.Copy).then_inc(proj_ready, 1)

            def expert_pass(it, first=False):
                for s in range(2):
                    act.wait_ge(up_mm, it * 2 + s + 1)
                    act.activation(hid[s], bank(2 + s)[:, 0:DE], ACT.Silu).then_inc(silu_ready, 1)
                    act.wait_ge(hid_mm, it * 2 + s + 1)
                    act.activation(hid_t[s], bank(4)[:, 0:2 * P].rearrange("p (k t) -> p k t", k=KE), ACT.Copy).then_inc(hidt_ready, 1)
                    act.wait_ge(down_mm, it * 4 + 2 * s + 1)
                    if not first:
                        act.wait_ge(y_out[s], it * 16)
                    act.activation(y_slot[s][:, 0:512], bank(5), ACT.Copy).then_inc(y_lo, 1)

            expert_pass(0, first=True)
            with act.Fori(1, NPAIR // 2) as it:
                expert_pass(it)
            with if_over(act):
                with act.Fori(0, NE) as e:
                    for t in range(NT):
                        act.wait_ge(over_mm, over_up(e, t))
                        act.activation(hid[0], bank(2)[:, 0:DE], ACT.Silu).then_inc(over_act, 1)
                        act.wait_ge(over_mm, over_turned(e, t))
                        act.activation(hid_t[0], bank(4)[:, 0:2 * P].rearrange("p (k t) -> p k t", k=KE), ACT.Copy).then_inc(over_act, 1)
            for t in range(NT):
                act.wait_ge(h_ready, 2 * NT + t + 1)
                ins = square_sum(t, h_res[:, t, :], n3_rows[:, t, :], ss3)
            chain(ins)
            rms(ss3, rs3)
            for t in range(NT):
                act.wait_ge(gate_pre, t + 1)
                act.activation(gate[t % 2], gate[t % 2], ACT.Sigmoid).then_inc(gate_ready, 1)
                act.wait_ge(h_ready, 3 * NT + t + 1)
                if t >= 2:
                    act.wait_ge(out_stored[t % 2], 16 * (t // 2))
                chain(square_sum(t, h_res[:, t, :], out_rows[t % 2], ss4))
                rms(ss4[:, t:t + 1], rs4[:, t:t + 1])

        @block.vector
        def _(dve):
            steps = [0]

            def chain(ins):
                steps[0] += 1
                ins.then_inc(dve_step, 1)
                dve.wait_ge(dve_step, steps[0])

            dve.memset(gn_eps, GN_EPS)
            dve.memset(norm_bias, 0.5 * NORM_SCALE_LOG2 * math.log(2.0))
            dve.memset(rms_eps, RMS_EPS).then_inc(eps_ready, 1)
            dve.wait_ge(consts_in, 32)
            dve.tensor_scalar(one_mu, vec[:, V_MU:V_MU + 14], -1.0, 1.0, ALU.mult, ALU.add)
            for t in range(NT):
                if t == 0:
                    dve.wait_ge(rs_ready, 1)
                dve.tensor_scalar(x_norm[:, t, :], x_in_sb[:, t, :], rs[:, t:t + 1], None, ALU.mult).then_inc(xn_ready, 1)

            def slot(k, seq, prep):
                if seq is not None:
                    q = seq
                    if k < 7:
                        if k == 0:
                            dve.wait_ge(q_ready, 2 * q + 2)
                        else:
                            dve.wait_ge(seq_mm, 6 * q + k)
                        for h in range(2):
                            rows, d = slice(64 * h, 64 * h + 64), slice(64 * h, 64 * h + 64)
                            if k == 0:
                                ins = dve.tensor_copy(state[rows, 1, d], step_add[rows, 0, d])
                            else:
                                ins = dve.tensor_tensor(state[rows, k + 1, d], bank(7)[rows, 64 * h + P * (k % 4):64 * h + P * (k % 4) + 64],
                                                        step_add[rows, k, d], ALU.add)
                        ins.then_inc(s_ready, 1)
                    if k == 7:
                        dve.wait_ge(y_mm, q + 1)
                        dve.wait_ge(y0_ready, q + 1)
                        dve.tensor_tensor(y_buf[:, C:T], bank(7)[:, C:T], y_buf[:, C:T], ALU.add).then_inc(y_ready, 1)
                        dve.wait_ge(y_ready, q + 1)
                        dve.wait_ge(stat_mm, 2 * q + 1)
                        dve.scalar_tensor_tensor(out=y_buf, in0=bank(7), scalar=-1.0 / HD, in1=y_buf, op0=ALU.mult, op1=ALU.add).then_inc(yc_ready, 1)
                        dve.wait_ge(yc_ready, q + 1)
                    if k == 9:
                        dve.wait_ge(rstd_ready, q + 1)
                        chain(dve.scalar_tensor_tensor(out=y_buf, in0=y_buf, scalar=vec[:, V_LNW + q:V_LNW + q + 1], in1=r_eff, op0=ALU.mult, op1=ALU.mult))
                        chain(dve.scalar_tensor_tensor(out=y_buf, in0=y_buf, scalar=vec[:, V_LNB + q:V_LNB + q + 1], in1=z[:, 4 + q, :], op0=ALU.add, op1=ALU.add))
                        dve.wait_ge(g_ready, q + 1)
                        dve.tensor_tensor(z[:, 8 + q, :], y_buf, z[:, q, :], ALU.mult).then_inc(yr_ready, 1)
                if prep is not None:
                    q = prep
                    r, kq, v = z[:, q, :], z[:, 4 + q, :], z[:, 8 + q, :]
                    if k == 0:
                        chain(dve.tensor_scalar(kkn, kq, vec[:, V_KK + q:V_KK + q + 1], None, ALU.mult))
                        dve.wait_ge(sg_ready, q + 1)
                        dve.tensor_tensor_scan(cum, const[:, K_RESET:K_RESET + T], sgw, 0.0, ALU.mult, ALU.add).then_inc(cum_ready, 1)
                    if k == 2:
                        dve.wait_ge(prep_mm, 5 * q + 3)
                        dve.tensor_scalar(knorm, bank(6), 1e-24, 2.0 ** NORM_SCALE_LOG2, ALU.max, ALU.mult).then_inc(ksum_ready, 1)
                        dve.wait_ge(aa_ready, q + 1)
                        chain(dve.tensor_scalar(k_mod, iclr, -1.0, vec[:, V_KA + q:V_KA + q + 1], ALU.add, ALU.mult))
                        chain(dve.scalar_tensor_tensor(out=k_mod, in0=k_mod, scalar=1.0, in1=kq, op0=ALU.add, op1=ALU.mult))
                    if k == 3:
                        dve.wait_ge(cum_split, 2 * q + 2)
                        dve.scalar_tensor_tensor(out=sgw, in0=r, scalar=vec[:, V_RK + q:V_RK + q + 1], in1=k_mod, op0=ALU.mult, op1=ALU.mult).then_inc(rk_ready, 1)
                    if k == 4:
                        dve.wait_ge(decay_ready, 4 * q + 1)
                        dve.tensor_copy(d_end[q % 2], dec[:, C - 1::C])
                        dve.tensor_tensor(r_dec[q % 2], r, dec, ALU.mult).then_inc(rt_ready, 1)
                        dve.wait_ge(prep_mm, 5 * q + 4)
                        dve.tensor_tensor(kq, bank(6), v, ALU.mult).then_inc(bonus_ready, 1)
                    if k == 5:
                        dve.wait_ge(kn_ready, q + 1)
                        chain(dve.tensor_tensor(kkn, kkn, knorm, ALU.mult))
                        dve.wait_ge(unit_in_used, q)
                        dve.wait_ge(ar_ready, 4 * q)
                        dve.wait_ge(decay_ready, 4 * q + 2)
                        dve.scalar_tensor_tensor(out=a_dec, in0=kkn, scalar=-1.0, in1=cum_x, op0=ALU.mult, op1=ALU.mult).then_inc(at_ready, 1)
                        chain(dve.tensor_tensor(knorm, kkn, iclr, ALU.mult))
                    if k == 6:
                        dve.wait_ge(decay_ready, 4 * q + 4)
                        dve.tensor_tensor(b_inc, knorm, cum, ALU.mult)
                        dve.tensor_tensor(k_inc, k_mod, cum, ALU.mult)
                    if k == 7:
                        dve.tensor_tensor(b_end, knorm, cum_e, ALU.mult)
                        dve.tensor_tensor(k_end, k_mod, cum_e, ALU.mult).then_inc(prep_out, 1)

            def split_lo(n):
                dve.wait_ge(slab_hi_ready, n + 1)
                dve.tensor_tensor(slab_lo[:, n % 2], slabs[:, n % RING], slab_hi[:, n % 2].bitcast(F32), ALU.subtract).then_inc(slab_lo_ready, 1)

            split_lo(0)
            for k in range(KD):
                dve.wait_ge(hf_hi, k + 1)
                dve.scalar_tensor_tensor(out=h_lo[:, k, :], in0=bank(k), scalar=vec[:, V_MIX + k:V_MIX + k + 1],
                                         in1=h_hi[:, k, :].bitcast(F32), op0=ALU.mult, op1=ALU.subtract).then_inc(hf_lo, 1)
            dve.wait_ge(zeros_ready, 5 + NH)
            for j, (n, kind, what) in enumerate(jobs):
                if first_job[n] == j and n + 1 < len(slab_order):
                    split_lo(n + 1)
                zb = bank(2 + j % 2)
                if z_reader(j) == "dve":
                    dve.wait_ge(z_mm, j + 1)
                if z_reader(j) != "dve":
                    pass
                elif kind == "tok":
                    half, t = what
                    dve.tensor_copy(v_tok[:, t, half * SLAB:(half + 1) * SLAB], zb[:, 0:SLAB]).then_inc(z_dve, 1)
                elif what < 14:
                    dve.wait_ge(z_shift, j + 1)
                    dve.scalar_tensor_tensor(out=z[:, what, :], in0=zb, scalar=one_mu[:, what:what + 1],
                                             in1=shift_buf[j % 2][:, 0:T], op0=ALU.mult, op1=ALU.add).then_inc(z_dve, 1)
                else:
                    h = 2 * (what - 14)
                    dve.tensor_scalar(q_head[0:64, h, :], zb[0:64, :], HD ** -0.5, None, ALU.mult)
                    dve.tensor_scalar(q_head[64:128, h + 1, :], zb[64:128, :], HD ** -0.5, None, ALU.mult).then_inc(z_dve, 1)
                if j == PREP_JOB:
                    z_done(dve, j - 1)
                if 0 <= j - PREP_JOB < NSLOT:
                    slot(j - PREP_JOB, None, 0)

            def scores(u):
                h, i = units()[u]
                n = P * (i + 1)
                dve.wait_ge(att_s_mm, u + 1)
                if i == 0:
                    dve.wait_ge(bias_masked, h + 1)
                if u >= 4:
                    dve.wait_ge(att_tr, u - 3)
                dve.tensor_tensor(prob[:, u % 4, 0:n], bank(4 + u % 2)[:, 0:n], bias_w[:, h % 4, T - n:T], ALU.add).then_inc(att_s_read, 1)
                dve.wait_ge(att_s_read, u + 1)
                dve.tensor_reduce(nmax[:, u:u + 1], prob[:, u % 4, 0:n], AX.X, ALU.max, negate=True).then_inc(att_max, 1)

            def normalise(u):
                h, i = units()[u]
                n = P * (i + 1)
                dve.wait_ge(att_exp, u + 1)
                chain(dve.reciprocal(prow_inv[:, u:u + 1], psumrow[:, u:u + 1]))
                dve.tensor_scalar(prob[:, u % 4, 0:n], prob[:, u % 4, 0:n], prow_inv[:, u:u + 1], None, ALU.mult).then_inc(att_p, 1)

            for step in range(4 * NH + 1):
                if step < 4 * NH:
                    scores(step)
                if step >= 1:
                    normalise(step - 1)

            dve.wait_ge(rwkv_zero, 1)
            for p in range(NP):
                for t in range(NT):
                    dve.wait_ge(s1_mm, NT * p + t + 1)
                    dve.tensor_tensor(within[:, t, :].rearrange("p (h n) -> p h n", h=2), bank(6).rearrange("p (h n) -> p h n", h=2), mask_2h, ALU.mult).then_inc(within_ready, 1)
                    dve.wait_ge(s2_mm, NT * p + t + 1)
                    dve.tensor_tensor(across[:, t, :].rearrange("p (h n) -> p h n", h=2), bank(7).rearrange("p (h n) -> p h n", h=2), mask_2h, ALU.mult).then_inc(across_ready, 1)
                dve.wait_ge(within_ready, NT * (p + 1))
                for s in range(2):
                    chain(dve.tensor_tensor(heads4(mats(t_inv_t)(s)), n_of(s), over(level_mask(0)), ALU.mult))
                    dve.tensor_tensor(heads4(mats(t_inv_t)(s)), heads4(mats(t_inv_t)(s)), over(ident), ALU.add).then_inc(tt_init, 1)
                for l in range(1, LV + 1):
                    m = LV * p + l - 1
                    for s in range(2):
                        dve.wait_ge(d_mm, 2 * m + s + 1)
                        dst = mats(t_inv if l < LV else t_inv_t)(s)
                        dve.tensor_tensor(dst, bank(2 + s).rearrange("p (m t) -> p m t", t=P), dst, ALU.add).then_inc(t_ready, 1)
                        slot(2 * (l - 1) + s, p - 1 if p else None, p + 1 if p + 1 < NP else None)
                dve.wait_ge(rp_mm, p + 1)
                dve.tensor_tensor(r_eff, bank(2), r_dec[p % 2], ALU.add).then_inc(rp_ready, 1)
                for s in range(2):
                    dve.wait_ge(mc_mm, 2 * p + s + 1)
                    for c in range(4 * s, 4 * s + 4):
                        ins = dve.scalar_tensor_tensor(out=step_mat[:, c, :], in0=ident, scalar=d_end[p % 2][:, c:c + 1],
                                                       in1=bank(4 + s)[:, (c % 4) * P:(c % 4 + 1) * P], op0=ALU.mult, op1=ALU.add)
                    ins.then_inc(mc_ready, 1)
            for k in range(NSLOT):
                slot(k, NP - 1, None)

            dve.wait_ge(res_in, 16)
            for o in range(2 * NT):
                t, n = o // 2, o % 2
                dve.wait_ge(op_mm, o + 1)
                dve.tensor_tensor(h_res[:, t, n * 512:(n + 1) * 512], bank(o), h_res[:, t, n * 512:(n + 1) * 512], ALU.add).then_inc(h_ready, 1)

            def turn_rows(t, n_t, b0, mm, mm_at, w, ready):
                for g in range(2):
                    dve.wait_ge(mm, mm_at + g)
                    scale = vec[:, w + 4 * g:w + 4 * g + 4].unsqueeze(2).to_broadcast([P, 4, P])
                    ins = dve.tensor_tensor(n_t[:, 4 * g:4 * g + 4, :], bank(b0 + g).rearrange("p (k t) -> p k t", k=4), scale, ALU.mult)
                ins.then_inc(ready, 1)

            for t in range(NT):
                turn_rows(t, n_feat[:, t], 2 * (t % 2), nrow_mm, 2 * t + 1, V_FFN, nf_ready)
            dve.wait_ge(router_in, 32)
            dve.memset(g_logit[:, :, NG:8], NEG)
            for x in range(2):
                dve.tensor_scalar(dest_u[:, :, x], const[:, K_TOK:K_TOK + NT], float(x * T), None, ALU.add)
            dve.wait_ge(route_mm, 1)
            lg = bank(4)[:, 0:NT * (NG + NE)].rearrange("p (n e) -> p n e", n=NT)
            bias = router_b.unsqueeze(1).to_broadcast([P, NT, NG + NE])
            scale = rs2.unsqueeze(2).to_broadcast([P, NT, NG + NE])
            e_rows = e_logit.rearrange("p n g e -> p n (g e)")
            dve.wait_ge(rs_ready, 2)
            dve.tensor_tensor(g_logit[:, :, 0:NG], lg[:, :, 0:NG], scale[:, :, 0:NG], ALU.mult)
            chain(dve.tensor_tensor(e_rows, lg[:, :, NG:], scale[:, :, NG:], ALU.mult))
            dve.tensor_tensor(g_logit[:, :, 0:NG], g_logit[:, :, 0:NG], bias[:, :, 0:NG], ALU.add)
            chain(dve.tensor_tensor(e_rows, e_rows, bias[:, :, NG:], ALU.add))
            for t in range(NT):
                chain(dve.max(g_top[:, t, :], g_logit[:, t, :]))
                chain(dve.max_index(g_idx[:, t, :], g_top[:, t, :], g_logit[:, t, :]))
            dve.tensor_copy(g_sel.unsqueeze(2), g_idx[:, :, 0:1])
            dve.tensor_tensor(g_exp, g_logit[:, :, 0:NG], g_top[:, :, 0:1].to_broadcast([P, NT, NG]), ALU.subtract).then_inc(routed, 1)
            dve.wait_ge(routed, GROUP_DIFF)
            iota = const[:, K_IOTA:K_IOTA + NE].unsqueeze(1)
            chain(dve.tensor_tensor(g_hot, iota[:, :, 0:NG].to_broadcast([P, NT, NG]), g_sel.unsqueeze(2).to_broadcast([P, NT, NG]), ALU.is_equal))
            chain(dve.tensor_tensor(e_mask.rearrange("p n e g -> p n g e"), e_logit, g_hot.unsqueeze(3).to_broadcast([P, NT, NG, EPG]), ALU.mult))
            chain(dve.tensor_reduce(sel, e_mask, AX.X, ALU.add))
            for t in range(NT):
                chain(dve.max(e_top[:, t, :], sel[:, t, :]))
                chain(dve.max_index(e_idx[:, t, :], e_top[:, t, :], sel[:, t, :]))
            dve.tensor_tensor(e_ratio.unsqueeze(2), e_top[:, :, 1:2], e_top[:, :, 0:1], ALU.subtract).then_inc(routed, 1)
            chain(dve.tensor_copy(e_loc, e_idx[:, :, 0:2]))
            chain(dve.scalar_tensor_tensor(out=expert, in0=g_sel.unsqueeze(2).to_broadcast([P, NT, 2]), scalar=float(EPG), in1=e_loc, op0=ALU.mult, op1=ALU.add))
            for x in range(2):
                chain(dve.tensor_tensor(hot[x], iota.to_broadcast([P, NT, NE]), expert[:, :, x:x + 1].to_broadcast([P, NT, NE]), ALU.is_equal))
            dve.tensor_tensor(hot_sum, hot[0], hot[1], ALU.add).then_inc(routed, 1)
            dve.wait_ge(route_exp, 1)
            chain(dve.tensor_reduce(g_sum, g_exp, AX.X, ALU.add))
            chain(dve.reciprocal(p_group, g_sum))
            dve.wait_ge(route_exp, 2)
            chain(dve.tensor_scalar(g_sum, e_ratio, 1.0, None, ALU.add))
            chain(dve.reciprocal(g_sum, g_sum))
            chain(dve.tensor_tensor(weight[:, :, 0:1], p_group.unsqueeze(2), g_sum.unsqueeze(2), ALU.mult))
            chain(dve.tensor_tensor(weight[:, :, 1:2], weight[:, :, 0:1], e_ratio.unsqueeze(2), ALU.mult))
            dve.wait_ge(route_mm, 2)
            rank = bank(5)[:, 0:NT * NE].rearrange("p (n e) -> p n e", n=NT)
            for x in range(2):
                chain(dve.tensor_tensor(hot_pos, rank, hot[x], ALU.mult))
                chain(dve.tensor_reduce(pos[:, :, x:x + 1].rearrange("p n o -> p (n o)"), hot_pos, AX.X, ALU.add))
            chain(dve.scalar_tensor_tensor(out=slot_f, in0=pos, scalar=float(NE), in1=expert, op0=ALU.mult, op1=ALU.add))
            dve.tensor_copy(slot_u, slot_f).then_inc(routed, 1)
            chain(dve.tensor_scalar(fits, pos, float(CAP), None, ALU.is_lt))
            chain(dve.tensor_tensor(w_main, weight, fits, ALU.mult))
            chain(dve.tensor_scalar(fits, fits, -1.0, 1.0, ALU.mult, ALU.add))
            chain(dve.tensor_reduce(over_rows, fits, AX.XY, ALU.add))
            dve.tensor_tensor(pos, weight, fits, ALU.mult).then_inc(over_counted, 1)
            dve.wait_ge(over_counted, 1)
            for x in range(2):
                chain(dve.tensor_tensor(hot[x], hot[x], pos[:, :, x:x + 1].to_broadcast([P, NT, NE]), ALU.mult))
            dve.tensor_tensor(w_over, hot[0], hot[1], ALU.add)
            dve.wait_ge(route_mm, 3)
            dve.tensor_copy(over_u, bank(5)[:, 0:1]).then_inc(routed, 1)

            def expert_rows(s, it):
                for g in range(2):
                    dve.wait_ge(xs_mm, it * 4 + 2 * s + 1 + g)
                    scale = vec[:, V_FFN + 4 * g:V_FFN + 4 * g + 4].unsqueeze(2).to_broadcast([P, 4, P])
                    ins = dve.tensor_tensor(x_slot_t[s][:, 4 * g:4 * g + 4, :], bank(g).rearrange("p (k t) -> p k t", k=4), scale, ALU.mult)
                ins.then_inc(xs_ready, 1)

            def expert_pass(it, last=False):
                for s in range(2):
                    dve.wait_ge(silu_ready, it * 2 + s + 1)
                    dve.tensor_tensor(hid[s], bank(2 + s)[:, DE:2 * DE], hid[s], ALU.mult).then_inc(hid_ready, 1)
                    if not (last and s == 1):
                        expert_rows(1 - s, it + s)
                    dve.wait_ge(down_mm, it * 4 + 2 * s + 2)
                    dve.wait_ge(y_lo, it * 2 + s + 1)
                    dve.tensor_copy(y_slot[s][:, 512:D], bank(6)).then_inc(y_hi, 1)

            dve.wait_ge(slot_dest_in, 16)
            chain(dve.tensor_copy(slot_tok_f, slot_dest))
            chain(dve.tensor_scalar(slot_second, slot_tok_f, float(T), float(T), ALU.is_ge, ALU.mult))
            dve.tensor_tensor(slot_tok, slot_tok_f, slot_second, ALU.subtract).then_inc(slot_tok_ready, 1)
            expert_rows(0, 0)
            with dve.Fori(0, NPAIR // 2 - 1) as it:
                expert_pass(it)
            expert_pass(NPAIR // 2 - 1, last=True)
            with if_over(dve):
                scale = vec[:, V_FFN:V_FFN + KD].unsqueeze(2).to_broadcast([P, KD, P])
                for t in range(NT):
                    for g in range(2):
                        dve.wait_ge(over_mm, 2 * t + 1 + g)
                        ins = dve.tensor_tensor(over_feat[:, t, 4 * g:4 * g + 4, :], bank(2 * (t % 2) + g).rearrange("p (k t) -> p k t", k=4),
                                                scale[:, 4 * g:4 * g + 4, :], ALU.mult)
                    ins.then_inc(over_dve, 1)
                with dve.Fori(0, NE) as e:
                    dve.wait_ge(over_dve, over_col(e) - 1)
                    dve.tensor_copy(w_col.unsqueeze(2), w_over[:, :, bass.ds(e, 1)]).then_inc(over_dve, 1)
                    dve.wait_ge(over_dve, over_col(e))
                    for t in range(NT):
                        dve.wait_ge(over_act, over_silu(e, t))
                        dve.tensor_tensor(hid[0], bank(2)[:, DE:2 * DE], hid[0], ALU.mult).then_inc(over_dve, 1)
                        dve.wait_ge(over_mm, over_down(e, t))
                        for n in range(2):
                            half = slice(n * 512, (n + 1) * 512)
                            ins = dve.scalar_tensor_tensor(out=h_res[:, t, half], in0=bank(5 + n), scalar=w_col[:, t:t + 1],
                                                           in1=h_res[:, t, half], op0=ALU.mult, op1=ALU.add)
                        ins.then_inc(over_dve, 1)
                dve.wait_ge(over_dve, over_col(NE - 1) + 2 * NT)
            for t in range(NT):
                dve.wait_ge(y_tok_in[t], 32)
                for x in range(2):
                    ins = dve.scalar_tensor_tensor(out=h_res[:, t, :], in0=y_tok[:, t, x, :], scalar=w_main[:, t, x:x + 1], in1=h_res[:, t, :], op0=ALU.mult, op1=ALU.add)
                    if x == 0:
                        chain(ins)
                ins.then_inc(h_ready, 1)
                turn_rows(t, n3_feat[:, t], 2 * (t % 2), nrow_mm, 2 * NT + 2 * t + 1, V_PLE, nf_ready)
            dve.wait_ge(ple_in, 64)
            dve.wait_ge(proj_ready, 2 * NT)
            dve.wait_ge(rs_ready, 3)
            for t in range(NT):
                for n in range(2):
                    half = slice(n * 512, (n + 1) * 512)
                    dve.wait_ge(gate_mm, 2 * t + n + 1)
                    ins = dve.scalar_tensor_tensor(out=gate[t % 2][:, half], in0=bank(4 + 2 * (t % 2) + n), scalar=rs3[:, t:t + 1], in1=gate_b[:, half], op0=ALU.mult, op1=ALU.add)
                ins.then_inc(gate_pre, 1)
                dve.wait_ge(gate_ready, t + 1)
                chain(dve.tensor_tensor(gate[t % 2], ple_proj[:, t, :], gate[t % 2], ALU.mult))
                dve.tensor_tensor(h_res[:, t, :], h_res[:, t, :], gate[t % 2], ALU.add).then_inc(h_ready, 1)
                dve.wait_ge(rs_ready, t + 4)
                dve.scalar_tensor_tensor(out=out_rows[t % 2], in0=h_res[:, t, :], scalar=rs4[:, t:t + 1], in1=final_w, op0=ALU.mult, op1=ALU.mult).then_inc(out_ready, 1)

        @block.tensor
        def _(pe):
            pe.wait_ge(consts_in, 32)
            for t in range(NT):
                pe.wait_ge(xn_ready, t + 1)
                for k in range(KD):
                    ins = pe.transpose(bank(k)[:, t * P:(t + 1) * P], x_norm[:, t, k:k + (P - 1) * KD + 1:KD], ident)
                    if t == NT - 1:
                        ins.then_inc(xt_mm, 1)
            def slot(k, seq, prep):
                if seq is not None:
                    q = seq
                    if 1 <= k < 7:
                        pe.wait_ge(s_ready, 7 * q + k)
                        pe.matmul(bank(7)[:, P * (k % 4):P * (k % 4) + P], step_mat[:, k, :], state[:, k, :], start=True, stop=True).then_inc(seq_mm, 1)
                    if k == 7:
                        pe.wait_ge(s_ready, 7 * q + 7)
                        for c in range(1, NC):
                            ins = pe.matmul(bank(7)[:, c * C:(c + 1) * C], state[:, c, :], r_eff[:, c * C:(c + 1) * C], start=True, stop=True)
                        ins.then_inc(y_mm, 1)
                        pe.wait_ge(y_ready, q + 1)
                        pe.matmul(bank(7), head_ones, y_buf, start=True, stop=True).then_inc(stat_mm, 1)
                    if k == 8:
                        pe.wait_ge(ysq_ready, q + 1)
                        pe.matmul(bank(7), head_ones, r_eff, start=True, stop=True).then_inc(stat_mm, 1)
                if prep is not None:
                    q = prep
                    cols = slice(q * P, (q + 1) * P)
                    if k == 0:
                        if q == 0:
                            pe.wait_ge(lo_ready, 2)
                            pe.wait_ge(lora_in, 48)
                            pe.wait_ge(zeros_ready, 3)
                        if q == 1:
                            pe.wait_ge(lora_in, 96)
                            pe.wait_ge(zeros_ready, 6 + NH)
                        pe.matmul(bank(6), lora_w[q > 0][:, 0, cols], z[:, 12, :], start=True, stop=True).then_inc(prep_mm, 1)
                    if k == 1:
                        pe.wait_ge(sg_ready, q + 1)
                        pe.matmul(bank(6), lora_w[q > 0][:, 1, cols], z[:, 12, :], start=True, stop=True).then_inc(prep_mm, 1)
                    if k == 2:
                        pe.wait_ge(aa_ready, q + 1)
                        pe.wait_ge(ksq_ready, q + 1)
                        pe.matmul(bank(6), head_ones, knorm, start=True, stop=True).then_inc(prep_mm, 1)
                    if k == 4:
                        pe.wait_ge(ksum_ready, q + 1)
                        pe.wait_ge(rk_ready, q + 1)
                        pe.matmul(bank(6), head_ones, sgw, start=True, stop=True).then_inc(prep_mm, 1)
                    if k == 5:
                        pe.wait_ge(bonus_ready, q + 1)
                        pe.matmul(bank(6), lora_w[q > 0][:, 2, cols], z[:, 13, :], start=True, stop=True).then_inc(prep_mm, 1)

            for j, (n, kind, what) in enumerate(jobs):
                pe.wait_ge(slab_lo_ready, n + 1)
                if j >= 2:
                    z_done(pe, j - 2)
                elif j == 0:
                    pe.wait_ge(hf_lo, 3)
                zb = bank(2 + j % 2)
                for k in range(KD):
                    if j == 0:
                        pe.wait_ge(hf_lo, k + 1)
                    for x, (h, w) in enumerate(((h_hi, slab_hi), (h_lo, slab_hi), (h_hi, slab_lo))):
                        first, last = k == 0 and x == 0, k == KD - 1 and x == 2
                        if kind == "tok":
                            ins = pe.matmul(zb[:, 0:SLAB], h[:, k, what[1] * P:(what[1] + 1) * P],
                                            w[:, n % 2, k, :], start=first, stop=last)
                        else:
                            c = (what % 2) * P
                            ins = pe.matmul(zb, w[:, n % 2, k, c:c + P], h[:, k, :], start=first, stop=last)
                ins.then_inc(z_mm, 1)
                if last_job[n] == j:
                    pe.wait_ge(z_mm, j + 1)
                    pe.sem_inc(slab_used, 1)
                if 0 <= j - PREP_JOB < NSLOT:
                    slot(j - PREP_JOB, None, 0)
            pe.wait_ge(z_act, z_count(NJ - 1, "act"))
            pe.wait_ge(z_dve, z_count(NJ - 1, "dve"))

            def scores(u):
                h, i = units()[u]
                if u >= 2:
                    pe.wait_ge(att_s_read, u - 1)
                n = P * (i + 1)
                pe.matmul(bank(4 + u % 2)[:, 0:n], q_head[:, h, i * P:(i + 1) * P], k_pair[:, h // 2, 0:n],
                          start=True, stop=True).then_inc(att_s_mm, 1)

            def turn(u):
                h, i = units()[u]
                pe.wait_ge(att_p, u + 1)
                if u >= 2:
                    pe.wait_ge(att_pt, u - 1)
                for j in range(i + 1):
                    ins = pe.transpose(bank(6 + u % 2)[:, j * P:(j + 1) * P], prob[:, u % 4, j * P:(j + 1) * P], ident)
                ins.then_inc(att_tr, 1)

            def values(pr):
                pe.wait_ge(att_pt, 8 * (pr + 1))
                if pr >= 2:
                    pe.wait_ge(att_y, pr - 1)
                for i in range(NT):
                    for j in range(i + 1):
                        for par in range(2):
                            h = 2 * pr + par
                            ins = pe.matmul(bank(2 + pr % 2)[64 * par:64 * par + 64, i * P:(i + 1) * P],
                                            v_tok[:, j, h * HD:(h + 1) * HD],
                                            prob_t[:, pr % 2, par, pt_col(i, j):pt_col(i, j) + P],
                                            start=(j == 0), stop=(j == i))
                ins.then_inc(att_pv, 1)

            for step in range(4 * NH + 7):
                if step < 4 * NH:
                    scores(step)
                if 3 <= step < 4 * NH + 3:
                    turn(step - 3)
                if step >= 13 and (step - 13) % 8 == 0:
                    values((step - 13) // 8)

            pe.wait_ge(rwkv_zero, 1)
            for p in range(NP):
                pe.wait_ge(prep_out, p + 1)
                pe.wait_ge(ar_ready, 4 * (p + 1))
                pe.wait_ge(g_ready, p + 1)
                if p >= 2:
                    pe.wait_ge(rstd_ready, p - 1)
                pe.wait_ge(mc_ready, 2 * p)
                for t in range(NT):
                    tok = slice(t * P, (t + 1) * P)
                    if t:
                        pe.wait_ge(within_ready, NT * p + t)
                    pe.matmul(bank(6), b_inc[:, tok], ar_head[:, t, :], start=True, stop=True).then_inc(s1_mm, 1)
                    if t:
                        pe.wait_ge(across_ready, NT * p + t)
                    pe.matmul(bank(7), k_inc[:, tok], ar_head[:, t, :], start=True, stop=True).then_inc(s2_mm, 1)
                    if t >= 2:
                        pe.wait_ge(tok_ready, NT * p + t - 1)
                    for n, src in enumerate((a_dec, z[:, 8 + p, :], b_end, k_end)):
                        ins = pe.transpose(bank(4 + t % 2)[:, n * P:(n + 1) * P], src[:, tok], ident)
                    ins.then_inc(tok_mm, 1)
                pe.wait_ge(tok_mm, NT * (p + 1))
                pe.sem_inc(unit_in_used, 1)
                pe.wait_ge(tok_ready, NT * (p + 1))
                for s in range(2):
                    pe.wait_ge(tt_init, 2 * p + s + 1)
                    for m in range(4):
                        ins = pe.transpose(bank(4 + s)[:, m * P:(m + 1) * P], t_inv_t[:, 4 * s + m, :], ident)
                    ins.then_inc(tr_mm, 1)
                pe.wait_ge(across_ready, NT * (p + 1))
                for t in range(NT):
                    for h in range(2):
                        n = 2 * t + h
                        ins = pe.matmul(bank(6)[:, n * HD:(n + 1) * HD], across[:, t, 2 * h * P:(2 * h + 1) * P],
                                        v_rows[:, t, h * HD:(h + 1) * HD], start=True, stop=True)
                ins.then_inc(g_mm, 1)
                pe.wait_ge(ga_ready, p + 1)
                pe.wait_ge(q_ready, 2 * p)
                pe.wait_ge(rp_ready, p)
                pe.wait_ge(y0_ready, p)
                for l in range(1, LV + 1):
                    m = LV * p + l - 1
                    for s in range(2):
                        if l >= 2:
                            pe.wait_ge(t_ready, 2 * (m - 1) + s + 1)
                            for n in range(4):
                                ins = pe.transpose(bank(4 + s)[:, n * P:(n + 1) * P], t_inv[:, 4 * s + n, :], ident)
                            ins.then_inc(tr_mm, 1)
                        else:
                            pe.wait_ge(tt_ready, 2 * LV * p + s + 1)
                        pe.wait_ge(mt_ready, 2 * m + s + 1)
                        for n in range(4):
                            ins = pe.matmul(bank(s)[:, n * P:(n + 1) * P], m_level[m % 2][:, 4 * s + n, :], t_inv[:, 4 * s + n, :], start=True, stop=True)
                        ins.then_inc(x_mm, 1)
                    for s in range(2):
                        pe.wait_ge(x_ready, 2 * m + s + 1)
                        if l >= 2:
                            pe.wait_ge(tt_ready, 2 * m + s + 1)
                        for n in range(4):
                            i = 4 * s + n
                            if l < LV:
                                ins = pe.matmul(bank(2 + s)[:, n * P:(n + 1) * P], t_inv_t[:, i, :], m_t[:, i, :], start=True, stop=True)
                            else:
                                ins = pe.matmul(bank(2 + s)[:, n * P:(n + 1) * P], m_t[:, i, :], t_inv_t[:, i, :], start=True, stop=True)
                        ins.then_inc(d_mm, 1)
                        slot(2 * (l - 1) + s, p - 1 if p else None, p + 1 if p + 1 < NP else None)
                for s in range(2):
                    pe.wait_ge(t_ready, 2 * (LV * p + LV - 1) + s + 1)
                    for n in range(4):
                        i = 4 * s + n
                        ins = pe.matmul(bank(s)[:, n * P:(n + 1) * P], t_inv_t[:, i, :], rhs[:, i // 2, i % 2, :], start=True, stop=True)
                    ins.then_inc(w_mm, 1)
                if p:
                    pe.wait_ge(yr_ready, p)
                pe.wait_ge(w_ready, 2 * p + 2)
                for t in range(NT):
                    tok = slice(t * P, (t + 1) * P)
                    for h in range(2):
                        ins = pe.matmul(bank(2)[64 * h:64 * h + 64, tok], wy[:, t, 0, h, :], within[:, t, (2 * h + 1) * P:(2 * h + 2) * P], start=True, stop=True)
                ins.then_inc(rp_mm, 1)
                for t in range(NT):
                    tok = slice(t * P, (t + 1) * P)
                    for x in range(2):
                        for h in range(2):
                            if x == 0:
                                ins = pe.matmul(bank(3)[64 * h:64 * h + 64, tok], wy[:, t, 1, h, :], within[:, t, (2 * h + 1) * P:(2 * h + 2) * P], start=True, stop=False)
                            else:
                                ins = pe.matmul(bank(3)[64 * h:64 * h + 64, tok], v_rows[:, t, h * HD:(h + 1) * HD], across[:, t, (2 * h + 1) * P:(2 * h + 2) * P], start=False, stop=True)
                ins.then_inc(y0_mm, 1)
                for s in range(2):
                    for c in range(4 * s, 4 * s + 4):
                        ins = pe.matmul(bank(4 + s)[:, (c % 4) * P:(c % 4 + 1) * P], wy[:, c // 2, 0, :, :].rearrange("p h d -> p (h d)"),
                                        bk_chunk[:, c // 2, c % 2, 0:P], start=True, stop=True)
                    ins.then_inc(mc_mm, 1)
                for s in range(2):
                    for c in range(4 * s, 4 * s + 4):
                        o = bank(s)[:, (c % 4) * P:(c % 4 + 1) * P]
                        pe.matmul(o, bk_chunk[:, c // 2, c % 2, 0:P], wy[:, c // 2, 1, :, :].rearrange("p h d -> p (h d)"), start=True, stop=False)
                        ins = pe.matmul(o, bk_chunk[:, c // 2, c % 2, P:2 * P], v_rows[:, c // 2, :], start=False, stop=True)
                    ins.then_inc(q_mm, 1)
            def project(o, rows, start):
                t, n = o // 2, o % 2
                for k in rows:
                    src = z[:, 8 + k, :] if k < NP else y_att[:, k - NP, :]
                    ins = pe.matmul(bank(o), src[:, t * P:(t + 1) * P], w_out[:, k, n * 512:(n + 1) * 512],
                                    start=(start and k == rows[0]), stop=(k == NP - 1))
                return ins

            pe.wait_ge(w_out_in[1], 16)
            pe.wait_ge(q_ready, 2 * NP)
            pe.wait_ge(rp_ready, NP)
            pe.wait_ge(y0_ready, NP)
            pe.wait_ge(mc_ready, 2 * NP)
            for k in range(NSLOT):
                if k < 7:
                    project(k, range(NP, 2 * NP), True)
                slot(k, NP - 1, None)
            pe.wait_ge(w_out_in[0], 16)
            pe.wait_ge(yr_ready, NP)
            for o in range(7):
                project(o, range(NP), False).then_inc(op_mm, 1)
            project(7, [4, 5, 6, 7, 0, 1, 2, 3], True).then_inc(op_mm, 1)

            def turn_rows(rows, b0, mm):
                for g in range(2):
                    for k in range(4 * g, 4 * g + 4):
                        ins = pe.transpose(bank(b0 + g)[:, (k % 4) * P:(k % 4 + 1) * P], rows[:, k:k + (P - 1) * KD + 1:KD], ident)
                    ins.then_inc(mm, 1)

            def logits(t):
                pe.wait_ge(nf_ready, t + 1)
                for k in range(KD):
                    ins = pe.matmul(bank(4)[:, t * (NG + NE):(t + 1) * (NG + NE)], n_feat[:, t, k, :], router_w[:, k, :], start=(k == 0), stop=(k == KD - 1))
                return ins

            pe.wait_ge(router_in, 32)
            for t in range(NT):
                pe.wait_ge(h_ready, (4, 2 * NT)[t > 0])
                if t >= 2:
                    pe.wait_ge(nf_ready, t - 1)
                turn_rows(h_res[:, t, :], 2 * (t % 2), nrow_mm)
                if t:
                    logits(t - 1)
            ins = logits(NT - 1)
            ins.then_inc(route_mm, 1)
            pe.wait_ge(routed, CHOICES)
            for t in range(NT):
                for u in range(t + 1):
                    k = K_TRI if u == t else K_ALL1
                    ins = pe.matmul(bank(5)[:, t * NE:(t + 1) * NE], const[:, k:k + P], hot_sum[:, u, :], start=(u == 0), stop=(u == t))
            ins.then_inc(route_mm, 1)
            pe.wait_ge(routed, SLOTS)
            pe.wait_ge(over_counted, 1)
            pe.matmul(bank(5)[:, 0:1], const[:, K_ALL1:K_ALL1 + P], over_rows, start=True, stop=True).then_inc(route_mm, 1)
            pe.wait_ge(ple_in, 64)
            for k in range(KE):
                for t in range(NT):
                    ins = pe.transpose(bank(6 + k)[:, t * P:(t + 1) * P], ple_p[:, t, k:k + (P - 1) * KE + 1:KE], ident)
            ins.then_inc(ple_mm, 1)
            def project_ple(t):
                for n in range(2):
                    if t == 0:
                        pe.wait_ge(ple_t_ready, KE)
                    else:
                        pe.wait_ge(proj_ready, 2 * t + n - 1)
                    for k in range(KE):
                        ins = pe.matmul(bank(6 + n), ple_pt[:, k, t * P:(t + 1) * P], ple_wp[:, k, n * 512:(n + 1) * 512], start=(k == 0), stop=(k == KE - 1))
                    ins.then_inc(proj_mm, 1)

            for t in range(NT):
                project_ple(t)
            pe.wait_ge(routed, OVERFLOWS)
            pe.wait_ge(proj_ready, 2 * NT)

            def expert_rows(s, it, first=False):
                pe.wait_ge(x_slot_in[s], it * 16 + 16)
                if not (first and s == 0):
                    pe.wait_ge(xs_ready, it * 2 + s)
                turn_rows(x_slot[s], 0, xs_mm)

            def expert_pass(it, first=False, last=False):
                for s in range(2):
                    pe.wait_ge(w_exp_in[s], it * 96 + 96)
                    pe.wait_ge(xs_ready, it * 2 + s + 1)
                    if not first:
                        pe.wait_ge(hid_ready, it * 2 + s - 1)
                    for w in range(2):
                        for k in range(KD):
                            for e in range(2):
                                ins = pe.matmul(bank(2 + s)[64 * e:64 * e + 64, w * DE:(w + 1) * DE], x_slot_t[s][:, k, 64 * e:64 * e + 64],
                                                (w1_sb, w3_sb)[w][s][:, e, k, :], start=(k == 0), stop=(k == KD - 1))
                    ins.then_inc(up_mm, 1)
                    if not (last and s == 1):
                        expert_rows(1 - s, it + s)
                    pe.wait_ge(hid_ready, it * 2 + s + 1)
                    for k in range(KE):
                        ins = pe.transpose(bank(4)[:, k * P:(k + 1) * P], hid[s][:, k:k + (P - 1) * KE + 1:KE], ident)
                    ins.then_inc(hid_mm, 1)
                    pe.wait_ge(hidt_ready, it * 2 + s + 1)
                    for n in range(2):
                        if not (first and s == 0):
                            pe.wait_ge((y_lo, y_hi)[n], it * 2 + s)
                        for k in range(KE):
                            for e in range(2):
                                ins = pe.matmul(bank(5 + n)[64 * e:64 * e + 64, :], hid_t[s][:, k, 64 * e:64 * e + 64],
                                                w2_sb[s][:, e, k, n * 512:(n + 1) * 512], start=(k == 0), stop=(k == KE - 1))
                        ins.then_inc(down_mm, 1)
                    pe.wait_ge(down_mm, it * 4 + 2 * s + 2)
                    pe.sem_inc(w_exp_used, 1)

            expert_rows(0, 0, first=True)
            expert_pass(0, first=True)
            with pe.Fori(1, NPAIR // 2 - 1) as it:
                expert_pass(it)
            expert_pass(NPAIR // 2 - 1, last=True)
            with if_over(pe):
                pe.wait_ge(y_lo, NPAIR)
                pe.wait_ge(y_hi, NPAIR)
                pe.wait_ge(over_in_ready, 16)
                for t in range(NT):
                    if t >= 2:
                        pe.wait_ge(over_dve, t - 1)
                    turn_rows(over_in[:, t, :], 2 * (t % 2), over_mm)
                pe.wait_ge(over_dve, NT)
                with pe.Fori(0, NE) as e:
                    for t in range(NT):
                        if t == 0:
                            pe.wait_ge(over_w_in, e * 48 + 48)
                        for w, sb in enumerate((over_w1, over_w3)):
                            for k in range(KD):
                                ins = pe.matmul(bank(2)[:, w * DE:(w + 1) * DE], over_feat[:, t, k, :], sb[:, k, :], start=(k == 0), stop=(k == KD - 1))
                        ins.then_inc(over_mm, 1)
                        pe.wait_ge(over_dve, over_hid(e, t))
                        for k in range(KE):
                            ins = pe.transpose(bank(4)[:, k * P:(k + 1) * P], hid[0][:, k:k + (P - 1) * KE + 1:KE], ident)
                        ins.then_inc(over_mm, 1)
                        pe.wait_ge(over_act, over_hid_t(e, t))
                        for n in range(2):
                            for k in range(KE):
                                ins = pe.matmul(bank(5 + n), hid_t[0][:, k, :], over_w2[:, k, n * 512:(n + 1) * 512], start=(k == 0), stop=(k == KE - 1))
                        ins.then_inc(over_mm, 1)
            def gate_product(t):
                pe.wait_ge(nf_ready, NT + t + 1)
                for n in range(2):
                    if t >= 2:
                        pe.wait_ge(gate_pre, t - 1)
                    for k in range(KD):
                        ins = pe.matmul(bank(4 + 2 * (t % 2) + n), n3_feat[:, t, k, :], gate_w[:, k, n * 512:(n + 1) * 512], start=(k == 0), stop=(k == KD - 1))
                    ins.then_inc(gate_mm, 1)

            for t in range(NT):
                pe.wait_ge(h_ready, 2 * NT + t + 1)
                if t >= 2:
                    pe.wait_ge(nf_ready, NT + t - 1)
                turn_rows(h_res[:, t, :], 2 * (t % 2), nrow_mm)
                if t == 0:
                    pe.wait_ge(gate_w_in, 16)
                    pe.wait_ge(y_lo, NPAIR)
                    pe.wait_ge(y_hi, NPAIR)
                else:
                    gate_product(t - 1)
            gate_product(NT - 1)


def tables(np):
    c = np.zeros((P, K_END), np.float32)
    i = np.arange(P)
    c[:, K_ID:K_ID + P] = np.eye(P)
    c[:, K_ONES:K_ONES + P] = (i[:, None] // HD == i[None] // HD)
    same = i[:, None] // C == i[None] // C
    before = i[:, None] < i[None]
    upto = i[:, None] <= i[None]
    c[:, K_MASK:K_MASK + 2 * P] = np.concatenate([same & before, same & upto], axis=1)
    for l in range(LEVELS):
        b = 1 << l
        m = (i[:, None] // (2 * b) == i[None] // (2 * b)) & (i[:, None] // b < i[None] // b)
        c[:, K_LEVEL + l * P:K_LEVEL + (l + 1) * P] = m
    c[:, K_RESET:K_RESET + T] = (np.arange(T) % C != 0)
    c[:, K_TRI:K_TRI + P] = before
    c[:, K_ALL1:K_ALL1 + P] = 1
    c[:, K_IOTA:K_IOTA + NE] = np.arange(NE)
    c[:, K_TOK:K_TOK + NT] = i[:, None] + P * np.arange(NT)
    return c


def layout(np, v):
    def cols(x):
        return np.asarray(x).reshape(-1, P).T
    vec = np.concatenate([cols(v[n][0]) for n in ("rwkv_mu", "rwkv_w0", "rwkv_a0", "rwkv_k_k", "rwkv_k_a",
                                                  "rwkv_r_k", "rwkv_ln_w", "rwkv_ln_b")]
                         + [np.asarray(v[n][0]).reshape(P, KD) for n in ("norm_mix_w", "norm_ffn_w", "norm_ple_w")], axis=1)
    rel = np.clip(np.arange(P)[:, None] - np.arange(T)[None] + T - P, -(C - 1), 256) + C - 1
    return {
        "const": tables(np), "vec": vec, "x": v["x"][0], "w_in": v["w_in"][0],
        "w_out": v["w_out"][0], "p": v["p"][0, 0],
        "router_w": np.concatenate([v["router_group_w"][0], v["router_expert_w"][0]], axis=1),
        "router_b": np.concatenate([v["router_group_b"], v["router_expert_b"]], axis=1),
        "w1": np.asarray(v["expert_w1"][0]).reshape(NE, D, DE), "w3": np.asarray(v["expert_w3"][0]).reshape(NE, D, DE),
        "w2e": np.asarray(v["expert_w2"][0]).reshape(NE, DE, D),
        "gate_w": v["ple_gate_w"][0], "gate_b": v["ple_gate_b"], "ple_wp": v["ple_proj_w"][0], "final_w": np.asarray(v["final_norm_w"])[None],
        "w2": v["rwkv_w2"][0], "a2": v["rwkv_a2"][0], "g2": v["rwkv_g2"][0],
        "bias": np.asarray(v["att_rel_bias"][0])[:, rel],
    }


def kernel(**inputs):
    import numpy as np
    import concourse.bacc as bacc
    from concourse.bass_utils import run_bass_kernel_spmd

    nc = bacc.Bacc("TRN2", target_bir_lowering=False, num_devices=1)
    arrays = {f"{name}_in": np.ascontiguousarray(x) for name, x in layout(np, inputs).items()}
    aps = {name[:-3]: nc.dram_tensor(name, x.shape, mybir.dt.from_np(x.dtype), kind="ExternalInput").ap()
           for name, x in arrays.items()}
    out = nc.dram_tensor("out", (T, D), F32, kind="ExternalOutput").ap()
    hybrid_trunk(nc, aps, out)
    r = run_bass_kernel_spmd(nc, [arrays], core_ids=[0])
    return r.results[0]["out"].reshape(1, T, D)
```

```python
import math
from contextlib import ExitStack

import concourse.bass as bass
from concourse import mybir

F32 = mybir.dt.float32
F32R = mybir.dt.float32r
U32 = mybir.dt.uint32
ALU = mybir.AluOpType
ACT = mybir.ActivationFunctionType
AX = mybir.AxisListType

P = 128
T = 512
NT = T // P
D = 1024
KD = D // P
DR = 512
NP = DR // P
NH = 8
HD = 64
C = 64
NC = T // C
N_RWKV = 3 * DR + 256
N_IN = N_RWKV + 3 * DR
SLAB = 256
RING = 2
NE = 32
NG = 4
EPG = 8
DE = 256
CAP = 64
KE = DE // P
NPAIR = NE // 2
PLE = 256
RMS_EPS = 1e-6
GN_EPS = 64e-5
DECAY_SCALE = 0.6065306597126334
NEG = -1e30
NO_ROW = 1 << 16
NORM_SCALE_LOG2 = 20

K_ID, K_ONES, K_MASK, K_LEVEL = 0, 128, 256, 512
LEVELS = 6
K_RESET = K_LEVEL + LEVELS * 128
K_TRI = K_RESET + T
K_ALL1 = K_TRI + 128
K_IOTA = K_ALL1 + 128
K_TOK = K_IOTA + P
K_END = K_TOK + NT

V_MU, V_W0, V_A0, V_KK, V_KA, V_RK, V_LNW, V_LNB = 0, 14, 18, 22, 26, 30, 34, 38
V_MIX, V_FFN, V_PLE = 42, 50, 58
V_END = 66


def hybrid_trunk(nc, a, out):
    with ExitStack() as ctx:
        def sem(name):
            return ctx.enter_context(nc.semaphore(name))

        arena, parts = [], {}
        for start, end in ((0, 48), (48, 104), (104, 120), (120, 136), (136, 152), (152, 207.8125)):
            words = int((end - start) * 256)
            if start not in (48, 152):
                with nc.sbuf_tensor(f"parts_{start}", [P, words], F32R) as parts[start]:
                    pass
            arena.append((start, ctx.enter_context(nc.sbuf_tensor(f"arena_{start}", [P, words], F32))))
        low_parts, high_parts = parts[0], parts[120]
        psum = ctx.enter_context(nc.psum_tensor("psum", [P, 8, 512], F32))

        def at(kib, n):
            base, part = [x for x in arena if x[0] <= kib][-1]
            first = int((kib - base) * 256)
            return part[:, first:first + n]

        def grid(kib, *dims):
            n = 1
            for d in dims:
                n *= d
            names = "abcd"[:len(dims)]
            spec = "p (" + " ".join(names) + ") -> p " + " ".join(names)
            return at(kib, n).rearrange(spec, **dict(zip(names[1:], dims[1:])))

        def bank(b):
            return psum[:, b, :]

        const = at(48, K_END)
        vec = at(48 + K_END / 256, V_END)
        small = at(48 + (K_END + V_END) / 256, 3072 - K_END - V_END)
        ident = const[:, K_ID:K_ID + P]
        head_ones = const[:, K_ONES:K_ONES + P]
        mask_2h = const[:, K_MASK:K_MASK + 2 * P].unsqueeze(1).to_broadcast([P, 2, 2 * P])
        z = grid(60, 14, T)
        q_head = grid(88, NH, T)
        k_pair = grid(104, NP, T)
        v_tok = grid(112, NT, DR)
        h_hi = low_parts[:, 0:KD * T].rearrange("p (k t) -> p k t", k=KD)
        h_lo = high_parts[:, 0:KD * T].rearrange("p (k t) -> p k t", k=KD)
        slab_hi, slab_lo = (low_parts[:, (1 + i) * KD * T:(2 + i) * KD * T].rearrange("p (r k n) -> p r k n", r=2, k=KD) for i in range(2))
        slabs = grid(136, RING, KD, SLAB)
        x_in_sb = grid(160, NT, D)
        x_norm = grid(176, NT, D)
        PROBS = 6
        LAG = 3
        prob = grid(136, PROBS, T)
        PT_W = 10 * P
        prob_t = grid(8, 2, 2, PT_W)
        bias_w = grid(152, 4, T)
        y_att = grid(196, NP, T)
        shift_buf = [grid(204, 520)[:, 0:T + 1], grid(192, 520)[:, 0:T + 1]]

        within = grid(88, NT, 4 * P)
        across = grid(96, NT, 4 * P)
        m_level = [grid(104, 8, P), grid(108, 8, P)]
        t_inv = grid(112, 8, P)
        t_inv_t = grid(116, 8, P)
        m_t = grid(120, 8, P)
        bk_chunk = grid(124, NT, 2, 2 * P)
        v_rows = grid(136, NT, P)
        rhs = grid(132, NT, 2, P)
        wy = grid(138, NT, 2, 2, HD)
        step_mat = grid(142, NC, P)
        step_add = grid(146, NC, P)
        r_eff = grid(150, T)
        y_buf = grid(152, T)
        state = grid(154, NC, P)
        r_dec = [grid(178, T), grid(158, T)]
        ar_head = grid(160, NT, 4 * P)
        a_dec = grid(168, T)
        b_inc = grid(170, T)
        k_inc = grid(172, T)
        b_end = grid(174, T)
        k_end = grid(176, T)
        sgw = grid(180, T)
        iclr = grid(182, T)
        cum = grid(184, T)
        cum_x = grid(186, T)
        dec = grid(188, T)
        cum_e = grid(190, T)
        kkn = grid(192, T)
        knorm = grid(194, T)
        k_mod = grid(204, T)
        lora_w = [grid(152, 3, DR), grid(0, 3, DR)]
        h_res = grid(88, NT, D)
        w_out = grid(160, KD, D)
        n_rows = grid(60, NT, D)
        n_feat = grid(160, NT, KD, P)
        router_w = grid(204, KD, NG + NE)
        router_b = grid(205.25, NG + NE)
        table = at(80, 2048)
        used = [0]

        def col(n, *dims, dtype=None):
            ap = table[:, used[0]:used[0] + n]
            used[0] += n
            if dtype is not None:
                ap = ap.bitcast(dtype)
            if dims:
                names = "abcd"[:len(dims)]
                ap = ap.rearrange("p (" + " ".join(names) + ") -> p " + " ".join(names), **dict(zip(names[1:], dims[1:])))
            return ap

        e_logit = col(NT * NE, NT, NG, EPG)
        g_logit = col(NT * 8, NT, 8)
        g_top = col(NT * 8, NT, 8)
        g_idx = col(NT * 8, NT, 8, dtype=U32)
        g_sel = col(NT)
        g_exp = col(NT * NG, NT, NG)
        g_sum = col(NT)
        p_group = col(NT)
        g_hot = col(NT * NG, NT, NG)
        e_mask = col(NT * NE, NT, EPG, NG)
        sel = col(NT * 8, NT, 8)
        e_top = col(NT * 8, NT, 8)
        e_idx = col(NT * 8, NT, 8, dtype=U32)
        e_loc = col(NT * 2, NT, 2)
        e_ratio = col(NT)
        weight = col(NT * 2, NT, 2)
        expert = col(NT * 2, NT, 2)
        hot = [col(NT * NE, NT, NE), col(NT * NE, NT, NE)]
        hot_sum = col(NT * NE, NT, NE)
        hot_before = col((NT - 1) * NE, NT - 1, NE)
        hot_pos = col(NT * NE, NT, NE)
        hot_pos2 = col(NT * NE, NT, NE)
        pos = col(NT * 2, NT, 2)
        fits = col(NT * 2, NT, 2)
        w_main = col(NT * 2, NT, 2)
        over_u = col(1, dtype=U32)
        over_rows = col(1)
        w_col = col(NT)
        slot_dest = col(NPAIR, dtype=U32)
        slot_tok_f = col(NPAIR)
        upper = col(NT * 2, NT, 2)
        pass_no = col(NT * 2, NT, 2)
        slot_no = col(NT * 2, NT, 2)
        beyond = col(NT * 2, NT, 2)
        row_no = col(NT * 2, NT, 2)
        row_in_pass = [col(NT * NPAIR, NT, NPAIR) for _ in range(2)]
        slot_hot = grid(76, 2, NT, P)
        slot_second = col(NPAIR)
        slot_tok = col(NPAIR, dtype=U32)
        tok_now = [col(1, dtype=U32), col(1, dtype=U32)]
        dest_now = [col(1, dtype=U32), col(1, dtype=U32)]

        w1_sb = [grid(b, 2, KD, DE) for b in (0, 104)]
        w3_sb = [grid(b + 16, 2, KD, DE) for b in (0, 104)]
        w2_sb = [grid(b + 32, 2, KE, D) for b in (0, 104)]
        x_slot = [grid(152, D), grid(156, D)]
        x_slot_t = [grid(160, KD, P), grid(164, KD, P)]
        y_slot = [grid(168, D), grid(172, D)]
        hid = [grid(176, DE), grid(177, DE)]
        hid_t = [grid(178, KE, P), grid(179, KE, P)]
        y_tok = grid(152, NT, 2, D)

        over_feat = grid(136, NT, KD, P)
        over_in = grid(32, NT, D)
        over_w1 = grid(104, KD, DE)
        over_w3 = grid(112, KD, DE)
        over_w2 = grid(120, KE, D)
        w_over = hot_pos
        assert used[0] <= 2048

        ple_wp = grid(180, KE, D)
        ple_p = grid(188, NT, PLE)
        ple_pt = grid(192, KE, T)
        gate_b = grid(196, D)
        final_w = grid(200, D)
        gate_w = grid(0, KD, D)
        ple_proj = grid(60, NT, D)
        gate_lo = low_parts[:, 0:KD * D].rearrange("p (k n) -> p k n", k=KD)
        gate_hi = [x.rearrange("p (k n) -> p k n", k=KD // 2) for x in (low_parts[:, KD * D:3 * KD * D // 2], high_parts[:, 0:KD * D // 2])]
        n3_hi, n3_lo = (parts[i][:, 0:NT * D].rearrange("p (t k n) -> p t k n", t=NT, k=KD) for i in (104, 136))
        gate = [grid(184, D), grid(188, D)]
        out_rows = [grid(192, D), grid(76, D)]

        norm_rows = nc.dram_tensor("norm_rows", (T, D), F32, kind="Internal").ap()
        y_rows = nc.dram_tensor("y_rows", (2 * T, D), F32, kind="Internal").ap()

        d_end = [small[:, 128:136], small[:, 136:144]]
        ss = small[:, 0:4]
        ms = small[:, 4:8]
        rs = small[:, 8:12]
        one_mu = small[:, 12:26]
        ss2, rs2 = small[:, 144:148], small[:, 148:152]
        ss3, rs3 = small[:, 152:156], small[:, 156:160]
        ss4, rs4 = small[:, 160:164], small[:, 164:168]
        rms_eps = small[:, 26:27]
        gn_eps = small[:, 27:28]
        norm_bias = small[:, 28:29]
        nmax = small[:, 32:64]
        psumrow = small[:, 64:96]
        prow_inv = small[:, 96:128]

        consts_in = sem("consts_in")
        x_in = [sem(f"x_in{t}") for t in range(NT)]
        root_ready = sem("root_ready")
        rs2_ready = sem("rs2_ready")
        eps_ready = sem("eps_ready")
        dve_step = sem("dve_step")
        act_step = sem("act_step")
        pool_step = sem("pool_step")
        xn_ready = sem("xn_ready")
        xt_mm = sem("xt_mm")
        hf_hi = sem("hf_hi")
        hf_lo = sem("hf_lo")
        slab_in = [sem(f"slab_in{i}") for i in range(RING)]
        slab_hi_ready = sem("slab_hi_ready")
        slab_lo_ready = sem("slab_lo_ready")
        z_mm = sem("z_mm")
        z_shift = sem("z_shift")
        z_act = sem("z_act")
        z_dve = sem("z_dve")
        zeros_ready = sem("zeros_ready")
        bias_in = [sem(f"bias_in{i}") for i in range(4)]
        bias_masked = sem("bias_masked")
        att_s_mm = sem("att_s_mm")
        att_s_read = sem("att_s_read")
        att_max = sem("att_max")
        att_exp = sem("att_exp")
        att_inv = sem("att_inv")
        att_p = sem("att_p")
        att_tr = sem("att_tr")
        att_pt = sem("att_pt")
        att_pv = sem("att_pv")
        att_y = sem("att_y")
        lora_in = sem("lora_in")
        w_out_in = [sem("w_out_in0"), sem("w_out_in1")]
        res_in = sem("res_in")
        op_mm = sem("op_mm")
        h_ready = sem("h_ready")
        nrow_mm = sem("nrow_mm")
        nf_ready = sem("nf_ready")
        rows_out = sem("rows_out")
        router_in = sem("router_in")
        route_mm = sem("route_mm")
        routed = sem("routed")
        GROUP_DIFF, EXPERT_DIFF, CHOICES, SLOTS, OVERFLOWS = 1, 2, 3, 4, 5
        route_exp = sem("route_exp")
        slot_tok_ready = sem("slot_tok_ready")
        tok_now_ready = sem("tok_now_ready")
        dest_now_ready = sem("dest_now_ready")
        gather_go = sem("gather_go")
        x_slot_in = [sem(f"x_slot_in{i}") for i in range(2)]
        w13_in = [sem(f"w13_in{i}") for i in range(2)]
        w2e_in = [sem(f"w2e_in{i}") for i in range(2)]
        xs_mm = sem("xs_mm")
        xs_ready = sem("xs_ready")
        up_mm = sem("up_mm")
        silu_ready = sem("silu_ready")
        hid_ready = sem("hid_ready")
        hid_mm = sem("hid_mm")
        hidt_ready = sem("hidt_ready")
        down_mm = sem("down_mm")
        y_lo = sem("y_lo")
        y_hi = sem("y_hi")
        y_out = [sem(f"y_out{i}") for i in range(2)]
        y_tok_in = [sem(f"y_tok_in{i}") for i in range(NT)]
        ple_in = sem("ple_in")
        ple_mm = sem("ple_mm")
        ple_ready = sem("ple_ready")
        gate_w_in = sem("gate_w_in")
        gw_hi_ready = sem("gw_hi_ready")
        gw_lo_ready = sem("gw_lo_ready")
        gw_lo2_ready = sem("gw_lo2_ready")
        n3_scaled = sem("n3_scaled")
        n3_hi_ready = sem("n3_hi_ready")
        gate_mm = sem("gate_mm")
        gate_pre = sem("gate_pre")
        gate_ready = sem("gate_ready")
        out_ready = sem("out_ready")
        over_counted = sem("over_counted")
        over_in_ready = sem("over_in_ready")
        y_cleared = sem("y_cleared")
        over_w_in = sem("over_w_in")
        over_mm = sem("over_mm")
        over_act = sem("over_act")
        over_dve = sem("over_dve")
        out_stored = [sem("out_stored0"), sem("out_stored1")]
        lo_ready = sem("lo_ready")
        prep_mm = sem("prep_mm")
        sg_ready = sem("sg_ready")
        aa_ready = sem("aa_ready")
        ksq_ready = sem("ksq_ready")
        cum_ready = sem("cum_ready")
        cum_split = sem("cum_split")
        decay_ready = sem("decay_ready")
        ksum_ready = sem("ksum_ready")
        kn_ready = sem("kn_ready")
        rk_ready = sem("rk_ready")
        rt_ready = sem("rt_ready")
        at_ready = sem("at_ready")
        prep_out = sem("prep_out")
        bonus_ready = sem("bonus_ready")
        g_ready = sem("g_ready")
        ar_ready = sem("ar_ready")
        unit_in_used = sem("unit_in_used")
        s1_mm = sem("s1_mm")
        s2_mm = sem("s2_mm")
        within_ready = sem("within_ready")
        across_ready = sem("across_ready")
        tok_mm = sem("tok_mm")
        tok_ready = sem("tok_ready")
        tt_init = sem("tt_init")
        mt_ready = sem("mt_ready")
        x_mm = sem("x_mm")
        x_ready = sem("x_ready")
        d_mm = sem("d_mm")
        t_ready = sem("t_ready")
        tr_mm = sem("tr_mm")
        tt_ready = sem("tt_ready")
        g_mm = sem("g_mm")
        ga_ready = sem("ga_ready")
        w_mm = sem("w_mm")
        w_ready = sem("w_ready")
        rp_mm = sem("rp_mm")
        rp_ready = sem("rp_ready")
        y0_mm = sem("y0_mm")
        y0_ready = sem("y0_ready")
        mc_mm = sem("mc_mm")
        mc_ready = sem("mc_ready")
        q_mm = sem("q_mm")
        q_ready = sem("q_ready")
        seq_mm = sem("seq_mm")
        s_ready = sem("s_ready")
        y_mm = sem("y_mm")
        y_ready = sem("y_ready")
        stat_mm = sem("stat_mm")
        yc_ready = sem("yc_ready")
        ysq_ready = sem("ysq_ready")
        rstd_ready = sem("rstd_ready")
        yr_ready = sem("yr_ready")
        rwkv_zero = sem("rwkv_zero")

        slab_order = [6, 2, 3, 0, 1, 4, 5, 7, 8, 9, 10, 11, 12]
        jobs = []
        for n, s in enumerate(slab_order):
            if s < 11:
                jobs += [(n, "feat", 2 * s), (n, "feat", 2 * s + 1)]
            else:
                jobs += [(n, "tok", (s - 11, t)) for t in range(NT)]
        NJ = len(jobs)
        PREP_JOB = 14
        last_job = {n: j for j, (n, _, _) in enumerate(jobs)}

        first_job = {n: min(j for j, job in enumerate(jobs) if job[0] == n) for n in range(len(slab_order))}

        def units():
            return [(h, i) for h in range(NH) for i in range(NT)]

        def pt_col(i, j):
            return (i * (i + 1) // 2 + j) * P

        def z_reader(j):
            _, kind, what = jobs[j]
            return "act" if kind == "feat" and what >= 18 else "dve"

        def z_count(j, reader):
            return sum(z_reader(i) == reader for i in range(j + 1))

        def z_done(eng, j):
            r = z_reader(j)
            eng.wait_ge({"act": z_act, "dve": z_dve}[r], z_count(j, r))

        def over_up(e, t):
            return e * (3 * NT) + (2 * NT + 3 * t + 1)

        def over_turned(e, t):
            return e * (3 * NT) + (2 * NT + 3 * t + 2)

        def over_down(e, t):
            return e * (3 * NT) + (2 * NT + 3 * t + 3)

        def over_col(e):
            return e * (2 * NT + 1) + (NT + 1)

        def over_hid(e, t):
            return e * (2 * NT + 1) + (NT + 2 * t + 2)

        def over_silu(e, t):
            return e * (2 * NT) + (2 * t + 1)

        def over_hid_t(e, t):
            return e * (2 * NT) + (2 * t + 2)

        PLE_STEPS = (range(0, 3), range(3, 6), range(6, KE + 2 * NT))

        def if_over(eng):
            eng.wait_ge(routed, OVERFLOWS)
            return eng.If(eng.value_load(over_u[0:1, 0:1], min_val=0, max_val=2 * T) > 0)

        def one_of(src, pair, i):
            return src[bass.ds(pair + i * NPAIR, 1), :, :].rearrange("o p f -> (o p) f")

        w_in_v = a["w_in"].rearrange("(p k) n -> p k n", k=KD)

        LV = LEVELS - 1
        NSLOT = 2 * LV
        PREP_STEPS = (0, 1, 2, 3, None, 4, 5, 6, 7, 8)

        def level_mask(l):
            return const[:, K_LEVEL + l * P:K_LEVEL + (l + 1) * P]

        def mats(m):
            return lambda s: m[:, 4 * s:4 * s + 4, :]

        def n_of(s):
            return within.rearrange("p n (h x t) -> p n h x t", h=2, x=2)[:, 2 * s:2 * s + 2, :, 0, :]

        def heads4(ap):
            return ap.rearrange("p (n h) t -> p n h t", h=2)

        def over(ap):
            return ap.unsqueeze(1).unsqueeze(1).to_broadcast([P, 2, 2, P])

        block = ctx.enter_context(nc.Block())

        @block.sync
        def _(sp):
            sp.dma_start(vec, a["vec"]).then_inc(consts_in, 16)
            for t in range(NT):
                sp.dma_start(x_in_sb[:, t, :], a["x"][t * P:(t + 1) * P, :]).then_inc(x_in[t], 16)
            sp.dma_start(const, a["const"]).then_inc(consts_in, 16)

            def lora_loads(w):
                sp.dma_start(w[0:64, 0, :], a["w2"]).then_inc(lora_in, 16)
                sp.dma_start(w[64:128, 1, :], a["a2"]).then_inc(lora_in, 16)
                sp.dma_start(w[:, 2, :], a["g2"]).then_inc(lora_in, 16)

            for n, s in enumerate(slab_order):
                if n >= RING:
                    sp.wait_ge(slab_lo_ready, n - RING + 1)
                sp.dma_start(slabs[:, n % RING], w_in_v[:, :, s * SLAB:(s + 1) * SLAB]).then_inc(slab_in[n % RING], 16)
                if n == 1:
                    lora_loads(lora_w[0])

            def bias_load(h):
                sp.dma_start(bias_w[:, h % 4, :], a["bias"][h]).then_inc(bias_in[h % 4], 16)

            sp.wait_ge(prep_mm, 5)
            for h in range(4):
                bias_load(h)
            sp.wait_ge(z_mm, NJ)
            lora_loads(lora_w[1])
            for h in range(4, NH):
                sp.wait_ge(att_s_read, 4 * (h - 4) + 4)
                bias_load(h)

            w_out_v = a["w_out"].rearrange("(k p) n -> p k n", p=P)
            sp.wait_ge(unit_in_used, NP)
            sp.wait_ge(prep_out, NP)
            sp.dma_start(w_out[:, 0:4, :], w_out_v[:, 0:4, :]).then_inc(w_out_in[0], 16)
            sp.wait_ge(rp_ready, NP)
            sp.dma_start(w_out[:, 4:8, :], w_out_v[:, 4:8, :]).then_inc(w_out_in[1], 16)
            sp.dma_start(router_w, a["router_w"].rearrange("(p k) n -> p k n", k=KD)).then_inc(router_in, 16)
            sp.dma_start(router_b, a["router_b"].to_broadcast([P, NG + NE])).then_inc(router_in, 16)
            sp.wait_ge(y0_mm, NP)
            sp.dma_start(h_res, a["x"].rearrange("(n p) d -> p n d", p=P)).then_inc(res_in, 16)

            def expert_loads(s, pair, matrices=("w1", "w3", "w2e")):
                for w in matrices:
                    sb, rows = {"w1": (w1_sb, KD), "w3": (w3_sb, KD), "w2e": (w2_sb, KE)}[w]
                    for i in range(2):
                        src = a[w].rearrange("e (p k) f -> e p (k f)", k=rows)
                        sp.dma_start(sb[s][:, i].rearrange("p k f -> p (k f)"), one_of(src, pair, i)).then_inc((w2e_in if w == "w2e" else w13_in)[s], 16)

            sp.wait_ge(prep_mm, 5 * NP)
            expert_loads(0, 0)
            sp.wait_ge(yr_ready, NP)
            expert_loads(1, 1)
            for t in range(NT):
                sp.wait_ge(xn_ready, NT + t + 1)
                sp.dma_start(norm_rows[t * P:(t + 1) * P, :], n_rows[:, t, :]).then_inc(rows_out, 16)
            sp.wait_ge(op_mm, 2 * NT)
            sp.dma_start(ple_wp, a["ple_wp"].rearrange("(p k) n -> p k n", k=KE)).then_inc(ple_in, 16)
            sp.dma_start(ple_p, a["p"].rearrange("(n p) f -> p n f", p=P)).then_inc(ple_in, 16)
            sp.dma_start(gate_b, a["gate_b"].to_broadcast([P, D])).then_inc(ple_in, 16)
            sp.dma_start(final_w, a["final_w"].to_broadcast([P, D])).then_inc(ple_in, 16)

            def expert_pass(it, last=False):
                for s in range(2):
                    if not last:
                        sp.wait_ge(up_mm, it * 2 + s + 1)
                        expert_loads(s, it * 2 + 2 + s, ("w1", "w3"))
                        sp.wait_ge(down_mm, it * 4 + 2 * s + 2)
                        expert_loads(s, it * 2 + 2 + s, ("w2e",))
                    elif s == 0:
                        sp.wait_ge(down_mm, 2 * NPAIR - 2)
                        sp.dma_start(gate_w, a["gate_w"].rearrange("(p k) n -> p k n", k=KD)).then_inc(gate_w_in, 16)

            with sp.Fori(0, NPAIR // 2 - 1) as it:
                expert_pass(it)
            expert_pass(NPAIR // 2 - 1, last=True)
            with if_over(sp):
                sp.wait_ge(down_mm, 2 * NPAIR)
                sp.dma_start(over_in, norm_rows.rearrange("(n p) d -> p n d", p=P)).then_inc(over_in_ready, 16)
                with sp.Fori(0, NE) as e:
                    sp.wait_ge(over_mm, e * (3 * NT) + 2 * NT)
                    for w, dst, rows in (("w1", over_w1, KD), ("w3", over_w3, KD), ("w2e", over_w2, KE)):
                        src = a[w].rearrange("e (p k) f -> e p (k f)", k=rows)
                        sp.dma_start(dst.rearrange("p k f -> p (k f)"), one_of(src, e, 0)).then_inc(over_w_in, 16)
                sp.wait_ge(over_dve, over_col(NE - 1) + 2 * NT)
            sp.wait_ge(down_mm, 2 * NPAIR)
            for s in range(2):
                sp.wait_ge(y_out[s], 16 * (NPAIR // 2))
            for t in range(NT):
                for x in range(2):
                    sp.dma_start(y_tok[:, t, x, :], y_rows[x * T + t * P:x * T + (t + 1) * P, :]).then_inc(y_tok_in[t], 16)
            for t in range(NT):
                sp.wait_ge(out_ready, t + 1)
                sp.dma_start(out[t * P:(t + 1) * P, :], out_rows[t % 2]).then_inc(out_stored[t % 2], 16)
            for b in out_stored:
                sp.wait_ge(b, 16 * NT // 2)

        @block.gpsimd
        def _(pool):
            steps = [0]

            def chain(ins):
                steps[0] += 1
                ins.then_inc(pool_step, 1)
                pool.wait_ge(pool_step, steps[0])

            def copy(out, in_):
                return pool.tensor_scalar(out, in_, 1.0, 1.0, ALU.mult, ALU.mult)

            pool.memset(lora_w[0][64:128, 0, :], 0.0).then_inc(zeros_ready, 1)
            pool.wait_ge(zeros_ready, 1)
            pool.memset(lora_w[0][0:64, 1, :], 0.0).then_inc(zeros_ready, 1)
            pool.wait_ge(zeros_ready, 2)
            for n, b in enumerate(shift_buf):
                pool.memset(b[:, 0:1], 0.0).then_inc(zeros_ready, 1)
                pool.wait_ge(zeros_ready, n + 3)
            for h in range(NH):
                other = 64 * (1 - h % 2)
                pool.memset(q_head[other:other + 64, h, :], 0.0).then_inc(zeros_ready, 1)
                pool.wait_ge(zeros_ready, h + 5)
            def slot(k, prep):
                if prep is None:
                    return
                if k == 1:
                    pool.wait_ge(cum_ready, prep + 1)
                    pool.wait_ge(prep_out, prep)
                    pool.tensor_tensor(cum_x, cum, sgw, ALU.subtract).then_inc(cum_split, 1)
                    pool.wait_ge(cum_split, 2 * prep + 1)
                    ends = cum.rearrange("p (c t) -> p c t", t=C)[:, :, C - 1:C].to_broadcast([P, NC, C])
                    pool.tensor_tensor(cum_e.rearrange("p (c t) -> p c t", t=C), ends, cum.rearrange("p (c t) -> p c t", t=C),
                                       ALU.subtract).then_inc(cum_split, 1)
                    pool.wait_ge(cum_split, 2 * prep + 2)
                if k == NSLOT - 1:
                    pool.wait_ge(unit_in_used, prep)
                    pool.wait_ge(rt_ready, prep + 1)
                    pool.wait_ge(at_ready, prep + 1)
                    for x, src in enumerate((a_dec, r_dec[prep % 2])):
                        for h in range(2):
                            rows = slice(64 * h, 64 * h + 64)
                            copy(ar_head[rows, :, (2 * h + x) * P:(2 * h + x + 1) * P],
                                 src[rows, :].rearrange("p (n t) -> p n t", t=P)).then_inc(ar_ready, 1)
                            pool.wait_ge(ar_ready, 4 * prep + 2 * x + h + 1)

            pool.wait_ge(xn_ready, NT)
            chain(pool.memset(ar_head, 0.0))
            for k in range(NSLOT):
                slot(k, 0)
            def mask(h):
                pool.wait_ge(bias_in[h % 4], 16 * (h // 4 + 1))
                pool.memset(bias_w[0:64, h % 4, T - 64:T], NEG).then_inc(bias_masked, 1)
                pool.wait_ge(bias_masked, h + 1)

            for h in range(4):
                mask(h)
            pool.wait_ge(z_mm, NJ)
            chain(pool.memset(lora_w[1][64:128, 0, :], 0.0))
            pool.memset(lora_w[1][0:64, 1, :], 0.0).then_inc(zeros_ready, 1)
            pool.wait_ge(zeros_ready, 5 + NH)
            chain(pool.memset(bk_chunk, 0.0))
            for u in range(4 * NH):
                h, i = units()[u]
                n = P * (i + 1)
                pool.wait_ge(att_inv, u + 1)
                pool.tensor_scalar(prob[:, u % PROBS, 0:n], prob[:, u % PROBS, 0:n], prow_inv[:, u:u + 1], 1.0, ALU.mult, ALU.mult).then_inc(att_p, 1)
                pool.wait_ge(att_p, u + 1)
                if i == 0 and 2 <= h < NH - 2:
                    mask(h + 2)
            pool.wait_ge(att_s_read, 4 * NH)
            pool.memset(state, 0.0).then_inc(rwkv_zero, 1)
            pool.wait_ge(rwkv_zero, 1)

            for p in range(NP):
                pool.wait_ge(within_ready, NT * (p + 1))
                for l in range(1, LV + 1):
                    m = LV * p + l - 1
                    for s in range(2):
                        if m >= 2:
                            pool.wait_ge(x_mm, 2 * (m - 2) + s + 1)
                        pool.tensor_tensor(heads4(mats(m_level[m % 2])(s)), n_of(s), over(level_mask(l)), ALU.mult).then_inc(mt_ready, 1)
                        pool.wait_ge(mt_ready, 2 * m + s + 1)
                    if l >= 2:
                        for k in (2 * l - 4, 2 * l - 3):
                            slot(k, p + 1 if p + 1 < NP else None)
                for k in (NSLOT - 2, NSLOT - 1):
                    slot(k, p + 1 if p + 1 < NP else None)

            pool.wait_ge(yr_ready, NP)
            for s in range(2):
                chain(pool.memset(x_slot[s], 0.0))
            pool.wait_ge(rs2_ready, 1)
            pool.wait_ge(h_ready, 2 * NT)
            for t in range(NT):
                pool.tensor_scalar(n_rows[:, t, :], h_res[:, t, :], rs2[:, t:t + 1], 1.0, ALU.mult, ALU.mult).then_inc(xn_ready, 1)
                pool.wait_ge(xn_ready, NT + t + 1)
            with if_over(pool):
                pool.dma_start(y_rows.rearrange("(n p) d -> p n d", p=P), x_slot[0].unsqueeze(1).to_broadcast([P, 2 * NT, D])).then_inc(y_cleared, 16)
                pool.wait_ge(y_cleared, 16)
            pool.wait_ge(slot_tok_ready, 1)
            pool.wait_ge(rows_out, 16 * NT)

            def gather(s, it):
                pool.tensor_copy(tok_now[s], slot_tok[:, bass.ds(it * 2 + s, 1)]).then_inc(tok_now_ready, 1)
                pool.wait_ge(tok_now_ready, it * 2 + s + 1)
                pool.sem_inc(gather_go, 1)
                pool.indirect_dma_start(x_slot[s], None, norm_rows, bass.IndirectOffsetOnAxis(ap=tok_now[s], axis=0),
                                        bounds_check=T - 1, oob_is_err=False).then_inc(x_slot_in[s], 16)

            def scatter(s, it, first=False):
                if not first:
                    pool.wait_ge(y_out[s], it * 16)
                pool.tensor_copy(dest_now[s], slot_dest[:, bass.ds(it * 2 + s, 1)]).then_inc(dest_now_ready, 1)
                pool.wait_ge(dest_now_ready, it * 2 + s + 1)
                pool.wait_ge(y_lo, it * 2 + s + 1)
                pool.wait_ge(y_hi, it * 2 + s + 1)
                pool.sem_inc(gather_go, 1)
                pool.indirect_dma_start(y_rows, bass.IndirectOffsetOnAxis(ap=dest_now[s], axis=0), y_slot[s], None,
                                        bounds_check=2 * T - 1, oob_is_err=False).then_inc(y_out[s], 16)

            for s in range(2):
                gather(s, 0)

            def expert_pass(it, first=False):
                for s in range(2):
                    pool.wait_ge(xs_mm, it * 4 + 2 * s + 2)
                    gather(s, it + 1)
                    scatter(s, it, first)

            expert_pass(0, first=True)
            with pool.Fori(1, NPAIR // 2 - 1) as it:
                expert_pass(it)
            for s in range(2):
                scatter(s, NPAIR // 2 - 1)
            for q in range(KD // 4, KD // 2):
                rows = slice(2 * q % (KD // 2), 2 * q % (KD // 2) + 2)
                pool.wait_ge(gw_hi_ready, q + 1)
                ins = pool.tensor_tensor(gate_lo[:, 2 * q:2 * q + 2, :], gate_w[:, 2 * q:2 * q + 2, :], gate_hi[q // 2][:, rows, :].bitcast(F32), ALU.subtract)
                ins.then_inc(gw_lo2_ready, 1)
                pool.wait_ge(gw_lo2_ready, q - KD // 4 + 1)

        @block.scalar
        def _(act):
            steps = [0]

            def chain(ins):
                steps[0] += 1
                ins.then_inc(act_step, 1)
                act.wait_ge(act_step, steps[0])

            act.wait_ge(eps_ready, 1)
            for t in range(NT):
                act.wait_ge(x_in[t], 16)
                ins = act.activation(x_norm[:, t, :], x_in_sb[:, t, :], ACT.Square, accum_out=ss[:, t:t + 1])
            chain(ins)
            act.activation(ms, ss, ACT.Sqrt, scale=1.0 / D, bias=rms_eps).then_inc(root_ready, 1)

            def slot(k, seq, prep):
                if prep is not None:
                    q = prep
                    step = PREP_STEPS[k]
                    w0, a0, kk = (vec[:, v + q:v + q + 1] for v in (V_W0, V_A0, V_KK))
                    if step == 0:
                        act.wait_ge(prep_out, q)
                        act.wait_ge(prep_mm, 5 * q + 1)
                        act.activation(sgw, bank(6), ACT.Sigmoid, bias=w0).then_inc(sg_ready, 1)
                        act.activation(knorm, z[:, 4 + q, :], ACT.Square, scale=kk).then_inc(ksq_ready, 1)
                    if step == 1:
                        act.wait_ge(prep_mm, 5 * q + 2)
                        act.activation(iclr, bank(6), ACT.Sigmoid, bias=a0).then_inc(aa_ready, 1)
                    if step == 3:
                        act.wait_ge(cum_split, 2 * q + 2)
                        act.activation(dec, cum, ACT.Exp, scale=-DECAY_SCALE).then_inc(decay_ready, 1)
                        act.activation(cum_x, cum_x, ACT.Exp, scale=-DECAY_SCALE).then_inc(decay_ready, 1)
                        act.activation(cum, cum, ACT.Exp, scale=DECAY_SCALE).then_inc(decay_ready, 1)
                        act.activation(cum_e, cum_e, ACT.Exp, scale=-DECAY_SCALE).then_inc(decay_ready, 1)
                    if step == 4:
                        act.wait_ge(ksum_ready, q + 1)
                        chain(act.activation(knorm, knorm, ACT.Ln))
                        act.activation(knorm, knorm, ACT.Exp, scale=-0.5, bias=norm_bias).then_inc(kn_ready, 1)
                    if step == 5:
                        act.wait_ge(rk_ready, q + 1)
                        act.wait_ge(rt_ready, q + 1)
                        act.wait_ge(prep_mm, 5 * q + 5)
                        act.activation(z[:, q, :], bank(6), ACT.Copy).then_inc(g_ready, 1)
                if seq is not None:
                    if k == 7:
                        act.wait_ge(yc_ready, seq + 1)
                        act.activation(r_eff, y_buf, ACT.Square).then_inc(ysq_ready, 1)
                    if k == 8:
                        act.wait_ge(stat_mm, 2 * seq + 2)
                        chain(act.activation(r_eff, bank(7), ACT.Ln, scale=1.0 / HD, bias=gn_eps))
                        act.activation(r_eff, r_eff, ACT.Exp, scale=-0.5).then_inc(rstd_ready, 1)

            def split_hi(n):
                act.wait_ge(slab_in[n % RING], 16 * (n // RING + 1))
                if n >= 2:
                    act.wait_ge(z_mm, last_job[n - 2] + 1)
                act.activation(slab_hi[:, n % 2], slabs[:, n % RING], ACT.Copy).then_inc(slab_hi_ready, 1)

            split_hi(0)
            for k in range(KD):
                act.wait_ge(xt_mm, k + 1)
                act.activation(h_hi[:, k, :], bank(k), ACT.Copy, scale=vec[:, V_MIX + k:V_MIX + k + 1]).then_inc(hf_hi, 1)
            split_hi(1)
            for j, (n, kind, what) in enumerate(jobs):
                if kind == "feat" and what < 14:
                    act.wait_ge(z_mm, j + 1)
                    if j >= 2:
                        z_done(act, j - 2)
                    act.activation(shift_buf[j % 2][:, 1:T + 1], bank(2 + j % 2), ACT.Copy,
                                   scale=vec[:, V_MU + what:V_MU + what + 1]).then_inc(z_shift, 1)
                    if j == 1:
                        z_done(act, 1)
                        act.activation(z[0:64, 12, :], z[0:64, 12, :], ACT.Tanh).then_inc(lo_ready, 1)
                        act.activation(z[:, 13, :], z[:, 13, :], ACT.Sigmoid).then_inc(lo_ready, 1)
                elif z_reader(j) == "act":
                    act.wait_ge(z_mm, j + 1)
                    act.activation(k_pair[:, what - 18, :], bank(2 + j % 2), ACT.Copy).then_inc(z_act, 1)
                if first_job[n] == j and 2 <= n + 1 < len(slab_order):
                    split_hi(n + 1)
                if j == PREP_JOB:
                    z_done(act, j - 1)
                if 0 <= j - PREP_JOB < NSLOT:
                    slot(j - PREP_JOB, None, 0)

            def exp(u):
                h, i = units()[u]
                n = P * (i + 1)
                act.wait_ge(att_max, u + 1)
                act.activation(prob[:, u % PROBS, 0:n], prob[:, u % PROBS, 0:n], ACT.Exp, bias=nmax[:, u:u + 1],
                               accum_out=psumrow[:, u:u + 1]).then_inc(att_exp, 1)

            def evac_t(u):
                h, i = units()[u]
                if u % 8 == 0 and u >= 16:
                    act.wait_ge(att_pv, u // 8 - 1)
                act.wait_ge(att_tr, u + 1)
                act.activation(prob_t[:, (h // 2) % 2, h % 2, pt_col(i, 0):pt_col(i, i) + P], bank(6 + u % 2)[:, 0:P * (i + 1)], ACT.Copy).then_inc(att_pt, 1)

            def evac_y(pr):
                act.wait_ge(att_pv, pr + 1)
                act.activation(y_att[:, pr, :], bank(2 + pr % 2), ACT.Copy).then_inc(att_y, 1)

            for step in range(4 * NH + LAG + 4):
                if step < 4 * NH:
                    exp(step)
                if LAG <= step < 4 * NH + LAG:
                    evac_t(step - LAG)
                if step >= LAG + 10 and (step - LAG - 10) % 8 == 0:
                    evac_y((step - LAG - 10) // 8)

            act.wait_ge(rwkv_zero, 1)
            for p in range(NP):
                for t in range(NT):
                    act.wait_ge(tok_mm, NT * p + t + 1)
                    b = bank(4 + t % 2)
                    act.activation(rhs[:, t, :, 0:HD], b[:, 0:P].rearrange("p (h d) -> p h d", h=2), ACT.Copy)
                    act.activation(v_rows[:, t, :], b[:, P:2 * P], ACT.Copy)
                    act.activation(bk_chunk[0:64, t, 0, :], b[0:64, 2 * P:4 * P], ACT.Copy)
                    act.activation(bk_chunk[64:128, t, 1, :], b[64:128, 2 * P:4 * P], ACT.Copy).then_inc(tok_ready, 1)
                for s in range(2):
                    if s == 1:
                        act.wait_ge(g_mm, p + 1)
                        act.activation(rhs[:, :, :, HD:P], bank(6).rearrange("p (n h d) -> p n h d", n=NT, h=2), ACT.Copy).then_inc(ga_ready, 1)
                    act.wait_ge(tr_mm, 2 * LV * p + s + 1)
                    act.activation(mats(t_inv)(s), bank(4 + s).rearrange("p (m t) -> p m t", t=P), ACT.Copy).then_inc(tt_ready, 1)
                for l in range(1, LV + 1):
                    m = LV * p + l - 1
                    for s in range(2):
                        if l >= 2:
                            act.wait_ge(tr_mm, 2 * m + s + 1)
                            act.activation(mats(t_inv_t)(s), bank(4 + s).rearrange("p (m t) -> p m t", t=P), ACT.Copy).then_inc(tt_ready, 1)
                        act.wait_ge(x_mm, 2 * m + s + 1)
                        act.activation(mats(m_t)(s), bank(s).rearrange("p (m t) -> p m t", t=P), ACT.Copy).then_inc(x_ready, 1)
                    for s in range(2):
                        slot(2 * (l - 1) + s, p - 1 if p else None, p + 1 if p + 1 < NP else None)
                for s in range(2):
                    act.wait_ge(w_mm, 2 * p + s + 1)
                    for t in (2 * s, 2 * s + 1):
                        ins = act.activation(wy[:, t, :, :, :].rearrange("p x h d -> p h x d"),
                                             bank(s)[:, (t % 2) * 2 * P:(t % 2 + 1) * 2 * P].rearrange("p (h x d) -> p h x d", h=2, x=2), ACT.Copy)
                    ins.then_inc(w_ready, 1)
                act.wait_ge(yr_ready, p)
                act.wait_ge(y0_mm, p + 1)
                act.activation(y_buf, bank(3), ACT.Copy).then_inc(y0_ready, 1)
                act.wait_ge(s_ready, 7 * p)
                for s in range(2):
                    act.wait_ge(q_mm, 2 * p + s + 1)
                    act.activation(step_add[:, 4 * s:4 * s + 4, :], bank(s).rearrange("p (c i) -> p c i", i=P), ACT.Copy).then_inc(q_ready, 1)
            for k in range(NSLOT):
                slot(k, NP - 1, None)

            def square_sum(t, rows, junk, ssq):
                return act.activation(junk, rows, ACT.Square, accum_out=ssq[:, t:t + 1])

            def root(ssq):
                act.activation(ssq, ssq, ACT.Sqrt, scale=1.0 / D, bias=rms_eps).then_inc(root_ready, 1)

            for t in range(NT):
                act.wait_ge(h_ready, 2 * t + 2)
                ins = square_sum(t, h_res[:, t, :], n_rows[:, t, :], ss2)
            chain(ins)
            root(ss2)
            act.wait_ge(routed, GROUP_DIFF)
            act.activation(g_exp, g_exp, ACT.Exp).then_inc(route_exp, 1)
            act.wait_ge(routed, EXPERT_DIFF)
            act.activation(e_ratio, e_ratio, ACT.Exp).then_inc(route_exp, 1)
            act.wait_ge(rows_out, 16 * NT)
            act.wait_ge(nrow_mm, 2 * NT)

            def ple(steps):
                for m in steps:
                    t, n = divmod(m - KE, 2)
                    dst = ple_pt[:, m, :] if m < KE else ple_proj[:, t, n * 512:(n + 1) * 512]
                    act.wait_ge(ple_mm, m + 1)
                    act.activation(dst, bank(7), ACT.Copy).then_inc(ple_ready, 1)

            ple(PLE_STEPS[0])

            def expert_pass(it, first=False):
                for s in range(2):
                    act.wait_ge(up_mm, it * 2 + s + 1)
                    act.activation(hid[s], bank(2 + s)[:, 0:DE], ACT.Silu).then_inc(silu_ready, 1)
                    act.wait_ge(hid_mm, it * 2 + s + 1)
                    act.activation(hid_t[s], bank(4)[:, 0:2 * P].rearrange("p (k t) -> p k t", k=KE), ACT.Copy).then_inc(hidt_ready, 1)
                    act.wait_ge(down_mm, it * 4 + 2 * s + 1)
                    if not first:
                        act.wait_ge(y_out[s], it * 16)
                    act.activation(y_slot[s][:, 0:512], bank(5), ACT.Copy).then_inc(y_lo, 1)
                    if first:
                        ple(PLE_STEPS[1 + s])

            expert_pass(0, first=True)
            with act.Fori(1, NPAIR // 2) as it:
                expert_pass(it)
            with if_over(act):
                with act.Fori(0, NE) as e:
                    for t in range(NT):
                        act.wait_ge(over_mm, over_up(e, t))
                        act.activation(hid[0], bank(2)[:, 0:DE], ACT.Silu).then_inc(over_act, 1)
                        act.wait_ge(over_mm, over_turned(e, t))
                        act.activation(hid_t[0], bank(4)[:, 0:2 * P].rearrange("p (k t) -> p k t", k=KE), ACT.Copy).then_inc(over_act, 1)
                act.wait_ge(over_dve, over_col(NE - 1) + 2 * NT)
            act.wait_ge(gate_w_in, 16)
            for q in range(KD // 2):
                rows = slice(2 * q % (KD // 2), 2 * q % (KD // 2) + 2)
                act.activation(gate_hi[q // 2][:, rows, :], gate_w[:, 2 * q:2 * q + 2, :], ACT.Copy).then_inc(gw_hi_ready, 1)
            for t in range(NT):
                act.wait_ge(h_ready, 2 * NT + t + 1)
                ins = square_sum(t, h_res[:, t, :], y_tok[:, t, 0, :], ss3)
                act.wait_ge(n3_scaled, t + 1)
                act.activation(n3_hi[:, t].rearrange("p k n -> p (k n)"), y_tok[:, t, 1, :], ACT.Copy).then_inc(n3_hi_ready, 1)
            chain(ins)
            root(ss3)
            for t in range(NT):
                act.wait_ge(gate_pre, t + 1)
                act.activation(gate[t % 2], gate[t % 2], ACT.Sigmoid).then_inc(gate_ready, 1)
                act.wait_ge(h_ready, 3 * NT + t + 1)
                if t >= 2:
                    act.wait_ge(out_stored[t % 2], 16 * (t // 2))
                chain(square_sum(t, h_res[:, t, :], out_rows[t % 2], ss4))
                root(ss4[:, t:t + 1])

        @block.vector
        def _(dve):
            steps = [0]

            def chain(ins):
                steps[0] += 1
                ins.then_inc(dve_step, 1)
                dve.wait_ge(dve_step, steps[0])

            dve.memset(gn_eps, GN_EPS)
            dve.memset(norm_bias, 0.5 * NORM_SCALE_LOG2 * math.log(2.0))
            dve.memset(rms_eps, RMS_EPS).then_inc(eps_ready, 1)
            dve.wait_ge(consts_in, 32)
            dve.tensor_scalar(one_mu, vec[:, V_MU:V_MU + 14], -1.0, 1.0, ALU.mult, ALU.add)
            for t in range(NT):
                if t == 0:
                    dve.wait_ge(root_ready, 1)
                    chain(dve.reciprocal(rs, ms))
                dve.tensor_scalar(x_norm[:, t, :], x_in_sb[:, t, :], rs[:, t:t + 1], None, ALU.mult).then_inc(xn_ready, 1)

            def slot(k, seq, prep):
                if seq is not None:
                    q = seq
                    if k < 7:
                        if k == 0:
                            dve.wait_ge(q_ready, 2 * q + 2)
                        else:
                            dve.wait_ge(seq_mm, 6 * q + k)
                        for h in range(2):
                            rows, d = slice(64 * h, 64 * h + 64), slice(64 * h, 64 * h + 64)
                            if k == 0:
                                ins = dve.tensor_copy(state[rows, 1, d], step_add[rows, 0, d])
                            else:
                                ins = dve.tensor_tensor(state[rows, k + 1, d], bank(7)[rows, 64 * h + P * (k % 4):64 * h + P * (k % 4) + 64],
                                                        step_add[rows, k, d], ALU.add)
                        ins.then_inc(s_ready, 1)
                    if k == 7:
                        dve.wait_ge(y_mm, q + 1)
                        dve.wait_ge(y0_ready, q + 1)
                        dve.tensor_tensor(y_buf[:, C:T], bank(7)[:, C:T], y_buf[:, C:T], ALU.add).then_inc(y_ready, 1)
                        dve.wait_ge(y_ready, q + 1)
                        dve.wait_ge(stat_mm, 2 * q + 1)
                        dve.scalar_tensor_tensor(out=y_buf, in0=bank(7), scalar=-1.0 / HD, in1=y_buf, op0=ALU.mult, op1=ALU.add).then_inc(yc_ready, 1)
                        dve.wait_ge(yc_ready, q + 1)
                    if k == 9:
                        dve.wait_ge(rstd_ready, q + 1)
                        chain(dve.scalar_tensor_tensor(out=y_buf, in0=y_buf, scalar=vec[:, V_LNW + q:V_LNW + q + 1], in1=r_eff, op0=ALU.mult, op1=ALU.mult))
                        chain(dve.scalar_tensor_tensor(out=y_buf, in0=y_buf, scalar=vec[:, V_LNB + q:V_LNB + q + 1], in1=z[:, 4 + q, :], op0=ALU.add, op1=ALU.add))
                        dve.wait_ge(g_ready, q + 1)
                        dve.tensor_tensor(z[:, 8 + q, :], y_buf, z[:, q, :], ALU.mult).then_inc(yr_ready, 1)
                if prep is not None:
                    q = prep
                    step = PREP_STEPS[k]
                    r, kq, v = z[:, q, :], z[:, 4 + q, :], z[:, 8 + q, :]
                    if step == 0:
                        chain(dve.tensor_scalar(kkn, kq, vec[:, V_KK + q:V_KK + q + 1], None, ALU.mult))
                        dve.wait_ge(sg_ready, q + 1)
                        dve.tensor_tensor_scan(cum, const[:, K_RESET:K_RESET + T], sgw, 0.0, ALU.mult, ALU.add).then_inc(cum_ready, 1)
                    if step == 2:
                        dve.wait_ge(prep_mm, 5 * q + 3)
                        dve.tensor_scalar(knorm, bank(6), 1e-24, 2.0 ** NORM_SCALE_LOG2, ALU.max, ALU.mult).then_inc(ksum_ready, 1)
                        dve.wait_ge(aa_ready, q + 1)
                        chain(dve.tensor_scalar(k_mod, iclr, -1.0, vec[:, V_KA + q:V_KA + q + 1], ALU.add, ALU.mult))
                        chain(dve.scalar_tensor_tensor(out=k_mod, in0=k_mod, scalar=1.0, in1=kq, op0=ALU.add, op1=ALU.mult))
                    if step == 3:
                        dve.wait_ge(cum_split, 2 * q + 2)
                        dve.scalar_tensor_tensor(out=sgw, in0=r, scalar=vec[:, V_RK + q:V_RK + q + 1], in1=k_mod, op0=ALU.mult, op1=ALU.mult).then_inc(rk_ready, 1)
                    if step == 4:
                        dve.wait_ge(decay_ready, 4 * q + 1)
                        dve.tensor_copy(d_end[q % 2], dec[:, C - 1::C])
                        dve.tensor_tensor(r_dec[q % 2], r, dec, ALU.mult).then_inc(rt_ready, 1)
                        dve.wait_ge(prep_mm, 5 * q + 4)
                        dve.tensor_tensor(kq, bank(6), v, ALU.mult).then_inc(bonus_ready, 1)
                    if step == 5:
                        dve.wait_ge(kn_ready, q + 1)
                        chain(dve.tensor_tensor(kkn, kkn, knorm, ALU.mult))
                        dve.wait_ge(unit_in_used, q)
                        dve.wait_ge(ar_ready, 4 * q)
                        dve.wait_ge(decay_ready, 4 * q + 2)
                        dve.scalar_tensor_tensor(out=a_dec, in0=kkn, scalar=-1.0, in1=cum_x, op0=ALU.mult, op1=ALU.mult).then_inc(at_ready, 1)
                        chain(dve.tensor_tensor(knorm, kkn, iclr, ALU.mult))
                    if step == 6:
                        dve.wait_ge(decay_ready, 4 * q + 4)
                        dve.tensor_tensor(b_inc, knorm, cum, ALU.mult)
                        dve.tensor_tensor(k_inc, k_mod, cum, ALU.mult)
                    if step == 7:
                        dve.tensor_tensor(b_end, knorm, cum_e, ALU.mult)
                        dve.tensor_tensor(k_end, k_mod, cum_e, ALU.mult).then_inc(prep_out, 1)

            def split_lo(n):
                dve.wait_ge(slab_hi_ready, n + 1)
                dve.tensor_tensor(slab_lo[:, n % 2], slabs[:, n % RING], slab_hi[:, n % 2].bitcast(F32), ALU.subtract).then_inc(slab_lo_ready, 1)

            split_lo(0)
            for k in range(KD):
                dve.wait_ge(hf_hi, k + 1)
                dve.scalar_tensor_tensor(out=h_lo[:, k, :], in0=bank(k), scalar=vec[:, V_MIX + k:V_MIX + k + 1],
                                         in1=h_hi[:, k, :].bitcast(F32), op0=ALU.mult, op1=ALU.subtract).then_inc(hf_lo, 1)
            dve.wait_ge(zeros_ready, 4 + NH)
            for j, (n, kind, what) in enumerate(jobs):
                if first_job[n] == j and n + 1 < len(slab_order):
                    split_lo(n + 1)
                zb = bank(2 + j % 2)
                if z_reader(j) == "dve":
                    dve.wait_ge(z_mm, j + 1)
                if z_reader(j) != "dve":
                    pass
                elif kind == "tok":
                    half, t = what
                    dve.tensor_copy(v_tok[:, t, half * SLAB:(half + 1) * SLAB], zb[:, 0:SLAB]).then_inc(z_dve, 1)
                elif what < 14:
                    dve.wait_ge(z_shift, j + 1)
                    dve.scalar_tensor_tensor(out=z[:, what, :], in0=zb, scalar=one_mu[:, what:what + 1],
                                             in1=shift_buf[j % 2][:, 0:T], op0=ALU.mult, op1=ALU.add).then_inc(z_dve, 1)
                else:
                    h = 2 * (what - 14)
                    dve.tensor_scalar(q_head[0:64, h, :], zb[0:64, :], HD ** -0.5, None, ALU.mult)
                    dve.tensor_scalar(q_head[64:128, h + 1, :], zb[64:128, :], HD ** -0.5, None, ALU.mult).then_inc(z_dve, 1)
                if j == PREP_JOB:
                    z_done(dve, j - 1)
                if 0 <= j - PREP_JOB < NSLOT:
                    slot(j - PREP_JOB, None, 0)

            def scores(u):
                h, i = units()[u]
                n = P * (i + 1)
                dve.wait_ge(att_s_mm, u + 1)
                if i == 0:
                    dve.wait_ge(bias_masked, h + 1)
                if u >= PROBS:
                    dve.wait_ge(att_tr, u - PROBS + 1)
                dve.tensor_tensor(prob[:, u % PROBS, 0:n], bank(4 + u % 2)[:, 0:n], bias_w[:, h % 4, T - n:T], ALU.add).then_inc(att_s_read, 1)
                dve.wait_ge(att_s_read, u + 1)
                dve.tensor_reduce(nmax[:, u:u + 1], prob[:, u % PROBS, 0:n], AX.X, ALU.max, negate=True).then_inc(att_max, 1)

            def invert(u):
                dve.wait_ge(att_exp, u + 1)
                dve.reciprocal(prow_inv[:, u:u + 1], psumrow[:, u:u + 1]).then_inc(att_inv, 1)

            for step in range(4 * NH + 1):
                if step < 4 * NH:
                    scores(step)
                if step >= 1:
                    invert(step - 1)

            dve.wait_ge(rwkv_zero, 1)
            for p in range(NP):
                for t in range(NT):
                    dve.wait_ge(s1_mm, NT * p + t + 1)
                    dve.tensor_tensor(within[:, t, :].rearrange("p (h n) -> p h n", h=2), bank(6).rearrange("p (h n) -> p h n", h=2), mask_2h, ALU.mult).then_inc(within_ready, 1)
                    dve.wait_ge(s2_mm, NT * p + t + 1)
                    dve.tensor_tensor(across[:, t, :].rearrange("p (h n) -> p h n", h=2), bank(7).rearrange("p (h n) -> p h n", h=2), mask_2h, ALU.mult).then_inc(across_ready, 1)
                    if t % 2 == 0:
                        continue
                    s = t // 2
                    dve.wait_ge(within_ready, NT * p + t + 1)
                    chain(dve.tensor_tensor(heads4(mats(t_inv_t)(s)), n_of(s), over(level_mask(0)), ALU.mult))
                    dve.tensor_tensor(heads4(mats(t_inv_t)(s)), heads4(mats(t_inv_t)(s)), over(ident), ALU.add).then_inc(tt_init, 1)
                for l in range(1, LV + 1):
                    m = LV * p + l - 1
                    for s in range(2):
                        dve.wait_ge(d_mm, 2 * m + s + 1)
                        dst = mats(t_inv if l < LV else t_inv_t)(s)
                        dve.tensor_tensor(dst, bank(2 + s).rearrange("p (m t) -> p m t", t=P), dst, ALU.add).then_inc(t_ready, 1)
                        slot(2 * (l - 1) + s, p - 1 if p else None, p + 1 if p + 1 < NP else None)
                dve.wait_ge(rp_mm, p + 1)
                dve.tensor_tensor(r_eff, bank(2), r_dec[p % 2], ALU.add).then_inc(rp_ready, 1)
                for s in range(2):
                    dve.wait_ge(mc_mm, 2 * p + s + 1)
                    for c in range(4 * s, 4 * s + 4):
                        ins = dve.scalar_tensor_tensor(out=step_mat[:, c, :], in0=ident, scalar=d_end[p % 2][:, c:c + 1],
                                                       in1=bank(4 + s)[:, (c % 4) * P:(c % 4 + 1) * P], op0=ALU.mult, op1=ALU.add)
                    ins.then_inc(mc_ready, 1)
            for k in range(NSLOT):
                slot(k, NP - 1, None)

            dve.wait_ge(res_in, 16)
            for o in range(2 * NT):
                t, n = o // 2, o % 2
                dve.wait_ge(op_mm, o + 1)
                dve.tensor_tensor(h_res[:, t, n * 512:(n + 1) * 512], bank(o), h_res[:, t, n * 512:(n + 1) * 512], ALU.add).then_inc(h_ready, 1)

            def turn_rows(t, n_t, b0, mm, mm_at, w, ready):
                for g in range(2):
                    dve.wait_ge(mm, mm_at + g)
                    scale = vec[:, w + 4 * g:w + 4 * g + 4].unsqueeze(2).to_broadcast([P, 4, P])
                    ins = dve.tensor_tensor(n_t[:, 4 * g:4 * g + 4, :], bank(b0 + g).rearrange("p (k t) -> p k t", k=4), scale, ALU.mult)
                ins.then_inc(ready, 1)

            for t in range(NT):
                turn_rows(t, n_feat[:, t], 2 * (t % 2), nrow_mm, 2 * t + 1, V_FFN, nf_ready)
            dve.wait_ge(root_ready, 2)
            dve.reciprocal(rs2, ss2).then_inc(rs2_ready, 1)
            dve.wait_ge(rs2_ready, 1)
            dve.wait_ge(router_in, 32)
            dve.memset(g_logit[:, :, NG:8], NEG)
            for x in range(2):
                dve.tensor_scalar(row_no[:, :, x], const[:, K_TOK:K_TOK + NT], float(x * T - NO_ROW), None, ALU.add)
            dve.wait_ge(route_mm, 1)
            lg = bank(4)[:, 0:NT * (NG + NE)].rearrange("p (n e) -> p n e", n=NT)
            bias = router_b.unsqueeze(1).to_broadcast([P, NT, NG + NE])
            scale = rs2.unsqueeze(2).to_broadcast([P, NT, NG + NE])
            e_rows = e_logit.rearrange("p n g e -> p n (g e)")
            dve.tensor_tensor(g_logit[:, :, 0:NG], lg[:, :, 0:NG], scale[:, :, 0:NG], ALU.mult)
            chain(dve.tensor_tensor(e_rows, lg[:, :, NG:], scale[:, :, NG:], ALU.mult))
            dve.tensor_tensor(g_logit[:, :, 0:NG], g_logit[:, :, 0:NG], bias[:, :, 0:NG], ALU.add)
            chain(dve.tensor_tensor(e_rows, e_rows, bias[:, :, NG:], ALU.add))
            for t in range(NT):
                ins = dve.max(g_top[:, t, :], g_logit[:, t, :])
            chain(ins)
            for t in range(NT):
                ins = dve.max_index(g_idx[:, t, :], g_top[:, t, :], g_logit[:, t, :])
            chain(ins)
            dve.tensor_copy(g_sel.unsqueeze(2), g_idx[:, :, 0:1])
            dve.tensor_tensor(g_exp, g_logit[:, :, 0:NG], g_top[:, :, 0:1].to_broadcast([P, NT, NG]), ALU.subtract).then_inc(routed, 1)
            dve.wait_ge(routed, GROUP_DIFF)
            iota = const[:, K_IOTA:K_IOTA + NE].unsqueeze(1)
            chain(dve.tensor_tensor(g_hot, iota[:, :, 0:NG].to_broadcast([P, NT, NG]), g_sel.unsqueeze(2).to_broadcast([P, NT, NG]), ALU.is_equal))
            chain(dve.tensor_tensor(e_mask.rearrange("p n e g -> p n g e"), e_logit, g_hot.unsqueeze(3).to_broadcast([P, NT, NG, EPG]), ALU.mult))
            chain(dve.tensor_reduce(sel, e_mask, AX.X, ALU.add))
            for t in range(NT):
                ins = dve.max(e_top[:, t, :], sel[:, t, :])
            chain(ins)
            for t in range(NT):
                ins = dve.max_index(e_idx[:, t, :], e_top[:, t, :], sel[:, t, :])
            chain(ins)
            dve.tensor_tensor(e_ratio.unsqueeze(2), e_top[:, :, 1:2], e_top[:, :, 0:1], ALU.subtract).then_inc(routed, 1)
            chain(dve.tensor_copy(e_loc, e_idx[:, :, 0:2]))
            chain(dve.scalar_tensor_tensor(out=expert, in0=g_sel.unsqueeze(2).to_broadcast([P, NT, 2]), scalar=float(EPG), in1=e_loc, op0=ALU.mult, op1=ALU.add))
            for x in range(2):
                chain(dve.tensor_tensor(hot[x], iota.to_broadcast([P, NT, NE]), expert[:, :, x:x + 1].to_broadcast([P, NT, NE]), ALU.is_equal))
            chain(dve.tensor_tensor(hot_sum, hot[0], hot[1], ALU.add))
            dve.tensor_copy(hot_before[:, 0, :], hot_sum[:, 0, :])
            chain(dve.tensor_tensor(hot_before[:, 1, :], hot_sum[:, 0, :], hot_sum[:, 1, :], ALU.add))
            dve.tensor_tensor(hot_before[:, 2, :], hot_before[:, 1, :], hot_sum[:, 2, :], ALU.add).then_inc(routed, 1)
            chain(dve.tensor_scalar(upper, expert, float(NPAIR), None, ALU.is_ge))
            chain(dve.scalar_tensor_tensor(out=pass_no, in0=upper, scalar=-float(NPAIR), in1=expert, op0=ALU.mult, op1=ALU.add))
            for x in range(2):
                chain(dve.tensor_tensor(row_in_pass[x], iota[:, :, 0:NPAIR].to_broadcast([P, NT, NPAIR]), pass_no[:, :, x:x + 1].to_broadcast([P, NT, NPAIR]), ALU.is_equal))
                chain(dve.tensor_tensor(row_in_pass[x], row_in_pass[x], row_no[:, :, x:x + 1].to_broadcast([P, NT, NPAIR]), ALU.mult))
            dve.wait_ge(route_mm, 2)
            rank = bank(5)[:, 0:NT * NE].rearrange("p (n e) -> p n e", n=NT)
            for x in range(2):
                ins = dve.tensor_tensor((hot_pos, hot_pos2)[x], rank, hot[x], ALU.mult)
            chain(ins)
            for x in range(2):
                ins = dve.tensor_reduce(pos[:, :, x:x + 1].rearrange("p n o -> p (n o)"), (hot_pos, hot_pos2)[x], AX.X, ALU.add)
            chain(ins)
            dve.tensor_scalar(beyond, pos, float(CAP), float(4 * P), ALU.is_ge, ALU.mult)
            dve.tensor_scalar(fits, pos, float(CAP), None, ALU.is_lt)
            chain(dve.scalar_tensor_tensor(out=slot_no, in0=upper, scalar=float(CAP), in1=pos, op0=ALU.mult, op1=ALU.add))
            chain(dve.tensor_tensor(slot_no, slot_no, beyond, ALU.add))
            slots = const[:, K_IOTA:K_IOTA + P].unsqueeze(1).to_broadcast([P, NT, P])
            for x in range(2):
                ins = dve.tensor_tensor(slot_hot[:, x], slots, slot_no[:, :, x:x + 1].to_broadcast([P, NT, P]), ALU.is_equal)
            ins.then_inc(routed, 1)
            dve.wait_ge(route_exp, 1)
            chain(dve.tensor_reduce(g_sum, g_exp, AX.X, ALU.add))
            chain(dve.reciprocal(p_group, g_sum))
            dve.wait_ge(route_exp, 2)
            chain(dve.tensor_scalar(g_sum, e_ratio, 1.0, None, ALU.add))
            chain(dve.reciprocal(g_sum, g_sum))
            chain(dve.tensor_tensor(weight[:, :, 0:1], p_group.unsqueeze(2), g_sum.unsqueeze(2), ALU.mult))
            chain(dve.tensor_tensor(weight[:, :, 1:2], weight[:, :, 0:1], e_ratio.unsqueeze(2), ALU.mult))
            chain(dve.tensor_tensor(w_main, weight, fits, ALU.mult))
            chain(dve.tensor_scalar(fits, fits, -1.0, 1.0, ALU.mult, ALU.add))
            chain(dve.tensor_reduce(over_rows, fits, AX.XY, ALU.add))
            dve.tensor_tensor(pos, weight, fits, ALU.mult).then_inc(over_counted, 1)
            dve.wait_ge(route_mm, 3)
            chain(dve.tensor_scalar(slot_tok_f, bank(4)[:, 0:NPAIR], float(NO_ROW), None, ALU.add))
            dve.tensor_copy(slot_dest, slot_tok_f)
            chain(dve.tensor_scalar(slot_second, slot_tok_f, float(T), float(T), ALU.is_ge, ALU.mult))
            dve.tensor_tensor(slot_tok, slot_tok_f, slot_second, ALU.subtract).then_inc(slot_tok_ready, 1)
            dve.wait_ge(over_counted, 1)
            for x in range(2):
                chain(dve.tensor_tensor(hot[x], hot[x], pos[:, :, x:x + 1].to_broadcast([P, NT, NE]), ALU.mult))
            dve.tensor_tensor(w_over, hot[0], hot[1], ALU.add)
            dve.wait_ge(route_mm, 4)
            dve.tensor_copy(over_u, bank(5)[:, 0:1]).then_inc(routed, 1)

            def expert_rows(s, it):
                for g in range(2):
                    dve.wait_ge(xs_mm, it * 4 + 2 * s + 1 + g)
                    scale = vec[:, V_FFN + 4 * g:V_FFN + 4 * g + 4].unsqueeze(2).to_broadcast([P, 4, P])
                    ins = dve.tensor_tensor(x_slot_t[s][:, 4 * g:4 * g + 4, :], bank(g).rearrange("p (k t) -> p k t", k=4), scale, ALU.mult)
                ins.then_inc(xs_ready, 1)

            def expert_pass(it, last=False):
                for s in range(2):
                    dve.wait_ge(silu_ready, it * 2 + s + 1)
                    dve.tensor_tensor(hid[s], bank(2 + s)[:, DE:2 * DE], hid[s], ALU.mult).then_inc(hid_ready, 1)
                    if not (last and s == 1):
                        expert_rows(1 - s, it + s)
                    dve.wait_ge(down_mm, it * 4 + 2 * s + 2)
                    dve.wait_ge(y_lo, it * 2 + s + 1)
                    dve.tensor_copy(y_slot[s][:, 512:D], bank(6)).then_inc(y_hi, 1)

            expert_rows(0, 0)
            with dve.Fori(0, NPAIR // 2 - 1) as it:
                expert_pass(it)
            expert_pass(NPAIR // 2 - 1, last=True)
            with if_over(dve):
                scale = vec[:, V_FFN:V_FFN + KD].unsqueeze(2).to_broadcast([P, KD, P])
                for t in range(NT):
                    for g in range(2):
                        dve.wait_ge(over_mm, 2 * t + 1 + g)
                        ins = dve.tensor_tensor(over_feat[:, t, 4 * g:4 * g + 4, :], bank(2 * (t % 2) + g).rearrange("p (k t) -> p k t", k=4),
                                                scale[:, 4 * g:4 * g + 4, :], ALU.mult)
                    ins.then_inc(over_dve, 1)
                with dve.Fori(0, NE) as e:
                    dve.wait_ge(over_dve, over_col(e) - 1)
                    dve.tensor_copy(w_col.unsqueeze(2), w_over[:, :, bass.ds(e, 1)]).then_inc(over_dve, 1)
                    dve.wait_ge(over_dve, over_col(e))
                    for t in range(NT):
                        dve.wait_ge(over_act, over_silu(e, t))
                        dve.tensor_tensor(hid[0], bank(2)[:, DE:2 * DE], hid[0], ALU.mult).then_inc(over_dve, 1)
                        dve.wait_ge(over_mm, over_down(e, t))
                        for n in range(2):
                            half = slice(n * 512, (n + 1) * 512)
                            ins = dve.scalar_tensor_tensor(out=h_res[:, t, half], in0=bank(5 + n), scalar=w_col[:, t:t + 1],
                                                           in1=h_res[:, t, half], op0=ALU.mult, op1=ALU.add)
                        ins.then_inc(over_dve, 1)
                dve.wait_ge(over_dve, over_col(NE - 1) + 2 * NT)
            for q in range(KD // 4):
                rows = slice(2 * q % (KD // 2), 2 * q % (KD // 2) + 2)
                dve.wait_ge(gw_hi_ready, q + 1)
                dve.tensor_tensor(gate_lo[:, 2 * q:2 * q + 2, :], gate_w[:, 2 * q:2 * q + 2, :], gate_hi[q // 2][:, rows, :].bitcast(F32), ALU.subtract).then_inc(gw_lo_ready, 1)

            def lower(t):
                dve.wait_ge(n3_hi_ready, t + 1)
                dve.tensor_tensor(n3_lo[:, t].rearrange("p k n -> p (k n)"), y_tok[:, t, 1, :], n3_hi[:, t].rearrange("p k n -> p (k n)").bitcast(F32), ALU.subtract).then_inc(nf_ready, 1)

            for t in range(NT):
                dve.wait_ge(y_tok_in[t], 32)
                for x in range(2):
                    ins = dve.scalar_tensor_tensor(out=h_res[:, t, :], in0=y_tok[:, t, x, :], scalar=w_main[:, t, x:x + 1], in1=h_res[:, t, :], op0=ALU.mult, op1=ALU.add)
                    if x == 0:
                        chain(ins)
                ins.then_inc(h_ready, 1)
                dve.wait_ge(h_ready, 2 * NT + t + 1)
                turn_rows(t, y_tok[:, t, 1, :].rearrange("p (k n) -> p k n", k=KD), 2 * (t % 2), nrow_mm, 2 * NT + 2 * t + 1, V_PLE, n3_scaled)
                if t:
                    lower(t - 1)
            lower(NT - 1)
            dve.wait_ge(ple_in, 64)
            dve.wait_ge(ple_ready, KE + 2 * NT)
            dve.wait_ge(root_ready, 3)
            chain(dve.reciprocal(rs3, ss3))
            for t in range(NT):
                for n in range(2):
                    half = slice(n * 512, (n + 1) * 512)
                    dve.wait_ge(gate_mm, 2 * t + n + 1)
                    ins = dve.scalar_tensor_tensor(out=gate[t % 2][:, half], in0=bank(4 + 2 * (t % 2) + n), scalar=rs3[:, t:t + 1], in1=gate_b[:, half], op0=ALU.mult, op1=ALU.add)
                ins.then_inc(gate_pre, 1)
                dve.wait_ge(gate_ready, t + 1)
                chain(dve.tensor_tensor(gate[t % 2], ple_proj[:, t, :], gate[t % 2], ALU.mult))
                dve.tensor_tensor(h_res[:, t, :], h_res[:, t, :], gate[t % 2], ALU.add).then_inc(h_ready, 1)
                dve.wait_ge(root_ready, t + 4)
                chain(dve.reciprocal(rs4[:, t:t + 1], ss4[:, t:t + 1]))
                dve.scalar_tensor_tensor(out=out_rows[t % 2], in0=h_res[:, t, :], scalar=rs4[:, t:t + 1], in1=final_w, op0=ALU.mult, op1=ALU.mult).then_inc(out_ready, 1)

        @block.tensor
        def _(pe):
            pe.wait_ge(consts_in, 32)
            for t in range(NT):
                pe.wait_ge(xn_ready, t + 1)
                for k in range(KD):
                    ins = pe.transpose(bank(k)[:, t * P:(t + 1) * P], x_norm[:, t, k:k + (P - 1) * KD + 1:KD], ident)
                    if t == NT - 1:
                        ins.then_inc(xt_mm, 1)
            def slot(k, seq, prep):
                if seq is not None:
                    q = seq
                    if 1 <= k < 7:
                        pe.wait_ge(s_ready, 7 * q + k)
                        pe.matmul(bank(7)[:, P * (k % 4):P * (k % 4) + P], step_mat[:, k, :], state[:, k, :], start=True, stop=True).then_inc(seq_mm, 1)
                    if k == 7:
                        pe.wait_ge(s_ready, 7 * q + 7)
                        for c in range(1, NC):
                            ins = pe.matmul(bank(7)[:, c * C:(c + 1) * C], state[:, c, :], r_eff[:, c * C:(c + 1) * C], start=True, stop=True)
                        ins.then_inc(y_mm, 1)
                        pe.wait_ge(y_ready, q + 1)
                        pe.matmul(bank(7), head_ones, y_buf, start=True, stop=True).then_inc(stat_mm, 1)
                    if k == 8:
                        pe.wait_ge(ysq_ready, q + 1)
                        pe.matmul(bank(7), head_ones, r_eff, start=True, stop=True).then_inc(stat_mm, 1)
                if prep is not None:
                    q = prep
                    step = PREP_STEPS[k]
                    cols = slice(q * P, (q + 1) * P)
                    if step == 0:
                        if q == 0:
                            pe.wait_ge(lo_ready, 2)
                            pe.wait_ge(lora_in, 48)
                            pe.wait_ge(zeros_ready, 2)
                        if q == 1:
                            pe.wait_ge(lora_in, 96)
                            pe.wait_ge(zeros_ready, 5 + NH)
                        pe.matmul(bank(6), lora_w[q > 0][:, 0, cols], z[:, 12, :], start=True, stop=True).then_inc(prep_mm, 1)
                    if step == 1:
                        pe.wait_ge(sg_ready, q + 1)
                        pe.matmul(bank(6), lora_w[q > 0][:, 1, cols], z[:, 12, :], start=True, stop=True).then_inc(prep_mm, 1)
                    if step == 2:
                        pe.wait_ge(aa_ready, q + 1)
                        pe.wait_ge(ksq_ready, q + 1)
                        pe.matmul(bank(6), head_ones, knorm, start=True, stop=True).then_inc(prep_mm, 1)
                    if step == 4:
                        pe.wait_ge(ksum_ready, q + 1)
                        pe.wait_ge(rk_ready, q + 1)
                        pe.matmul(bank(6), head_ones, sgw, start=True, stop=True).then_inc(prep_mm, 1)
                    if step == 5:
                        pe.wait_ge(bonus_ready, q + 1)
                        pe.matmul(bank(6), lora_w[q > 0][:, 2, cols], z[:, 13, :], start=True, stop=True).then_inc(prep_mm, 1)

            for j, (n, kind, what) in enumerate(jobs):
                pe.wait_ge(slab_lo_ready, n + 1)
                if j >= 2:
                    z_done(pe, j - 2)
                elif j == 0:
                    pe.wait_ge(hf_lo, 3)
                zb = bank(2 + j % 2)
                for k in range(KD):
                    if j == 0:
                        pe.wait_ge(hf_lo, k + 1)
                    for x, (h, w) in enumerate(((h_hi, slab_hi), (h_lo, slab_hi), (h_hi, slab_lo))):
                        first, last = k == 0 and x == 0, k == KD - 1 and x == 2
                        if kind == "tok":
                            ins = pe.matmul(zb[:, 0:SLAB], h[:, k, what[1] * P:(what[1] + 1) * P],
                                            w[:, n % 2, k, :], start=first, stop=last)
                        else:
                            c = (what % 2) * P
                            ins = pe.matmul(zb, w[:, n % 2, k, c:c + P], h[:, k, :], start=first, stop=last)
                ins.then_inc(z_mm, 1)
                if 0 <= j - PREP_JOB < NSLOT:
                    slot(j - PREP_JOB, None, 0)
            pe.wait_ge(z_act, z_count(NJ - 1, "act"))
            pe.wait_ge(z_dve, z_count(NJ - 1, "dve"))

            def scores(u):
                h, i = units()[u]
                if u >= 2:
                    pe.wait_ge(att_s_read, u - 1)
                n = P * (i + 1)
                pe.matmul(bank(4 + u % 2)[:, 0:n], q_head[:, h, i * P:(i + 1) * P], k_pair[:, h // 2, 0:n],
                          start=True, stop=True).then_inc(att_s_mm, 1)

            def turn(u):
                h, i = units()[u]
                pe.wait_ge(att_p, u + 1)
                if u >= 2:
                    pe.wait_ge(att_pt, u - 1)
                for j in range(i + 1):
                    ins = pe.transpose(bank(6 + u % 2)[:, j * P:(j + 1) * P], prob[:, u % PROBS, j * P:(j + 1) * P], ident)
                ins.then_inc(att_tr, 1)

            def values(pr):
                pe.wait_ge(att_pt, 8 * (pr + 1))
                if pr >= 2:
                    pe.wait_ge(att_y, pr - 1)
                for i in range(NT):
                    for j in range(i + 1):
                        for par in range(2):
                            h = 2 * pr + par
                            ins = pe.matmul(bank(2 + pr % 2)[64 * par:64 * par + 64, i * P:(i + 1) * P],
                                            v_tok[:, j, h * HD:(h + 1) * HD],
                                            prob_t[:, pr % 2, par, pt_col(i, j):pt_col(i, j) + P],
                                            start=(j == 0), stop=(j == i))
                ins.then_inc(att_pv, 1)

            scores(0)
            for step in range(4 * NH + LAG + 4):
                if step + 1 < 4 * NH:
                    scores(step + 1)
                if LAG <= step < 4 * NH + LAG:
                    turn(step - LAG)
                if step >= LAG + 9 and (step - LAG - 9) % 8 == 0:
                    values((step - LAG - 9) // 8)

            pe.wait_ge(rwkv_zero, 1)
            for p in range(NP):
                pe.wait_ge(prep_out, p + 1)
                pe.wait_ge(ar_ready, 4 * (p + 1))
                pe.wait_ge(g_ready, p + 1)
                if p >= 2:
                    pe.wait_ge(rstd_ready, p - 1)
                pe.wait_ge(mc_ready, 2 * p)
                for t in range(NT):
                    tok = slice(t * P, (t + 1) * P)
                    if t:
                        pe.wait_ge(within_ready, NT * p + t)
                    pe.matmul(bank(6), b_inc[:, tok], ar_head[:, t, :], start=True, stop=True).then_inc(s1_mm, 1)
                    if t:
                        pe.wait_ge(across_ready, NT * p + t)
                    pe.matmul(bank(7), k_inc[:, tok], ar_head[:, t, :], start=True, stop=True).then_inc(s2_mm, 1)
                    if t >= 2:
                        pe.wait_ge(tok_ready, NT * p + t - 1)
                    for n, src in enumerate((a_dec, z[:, 8 + p, :], b_end, k_end)):
                        ins = pe.transpose(bank(4 + t % 2)[:, n * P:(n + 1) * P], src[:, tok], ident)
                    ins.then_inc(tok_mm, 1)
                pe.wait_ge(tok_mm, NT * (p + 1))
                pe.sem_inc(unit_in_used, 1)
                for s in range(2):
                    if s == 1:
                        pe.wait_ge(tok_ready, NT * (p + 1))
                        pe.wait_ge(across_ready, NT * (p + 1))
                        for t in range(NT):
                            for h in range(2):
                                n = 2 * t + h
                                ins = pe.matmul(bank(6)[:, n * HD:(n + 1) * HD], across[:, t, 2 * h * P:(2 * h + 1) * P],
                                                v_rows[:, t, h * HD:(h + 1) * HD], start=True, stop=True)
                        ins.then_inc(g_mm, 1)
                    pe.wait_ge(tok_ready, NT * p + 3 + s)
                    pe.wait_ge(tt_init, 2 * p + s + 1)
                    for m in range(4):
                        ins = pe.transpose(bank(4 + s)[:, m * P:(m + 1) * P], t_inv_t[:, 4 * s + m, :], ident)
                    ins.then_inc(tr_mm, 1)
                pe.wait_ge(ga_ready, p + 1)
                if p == 0:
                    pe.wait_ge(att_y, NP)
                pe.wait_ge(q_ready, 2 * p)
                pe.wait_ge(rp_ready, p)
                pe.wait_ge(y0_ready, p)
                for l in range(1, LV + 1):
                    m = LV * p + l - 1
                    for s in range(2):
                        if l >= 2:
                            pe.wait_ge(t_ready, 2 * (m - 1) + s + 1)
                            for n in range(4):
                                ins = pe.transpose(bank(4 + s)[:, n * P:(n + 1) * P], t_inv[:, 4 * s + n, :], ident)
                            ins.then_inc(tr_mm, 1)
                        else:
                            pe.wait_ge(tt_ready, 2 * LV * p + s + 1)
                        pe.wait_ge(mt_ready, 2 * m + s + 1)
                        for n in range(4):
                            ins = pe.matmul(bank(s)[:, n * P:(n + 1) * P], m_level[m % 2][:, 4 * s + n, :], t_inv[:, 4 * s + n, :], start=True, stop=True)
                        ins.then_inc(x_mm, 1)
                    for s in range(2):
                        pe.wait_ge(x_ready, 2 * m + s + 1)
                        if l >= 2:
                            pe.wait_ge(tt_ready, 2 * m + s + 1)
                        for n in range(4):
                            i = 4 * s + n
                            if l < LV:
                                ins = pe.matmul(bank(2 + s)[:, n * P:(n + 1) * P], t_inv_t[:, i, :], m_t[:, i, :], start=True, stop=True)
                            else:
                                ins = pe.matmul(bank(2 + s)[:, n * P:(n + 1) * P], m_t[:, i, :], t_inv_t[:, i, :], start=True, stop=True)
                        ins.then_inc(d_mm, 1)
                        slot(2 * (l - 1) + s, p - 1 if p else None, p + 1 if p + 1 < NP else None)
                for s in range(2):
                    pe.wait_ge(t_ready, 2 * (LV * p + LV - 1) + s + 1)
                    for n in range(4):
                        i = 4 * s + n
                        ins = pe.matmul(bank(s)[:, n * P:(n + 1) * P], t_inv_t[:, i, :], rhs[:, i // 2, i % 2, :], start=True, stop=True)
                    ins.then_inc(w_mm, 1)
                for t in range(NT):
                    tok = slice(t * P, (t + 1) * P)
                    for h in range(2):
                        pe.matmul(bank(3)[64 * h:64 * h + 64, tok], v_rows[:, t, h * HD:(h + 1) * HD], across[:, t, (2 * h + 1) * P:(2 * h + 2) * P], start=(t == 0), stop=False)
                pe.wait_ge(w_ready, 2 * p + 2)
                for t in range(NT):
                    tok = slice(t * P, (t + 1) * P)
                    for h in range(2):
                        ins = pe.matmul(bank(2)[64 * h:64 * h + 64, tok], wy[:, t, 0, h, :], within[:, t, (2 * h + 1) * P:(2 * h + 2) * P], start=True, stop=True)
                ins.then_inc(rp_mm, 1)
                for t in range(NT):
                    tok = slice(t * P, (t + 1) * P)
                    for h in range(2):
                        ins = pe.matmul(bank(3)[64 * h:64 * h + 64, tok], wy[:, t, 1, h, :], within[:, t, (2 * h + 1) * P:(2 * h + 2) * P], start=False, stop=(t == NT - 1))
                ins.then_inc(y0_mm, 1)
                for s in range(2):
                    for c in range(4 * s, 4 * s + 4):
                        ins = pe.matmul(bank(4 + s)[:, (c % 4) * P:(c % 4 + 1) * P], wy[:, c // 2, 0, :, :].rearrange("p h d -> p (h d)"),
                                        bk_chunk[:, c // 2, c % 2, 0:P], start=True, stop=True)
                    ins.then_inc(mc_mm, 1)
                for s in range(2):
                    for c in range(4 * s, 4 * s + 4):
                        o = bank(s)[:, (c % 4) * P:(c % 4 + 1) * P]
                        pe.matmul(o, bk_chunk[:, c // 2, c % 2, 0:P], wy[:, c // 2, 1, :, :].rearrange("p h d -> p (h d)"), start=True, stop=False)
                        ins = pe.matmul(o, bk_chunk[:, c // 2, c % 2, P:2 * P], v_rows[:, c // 2, :], start=False, stop=True)
                    ins.then_inc(q_mm, 1)
            def project(o, k, start=False, stop=False):
                t, n = o // 2, o % 2
                src = z[:, 8 + k, :] if k < NP else y_att[:, k - NP, :]
                return pe.matmul(bank(o), src[:, t * P:(t + 1) * P], w_out[:, k, n * 512:(n + 1) * 512], start=start, stop=stop)

            pe.wait_ge(w_out_in[1], 16)
            pe.wait_ge(q_ready, 2 * NP)
            pe.wait_ge(rp_ready, NP)
            pe.wait_ge(y0_ready, NP)
            pe.wait_ge(mc_ready, 2 * NP)
            ready_rows = [4, 5, 6, 7, 0, 1, 2]
            products = [(o, k) for k in ready_rows for o in range(7)]
            done = 0
            for k in range(NSLOT):
                slot(k, NP - 1, None)
                until = min(len(products), done + (3 if k < 7 else 10))
                for o, row in products[done:until]:
                    if row == 0 and o == 0:
                        pe.wait_ge(w_out_in[0], 16)
                    project(o, row, start=(row == ready_rows[0]))
                done = until
            pe.wait_ge(rstd_ready, NP)
            for row in ready_rows:
                project(7, row, start=(row == ready_rows[0]))
            pe.wait_ge(yr_ready, NP)
            for o in range(8):
                project(o, NP - 1, stop=True).then_inc(op_mm, 1)

            def turn_rows(rows, b0, mm):
                for g in range(2):
                    for k in range(4 * g, 4 * g + 4):
                        ins = pe.transpose(bank(b0 + g)[:, (k % 4) * P:(k % 4 + 1) * P], rows[:, k:k + (P - 1) * KD + 1:KD], ident)
                    ins.then_inc(mm, 1)

            def logits(t):
                pe.wait_ge(nf_ready, t + 1)
                for k in range(KD):
                    ins = pe.matmul(bank(4)[:, t * (NG + NE):(t + 1) * (NG + NE)], n_feat[:, t, k, :], router_w[:, k, :], start=(k == 0), stop=(k == KD - 1))
                return ins

            pe.wait_ge(router_in, 32)
            for t in range(NT):
                pe.wait_ge(h_ready, (4, 2 * NT)[t > 0])
                if t >= 2:
                    pe.wait_ge(nf_ready, t - 1)
                turn_rows(h_res[:, t, :], 2 * (t % 2), nrow_mm)
                if t:
                    logits(t - 1)
            ins = logits(NT - 1)
            ins.then_inc(route_mm, 1)
            pe.wait_ge(routed, CHOICES)
            pe.matmul(bank(5)[:, 0:NT * NE], const[:, K_TRI:K_TRI + P], hot_sum.rearrange("p n e -> p (n e)"), start=True, stop=False)
            pe.matmul(bank(5)[:, NE:NT * NE], const[:, K_ALL1:K_ALL1 + P], hot_before.rearrange("p n e -> p (n e)"), start=False, stop=True).then_inc(route_mm, 1)
            pe.wait_ge(routed, SLOTS)
            for n in range(2 * NT):
                ins = pe.matmul(bank(4)[:, 0:NPAIR], slot_hot[:, n % 2, n // 2, :], row_in_pass[n % 2][:, n // 2, :], start=(n == 0), stop=(n == 2 * NT - 1))
            ins.then_inc(route_mm, 1)
            pe.wait_ge(over_counted, 1)
            pe.matmul(bank(5)[:, 0:1], const[:, K_ALL1:K_ALL1 + P], over_rows, start=True, stop=True).then_inc(route_mm, 1)
            pe.wait_ge(routed, OVERFLOWS)

            def ple(steps):
                for m in steps:
                    if m == 0:
                        pe.wait_ge(ple_in, 64)
                    else:
                        pe.wait_ge(ple_ready, m)
                    t, n = divmod(m - KE, 2)
                    if m < KE:
                        for t in range(NT):
                            ins = pe.transpose(bank(7)[:, t * P:(t + 1) * P], ple_p[:, t, m:m + (P - 1) * KE + 1:KE], ident)
                    else:
                        for k in range(KE):
                            ins = pe.matmul(bank(7), ple_pt[:, k, t * P:(t + 1) * P], ple_wp[:, k, n * 512:(n + 1) * 512], start=(k == 0), stop=(k == KE - 1))
                    ins.then_inc(ple_mm, 1)

            ple(PLE_STEPS[0])

            def expert_rows(s, it, first=False):
                pe.wait_ge(x_slot_in[s], it * 16 + 16)
                if not (first and s == 0):
                    pe.wait_ge(xs_ready, it * 2 + s)
                turn_rows(x_slot[s], 0, xs_mm)

            def expert_pass(it, first=False, last=False):
                for s in range(2):
                    pe.wait_ge(w13_in[s], it * 64 + 64)
                    pe.wait_ge(xs_ready, it * 2 + s + 1)
                    if not first:
                        pe.wait_ge(hid_ready, it * 2 + s - 1)
                    for w in range(2):
                        for k in range(KD):
                            for e in range(2):
                                ins = pe.matmul(bank(2 + s)[64 * e:64 * e + 64, w * DE:(w + 1) * DE], x_slot_t[s][:, k, 64 * e:64 * e + 64],
                                                (w1_sb, w3_sb)[w][s][:, e, k, :], start=(k == 0), stop=(k == KD - 1))
                    ins.then_inc(up_mm, 1)
                    if not (last and s == 1):
                        expert_rows(1 - s, it + s)
                    pe.wait_ge(hid_ready, it * 2 + s + 1)
                    for k in range(KE):
                        ins = pe.transpose(bank(4)[:, k * P:(k + 1) * P], hid[s][:, k:k + (P - 1) * KE + 1:KE], ident)
                    ins.then_inc(hid_mm, 1)
                    pe.wait_ge(hidt_ready, it * 2 + s + 1)
                    pe.wait_ge(w2e_in[s], it * 32 + 32)
                    for n in range(2):
                        if not (first and s == 0):
                            pe.wait_ge((y_lo, y_hi)[n], it * 2 + s)
                        for k in range(KE):
                            for e in range(2):
                                ins = pe.matmul(bank(5 + n)[64 * e:64 * e + 64, :], hid_t[s][:, k, 64 * e:64 * e + 64],
                                                w2_sb[s][:, e, k, n * 512:(n + 1) * 512], start=(k == 0), stop=(k == KE - 1))
                        ins.then_inc(down_mm, 1)
                    if first:
                        ple(PLE_STEPS[1 + s])

            expert_rows(0, 0, first=True)
            expert_pass(0, first=True)
            with pe.Fori(1, NPAIR // 2 - 1) as it:
                expert_pass(it)
            expert_pass(NPAIR // 2 - 1, last=True)
            with if_over(pe):
                pe.wait_ge(y_lo, NPAIR)
                pe.wait_ge(y_hi, NPAIR)
                pe.wait_ge(over_in_ready, 16)
                for t in range(NT):
                    if t >= 2:
                        pe.wait_ge(over_dve, t - 1)
                    turn_rows(over_in[:, t, :], 2 * (t % 2), over_mm)
                pe.wait_ge(over_dve, NT)
                with pe.Fori(0, NE) as e:
                    for t in range(NT):
                        if t == 0:
                            pe.wait_ge(over_w_in, e * 48 + 48)
                        for w, sb in enumerate((over_w1, over_w3)):
                            for k in range(KD):
                                ins = pe.matmul(bank(2)[:, w * DE:(w + 1) * DE], over_feat[:, t, k, :], sb[:, k, :], start=(k == 0), stop=(k == KD - 1))
                        ins.then_inc(over_mm, 1)
                        pe.wait_ge(over_dve, over_hid(e, t))
                        for k in range(KE):
                            ins = pe.transpose(bank(4)[:, k * P:(k + 1) * P], hid[0][:, k:k + (P - 1) * KE + 1:KE], ident)
                        ins.then_inc(over_mm, 1)
                        pe.wait_ge(over_act, over_hid_t(e, t))
                        for n in range(2):
                            for k in range(KE):
                                ins = pe.matmul(bank(5 + n), hid_t[0][:, k, :], over_w2[:, k, n * 512:(n + 1) * 512], start=(k == 0), stop=(k == KE - 1))
                        ins.then_inc(over_mm, 1)
            def gate_product(t, n):
                pe.wait_ge(nf_ready, NT + t + 1)
                if t >= 2:
                    pe.wait_ge(gate_pre, t - 1)
                for k in range(KD):
                    hi = gate_hi[k // (KD // 2)][:, k % (KD // 2), n * 512:(n + 1) * 512]
                    for x, (rows, w) in enumerate(((n3_hi, hi), (n3_hi, gate_lo[:, k, n * 512:(n + 1) * 512]), (n3_lo, hi))):
                        ins = pe.matmul(bank(4 + 2 * (t % 2) + n), rows[:, t, k, :], w, start=(k == 0 and x == 0), stop=(k == KD - 1 and x == 2))
                ins.then_inc(gate_mm, 1)

            def turn_tile(t):
                pe.wait_ge(h_ready, 2 * NT + t + 1)
                if t >= 2:
                    pe.wait_ge(n3_scaled, t - 1)
                turn_rows(h_res[:, t, :], 2 * (t % 2), nrow_mm)

            turn_tile(0)
            turn_tile(1)
            pe.wait_ge(gw_lo_ready, KD // 4)
            pe.wait_ge(gw_lo2_ready, KD // 4)
            pe.wait_ge(y_lo, NPAIR)
            pe.wait_ge(y_hi, NPAIR)
            gate_product(0, 0)
            turn_tile(2)
            gate_product(0, 1)
            turn_tile(3)
            for t in range(1, NT):
                for n in range(2):
                    gate_product(t, n)


def tables(np):
    c = np.zeros((P, K_END), np.float32)
    i = np.arange(P)
    c[:, K_ID:K_ID + P] = np.eye(P)
    c[:, K_ONES:K_ONES + P] = (i[:, None] // HD == i[None] // HD)
    same = i[:, None] // C == i[None] // C
    before = i[:, None] < i[None]
    upto = i[:, None] <= i[None]
    c[:, K_MASK:K_MASK + 2 * P] = np.concatenate([same & before, same & upto], axis=1)
    for l in range(LEVELS):
        b = 1 << l
        m = (i[:, None] // (2 * b) == i[None] // (2 * b)) & (i[:, None] // b < i[None] // b)
        c[:, K_LEVEL + l * P:K_LEVEL + (l + 1) * P] = m
    c[:, K_RESET:K_RESET + T] = (np.arange(T) % C != 0)
    c[:, K_TRI:K_TRI + P] = before
    c[:, K_ALL1:K_ALL1 + P] = 1
    c[:, K_IOTA:K_IOTA + P] = np.arange(P)
    c[:, K_TOK:K_TOK + NT] = i[:, None] + P * np.arange(NT)
    return c


def layout(np, v):
    def cols(x):
        return np.asarray(x).reshape(-1, P).T
    vec = np.concatenate([cols(v[n][0]) for n in ("rwkv_mu", "rwkv_w0", "rwkv_a0", "rwkv_k_k", "rwkv_k_a",
                                                  "rwkv_r_k", "rwkv_ln_w", "rwkv_ln_b")]
                         + [np.asarray(v[n][0]).reshape(P, KD) for n in ("norm_mix_w", "norm_ffn_w", "norm_ple_w")], axis=1)
    rel = np.clip(np.arange(P)[:, None] - np.arange(T)[None] + T - P, -(C - 1), 256) + C - 1
    return {
        "const": tables(np), "vec": vec, "x": v["x"][0], "w_in": v["w_in"][0],
        "w_out": v["w_out"][0], "p": v["p"][0, 0],
        "router_w": np.concatenate([v["router_group_w"][0], v["router_expert_w"][0]], axis=1),
        "router_b": np.concatenate([v["router_group_b"], v["router_expert_b"]], axis=1),
        "w1": np.asarray(v["expert_w1"][0]).reshape(NE, D, DE), "w3": np.asarray(v["expert_w3"][0]).reshape(NE, D, DE),
        "w2e": np.asarray(v["expert_w2"][0]).reshape(NE, DE, D),
        "gate_w": v["ple_gate_w"][0], "gate_b": v["ple_gate_b"], "ple_wp": v["ple_proj_w"][0], "final_w": np.asarray(v["final_norm_w"])[None],
        "w2": v["rwkv_w2"][0], "a2": v["rwkv_a2"][0], "g2": v["rwkv_g2"][0],
        "bias": np.asarray(v["att_rel_bias"][0])[:, rel],
    }


def kernel(**inputs):
    import numpy as np
    import concourse.bacc as bacc
    from concourse.bass_utils import run_bass_kernel_spmd

    nc = bacc.Bacc("TRN2", target_bir_lowering=False, num_devices=1)
    arrays = {f"{name}_in": np.ascontiguousarray(x) for name, x in layout(np, inputs).items()}
    aps = {name[:-3]: nc.dram_tensor(name, x.shape, mybir.dt.from_np(x.dtype), kind="ExternalInput").ap()
           for name, x in arrays.items()}
    out = nc.dram_tensor("out", (T, D), F32, kind="ExternalOutput").ap()
    hybrid_trunk(nc, aps, out)
    r = run_bass_kernel_spmd(nc, [arrays], core_ids=[0])
    return r.results[0]["out"].reshape(1, T, D)
```
